# Optimizing a Trainium2 kernel written in Bass

```python
import math
import jax, jax.numpy as jnp
from jax import lax
import numpy as np

D_MODEL = 1024
BATCH = 1
SEQ = 512
DEPTH = 1
DEC_BATCH = 8
DEC_SEQ = 1
PAST_LEN = 1024
PAGE_SIZE = 128

ATT_GROUPS = ((128, 1), (512, 4), (2048, 16))
N_GROUPS_A = 3
HEADS_PER_GROUP = 8
HEAD_DIM = 64
ATT_W = HEADS_PER_GROUP * HEAD_DIM
Q_COLS = N_GROUPS_A * ATT_W
ROPE_THETA = 10000.0
D_INNER = 2 * D_MODEL
SSD_HEAD_DIM = 64
SSD_HEADS = D_INNER // SSD_HEAD_DIM
SSD_GROUPS = 8
SSD_HPG = SSD_HEADS // SSD_GROUPS
D_STATE = 128
CONV_W = 4
CONV_CH = D_INNER + 2 * SSD_GROUPS * D_STATE
SSD_CHUNK = 64
N_KEYS = 128
N_EXPERTS = N_KEYS * N_KEYS
PEER_HEADS = 8
PEER_DKEY = 256
PEER_TOPK = 16
PEER_BLOCK = 256
PLE_DIM = 256
EPS = 1e-6

kernel_name = 'hybrid_dilated_ssd_peer_step'

def rmsnorm(x, g):
    xf = x.astype(jnp.float32)
    y = xf * lax.rsqrt(jnp.mean(xf * xf, axis=-1, keepdims=True) + EPS)
    return (y * g.astype(jnp.float32)).astype(x.dtype)

def rope(x, pos):
    half = HEAD_DIM // 2
    inv = jnp.exp(jnp.arange(half, dtype=jnp.float32) * (-2.0 * math.log(ROPE_THETA) / HEAD_DIM))
    ang = pos.astype(jnp.float32)[:, None] * inv[None, :]
    shape = (1, pos.shape[0]) + (1,) * (x.ndim - 3) + (half,)
    cos, sin = jnp.cos(ang).reshape(shape), jnp.sin(ang).reshape(shape)
    xf = x.astype(jnp.float32)
    x1, x2 = xf[..., :half], xf[..., half:]
    return jnp.concatenate([x1 * cos - x2 * sin, x2 * cos + x1 * sin], axis=-1).astype(x.dtype)

def dilated_attn_prompt(q, k, v, window, dil):
    b, s, h, c = q.shape
    nk = window // dil
    span = nk * dil
    sp = -(-s // span) * span
    nb = sp // span
    padw = ((0, 0), (0, sp - s), (0, 0), (0, 0))
    blk = lambda t: jnp.pad(t, padw).reshape(b, nb, nk, dil, h, c)
    qb, kb, vb = blk(q), blk(k), blk(v)
    prev = lambda t: jnp.concatenate([jnp.zeros_like(t[:, :1]), t[:, :-1]], axis=1)
    kk = jnp.concatenate([prev(kb), kb], axis=2)
    vv = jnp.concatenate([prev(vb), vb], axis=2)
    sc = jnp.einsum('bnirhc,bnjrhc->bnrhij', qb, kk, preferred_element_type=jnp.float32) * (c ** -0.5)
    i_idx = jnp.arange(nk)[:, None]
    j_idx = jnp.arange(2 * nk)[None, :]
    delta = nk + i_idx - j_idx
    band = (delta >= 0) & (delta <= nk)
    has_prev = (jnp.arange(nb)[:, None] > 0) | (jnp.arange(2 * nk)[None, :] >= nk)
    mask = band[None] & has_prev[:, None, :]
    sc = jnp.where(mask[None, :, None, None], sc, -jnp.inf)
    m = jnp.max(sc, axis=-1, keepdims=True)
    e = jnp.exp(sc - m)
    den = jnp.sum(e, axis=-1)
    o = jnp.einsum('bnrhij,bnjrhc->bnirhc', e, vv.astype(jnp.float32))
    o = o / jnp.transpose(den, (0, 1, 4, 2, 3))[..., None]
    lse = jnp.transpose(m[..., 0] + jnp.log(den), (0, 1, 4, 2, 3))
    return o.reshape(b, sp, h, c)[:, :s], lse.reshape(b, sp, h)[:, :s]

def dilated_attn_step(q, k_all, v_all, n_past, window, dil):
    t = q.shape[1]
    nk = window // dil
    idx = n_past + jnp.arange(t)[:, None] - dil * jnp.arange(nk + 1)[None, :]
    valid = idx >= 0
    idxc = jnp.clip(idx, 0)
    kg = k_all[:, idxc]
    vg = v_all[:, idxc]
    sc = jnp.einsum('bthc,btmhc->bthm', q, kg, preferred_element_type=jnp.float32) * (q.shape[-1] ** -0.5)
    sc = jnp.where(valid[None, :, None, :], sc, -jnp.inf)
    m = jnp.max(sc, axis=-1, keepdims=True)
    e = jnp.exp(sc - m)
    den = jnp.sum(e, axis=-1)
    o = jnp.einsum('bthm,btmhc->bthc', e, vg.astype(jnp.float32)) / den[..., None]
    return o, m[..., 0] + jnp.log(den)

def ssd_scan(xs, dt, A, Bm, Cm, h0, chunk):
    b, l = xs.shape[:2]
    nc = l // chunk
    r = lambda t: t.reshape((b, nc, chunk) + t.shape[2:])
    xdt = r(xs * dt[..., None])
    acs = jnp.cumsum(r(dt * A), axis=2)
    Bc, Cc = r(Bm), r(Cm)
    tril = jnp.tril(jnp.ones((chunk, chunk), dtype=bool))
    diff = acs[:, :, :, None] - acs[:, :, None, :]
    lmat = jnp.exp(jnp.where(tril[None, None, :, :, None, None], diff, -jnp.inf))
    cb = jnp.einsum('bcign,bcjgn->bcijg', Cc, Bc)
    y_diag = jnp.einsum('bcijge,bcjgep->bcigep', cb[..., None] * lmat, xdt)
    decay = jnp.exp(acs[:, :, -1:] - acs)
    states = jnp.einsum('bcjgn,bcjgep->bcgepn', Bc, xdt * decay[..., None])
    chunk_decay = jnp.exp(acs[:, :, -1])

    def step(hc, inp):
        st, dec = inp
        return hc * dec[..., None, None] + st, hc

    h_last, h_prev = lax.scan(step, h0, (jnp.moveaxis(states, 1, 0), jnp.moveaxis(chunk_decay, 1, 0)))
    h_prev = jnp.moveaxis(h_prev, 0, 1)
    y_off = jnp.einsum('bcign,bcgepn->bcigep', Cc, h_prev) * jnp.exp(acs)[..., None]
    y = (y_diag + y_off).reshape((b, l) + xs.shape[2:])
    return y, h_last

def mixer(h, pos, kv_bufs, conv_state, ssm_state, w_in, conv_w, conv_b, dt_bias, a_log, d_skip,
          ssd_norm, w_att_out, w_ssd_out, w_out):
    b, l, _ = h.shape
    proj = jnp.einsum('bld,de->ble', h, w_in)
    sizes = (Q_COLS, Q_COLS, Q_COLS, D_INNER, CONV_CH, SSD_HEADS, D_MODEL)
    cuts = [sum(sizes[:i + 1]) for i in range(len(sizes) - 1)]
    q, k, v, z, xbc, dt_raw, gates = jnp.split(proj, cuts, axis=-1)
    grp = lambda t: t.reshape(b, l, N_GROUPS_A, HEADS_PER_GROUP, HEAD_DIM)
    q, k, v = rope(grp(q), pos), rope(grp(k), pos), grp(v)
    outs, lses, new_kv = [], [], []
    for g, (win, dil) in enumerate(ATT_GROUPS):
        qg, kg, vg = q[:, :, g], k[:, :, g], v[:, :, g]
        kv_new = jnp.stack([kg, vg], axis=2)
        if kv_bufs is None:
            o, lse = dilated_attn_prompt(qg, kg, vg, win, dil)
            new_kv.append(kv_new[:, l - min(win, l):])
        else:
            buf = kv_bufs[g]
            kv_all = jnp.concatenate([buf.astype(kv_new.dtype), kv_new], axis=1)
            o, lse = dilated_attn_step(qg, kv_all[:, :, 0], kv_all[:, :, 1], buf.shape[1], win, dil)
            new_kv.append(kv_new)
        outs.append(o)
        lses.append(lse)
    wts = jax.nn.softmax(jnp.stack(lses), axis=0)
    att = jnp.sum(wts[..., None] * jnp.stack(outs), axis=0).reshape(b, l, ATT_W).astype(h.dtype)
    out_a = jnp.einsum('blc,cd->bld', att, w_att_out)
    if conv_state is None:
        conv_state = jnp.zeros((b, CONV_W - 1, CONV_CH), xbc.dtype)
    if ssm_state is None:
        ssm_state = jnp.zeros((b, SSD_HEADS, SSD_HEAD_DIM, D_STATE), jnp.float32)
    xpad = jnp.concatenate([conv_state.astype(xbc.dtype), xbc], axis=1)
    conv = conv_b
    for j in range(CONV_W):
        conv = conv + xpad[:, j:j + l] * conv_w[j]
    xc = jax.nn.silu(conv)
    new_conv = xpad[:, xpad.shape[1] - (CONV_W - 1):]
    xs, Bm, Cm = jnp.split(xc, [D_INNER, D_INNER + SSD_GROUPS * D_STATE], axis=-1)
    xs5 = xs.reshape(b, l, SSD_GROUPS, SSD_HPG, SSD_HEAD_DIM).astype(jnp.float32)
    Bm = Bm.reshape(b, l, SSD_GROUPS, D_STATE).astype(jnp.float32)
    Cm = Cm.reshape(b, l, SSD_GROUPS, D_STATE).astype(jnp.float32)
    dt = jax.nn.softplus(dt_raw.astype(jnp.float32) + dt_bias.astype(jnp.float32))
    dt = dt.reshape(b, l, SSD_GROUPS, SSD_HPG)
    A = -jnp.exp(a_log.astype(jnp.float32)).reshape(SSD_GROUPS, SSD_HPG)
    h0 = ssm_state.astype(jnp.float32).reshape(b, SSD_GROUPS, SSD_HPG, SSD_HEAD_DIM, D_STATE)
    y, h_last = ssd_scan(xs5, dt, A, Bm, Cm, h0, math.gcd(l, SSD_CHUNK))
    y = y + d_skip.astype(jnp.float32).reshape(SSD_GROUPS, SSD_HPG)[:, :, None] * xs5
    y = y.reshape(b, l, D_INNER) * jax.nn.silu(z.astype(jnp.float32))
    y = rmsnorm(y, ssd_norm).astype(h.dtype)
    out_b = jnp.einsum('ble,ed->bld', y, w_ssd_out)
    ga, gb = jnp.split(gates, 2, axis=-1)
    merged = jax.nn.sigmoid(ga) * out_a + jax.nn.sigmoid(gb) * out_b
    new_ssm = h_last.reshape(b, SSD_HEADS, SSD_HEAD_DIM, D_STATE).astype(h.dtype)
    return jnp.einsum('bld,de->ble', merged, w_out), new_kv, new_conv, new_ssm

def peer(h, w_peer_q, peer_keys1, peer_keys2, peer_u, peer_v):
    b, l, d = h.shape
    x = h.reshape(b * l, d)
    nt = x.shape[0]
    q = jnp.einsum('td,de->te', x, w_peer_q).reshape(nt, PEER_HEADS, 2, PEER_DKEY // 2)
    s1 = jnp.einsum('thc,hkc->thk', q[:, :, 0], peer_keys1, preferred_element_type=jnp.float32)
    s2 = jnp.einsum('thc,hkc->thk', q[:, :, 1], peer_keys2, preferred_element_type=jnp.float32)
    v1, i1 = lax.top_k(s1, PEER_TOPK)
    v2, i2 = lax.top_k(s2, PEER_TOPK)
    cand = (v1[..., :, None] + v2[..., None, :]).reshape(nt, PEER_HEADS, PEER_TOPK * PEER_TOPK)
    cidx = (i1[..., :, None] * N_KEYS + i2[..., None, :]).reshape(nt, PEER_HEADS, PEER_TOPK * PEER_TOPK)
    sc, sel = lax.top_k(cand, PEER_TOPK)
    eidx = jnp.take_along_axis(cidx, sel, axis=-1)
    gate = jax.nn.softmax(sc, axis=-1)
    blk = math.gcd(nt, PEER_BLOCK)
    nbk = nt // blk

    def block_fn(args):
        xb, eb, gb = args
        u = peer_u[eb]
        act = jax.nn.gelu(jnp.einsum('thkd,td->thk', u, xb, preferred_element_type=jnp.float32))
        return jnp.einsum('thk,thkd->td', (gb * act).astype(xb.dtype), peer_v[eb])

    out = lax.map(block_fn, (x.reshape(nbk, blk, d),
                             eidx.reshape(nbk, blk, PEER_HEADS, PEER_TOPK),
                             gate.reshape(nbk, blk, PEER_HEADS, PEER_TOPK)))
    return out.reshape(b, l, d)

def trunk(x, p, pos, kv_bufs, conv_state, ssm_state, layer_w, norm_final):
    (norm_mix, w_in, conv_w, conv_b, dt_bias, a_log, d_skip, ssd_norm, w_att_out, w_ssd_out, w_out,
     norm_ffn, w_peer_q, peer_keys1, peer_keys2, peer_u, peer_v, norm_ple, w_ple_gate, w_ple_proj) = layer_w
    kv_out = [[] for _ in ATT_GROUPS]
    conv_out, ssm_out = [], []
    for i in range(DEPTH):
        bufs = None if kv_bufs is None else tuple(c[i] for c in kv_bufs)
        cs = None if conv_state is None else conv_state[i]
        ss = None if ssm_state is None else ssm_state[i]
        mo, kv, nc, ns = mixer(rmsnorm(x, norm_mix[i]), pos, bufs, cs, ss, w_in[i], conv_w[i], conv_b[i],
                               dt_bias[i], a_log[i], d_skip[i], ssd_norm[i], w_att_out[i], w_ssd_out[i], w_out[i])
        x = x + mo
        x = x + peer(rmsnorm(x, norm_ffn[i]), w_peer_q[i], peer_keys1[i], peer_keys2[i], peer_u[i], peer_v[i])
        pg = jax.nn.sigmoid(jnp.einsum('bld,de->ble', rmsnorm(x, norm_ple[i]), w_ple_gate[i]))
        x = x + pg * jnp.einsum('blc,cd->bld', p[i].astype(x.dtype), w_ple_proj[i])
        for g in range(N_GROUPS_A):
            kv_out[g].append(kv[g])
        conv_out.append(nc)
        ssm_out.append(ns)
    kvs = [jnp.stack(t) for t in kv_out]
    return rmsnorm(x, norm_final), kvs, jnp.stack(conv_out), jnp.stack(ssm_out)

def setup_inputs(seed: int = 0) -> dict:
    key = jax.random.key(seed)
    ks = iter(jax.random.split(key, 40))
    nrm = lambda shape, scale: jax.random.normal(next(ks), shape, jnp.float32) * scale
    inp = {}
    inp['x_prompt'] = nrm((BATCH, SEQ, D_MODEL), 1.0)
    inp['x_sample'] = nrm((DEC_BATCH, DEC_SEQ, D_MODEL), 1.0)
    for win, _ in ATT_GROUPS:
        inp['cache_kv_w%d' % win] = nrm((DEPTH, DEC_BATCH, min(win, PAST_LEN), 2, HEADS_PER_GROUP, HEAD_DIM), 1.0)
    inp['state_conv'] = nrm((DEPTH, DEC_BATCH, CONV_W - 1, CONV_CH), 1.0)
    inp['state_ssm'] = nrm((DEPTH, DEC_BATCH, SSD_HEADS, SSD_HEAD_DIM, D_STATE), 0.1)
    inp['p_prompt'] = nrm((DEPTH, BATCH, SEQ, PLE_DIM), 1.0)
    inp['p_sample'] = nrm((DEPTH, DEC_BATCH, DEC_SEQ, PLE_DIM), 1.0)
    in_cols = 3 * Q_COLS + D_INNER + CONV_CH + SSD_HEADS + 2 * D_MODEL
    inp['norm_mix'] = 1.0 + nrm((DEPTH, D_MODEL), 0.02)
    inp['w_in'] = nrm((DEPTH, D_MODEL, in_cols), D_MODEL ** -0.5)
    inp['conv_w'] = nrm((DEPTH, CONV_W, CONV_CH), CONV_W ** -0.5)
    inp['conv_b'] = nrm((DEPTH, CONV_CH), 0.01)
    dt0 = jnp.exp(jax.random.uniform(next(ks), (DEPTH, SSD_HEADS), jnp.float32, math.log(1e-3), math.log(1e-1)))
    inp['dt_bias'] = dt0 + jnp.log(-jnp.expm1(-dt0))
    inp['a_log'] = jnp.log(jax.random.uniform(next(ks), (DEPTH, SSD_HEADS), jnp.float32, 1.0, 16.0))
    inp['d_skip'] = 1.0 + nrm((DEPTH, SSD_HEADS), 0.1)
    inp['ssd_norm'] = 1.0 + nrm((DEPTH, D_INNER), 0.02)
    inp['w_att_out'] = nrm((DEPTH, ATT_W, D_MODEL), ATT_W ** -0.5)
    inp['w_ssd_out'] = nrm((DEPTH, D_INNER, D_MODEL), D_INNER ** -0.5)
    inp['w_out'] = nrm((DEPTH, D_MODEL, D_MODEL), D_MODEL ** -0.5)
    inp['norm_ffn'] = 1.0 + nrm((DEPTH, D_MODEL), 0.02)
    inp['w_peer_q'] = nrm((DEPTH, D_MODEL, PEER_HEADS * PEER_DKEY), D_MODEL ** -0.5)
    inp['peer_keys1'] = nrm((DEPTH, PEER_HEADS, N_KEYS, PEER_DKEY // 2), (PEER_DKEY // 2) ** -0.5)
    inp['peer_keys2'] = nrm((DEPTH, PEER_HEADS, N_KEYS, PEER_DKEY // 2), (PEER_DKEY // 2) ** -0.5)
    inp['peer_u'] = nrm((DEPTH, N_EXPERTS, D_MODEL), D_MODEL ** -0.5)
    inp['peer_v'] = nrm((DEPTH, N_EXPERTS, D_MODEL), PEER_HEADS ** -0.5)
    inp['norm_ple'] = 1.0 + nrm((DEPTH, D_MODEL), 0.02)
    inp['w_ple_gate'] = nrm((DEPTH, D_MODEL, D_MODEL), D_MODEL ** -0.5)
    inp['w_ple_proj'] = nrm((DEPTH, PLE_DIM, D_MODEL), PLE_DIM ** -0.5)
    inp['norm_final'] = 1.0 + nrm((D_MODEL,), 0.02)
    return inp

def reference(x_prompt, x_sample, cache_kv_w128, cache_kv_w512, cache_kv_w2048, state_conv, state_ssm,
              p_prompt, p_sample, norm_mix, w_in, conv_w, conv_b, dt_bias, a_log, d_skip, ssd_norm,
              w_att_out, w_ssd_out, w_out, norm_ffn, w_peer_q, peer_keys1, peer_keys2, peer_u, peer_v,
              norm_ple, w_ple_gate, w_ple_proj, norm_final):
    layer_w = (norm_mix, w_in, conv_w, conv_b, dt_bias, a_log, d_skip, ssd_norm, w_att_out, w_ssd_out, w_out,
               norm_ffn, w_peer_q, peer_keys1, peer_keys2, peer_u, peer_v, norm_ple, w_ple_gate, w_ple_proj)
    pos_p = jnp.arange(x_prompt.shape[1], dtype=jnp.int32)
    pos_s = PAST_LEN + jnp.arange(x_sample.shape[1], dtype=jnp.int32)
    y_prompt, kv_p, conv_p, ssm_p = trunk(x_prompt, p_prompt, pos_p, None, None, None, layer_w, norm_final)
    y_sample, kv_s, conv_s, ssm_s = trunk(x_sample, p_sample, pos_s, (cache_kv_w128, cache_kv_w512, cache_kv_w2048),
                                          state_conv, state_ssm, layer_w, norm_final)
    return (y_prompt, y_sample, kv_p[0], kv_p[1], kv_p[2], conv_p, ssm_p, kv_s[0], kv_s[1], kv_s[2], conv_s, ssm_s)


_drawn_inputs = setup_inputs


def setup_inputs(seed=0):
    import zlib

    import numpy as np

    out = dict(_drawn_inputs(seed))
    spreads = {}
    factors = {'conv_b': 3.912,
     'ssd_norm': 3.26,
     'norm_ffn': 2.725,
     'norm_ple': 200.0,
     'norm_final': 25.158,
     'cache_kv_w2048': 3.266,
     'cache_kv_w128': 6.118,
     'cache_kv_w512': 4.376}
    for name, (base, spread) in spreads.items():
        noise = np.random.default_rng([zlib.crc32(name.encode()), seed]).standard_normal(out[name].shape)
        drawn = base * np.exp(spread * noise) if base else spread * noise
        out[name] = __import__('jax').numpy.asarray(drawn.astype(out[name].dtype))
    for name, factor in factors.items():
        out[name] = (out[name] * factor).astype(out[name].dtype)
    return out
```

```python
import math
from contextlib import ExitStack

import numpy as np
import concourse.bass as bass
from concourse import mybir

P = 128
D_MODEL, SEQ, N_S, PAST_LEN = 1024, 512, 8, 1024
T_ALL = SEQ + N_S
N_T = 5
ATT_W, Q_COLS = 512, 1536
D_INNER, SSD_HEADS, SSD_GROUPS, D_STATE, CONV_W = 2048, 32, 8, 128, 4
CONV_CH = D_INNER + 2 * SSD_GROUPS * D_STATE
N_KEYS, TOPK = 128, 16
EPS = 1e-6
SCALE = 0.125
NEG = -1.0e30
F32 = mybir.dt.float32
U32 = mybir.dt.uint32
ALU = mybir.AluOpType
ACT = mybir.ActivationFunctionType
X_AXIS = mybir.AxisListType.X
XY_AXIS = mybir.AxisListType.XY

B_QKV = 0
B_SSD = 9
B_GATE = 21
B_ATT = 25
B_YOUT = 26
B_OUT = 30
B_PQ = 32
B_PLE = 36
N_BLOCKS = 38

C_IDENT, C_TRI, C_ONES, C_CAUSAL, C_PREV, C_RES, C_EXPAND = 0, 128, 256, 384, 512, 640, 768
C_SEL, C_DELTA, C_IND, C_IOTA, N_CONST = 2816, 3840, 3904, 3912, 3928


def shape_constants():
    c = np.zeros((P, N_CONST), np.float32)
    row, col = np.arange(P)[:, None], np.arange(P)[None, :]
    c[:, C_IDENT:C_IDENT + P] = row == col
    c[:, C_TRI:C_TRI + P] = row <= col
    c[:, C_ONES:C_ONES + P] = 1.0
    c[:, C_CAUSAL:C_CAUSAL + P] = np.where(col <= row, 0.0, NEG)
    c[:, C_PREV:C_PREV + P] = np.where(col >= row, 0.0, NEG)
    c[:, C_RES:C_RES + P] = np.where((col <= row) & (col % 4 == row % 4), 0.0, NEG)
    for pair in range(16):
        c[:32, C_EXPAND + P * pair:C_EXPAND + P * (pair + 1)] = np.arange(32)[:, None] == 2 * pair + col // 64
    c[:8, C_SEL:C_SEL + 1024] = np.arange(8)[:, None] == np.arange(1024)[None, :] // P
    c[:8, C_DELTA:C_DELTA + 64] = np.arange(8)[:, None] == np.arange(64)[None, :] // 8
    c[:64, C_IND:C_IND + 8] = np.arange(64)[:, None] // 8 == np.arange(8)[None, :]
    c[:, C_IOTA:C_IOTA + 16] = np.arange(16)[None, :]
    return c


def tile_positions(g, s):
    i = np.arange(P)
    return P * s + i if g == 0 else 4 * i + s


def rope_table():
    half = 32
    inv = np.exp(np.arange(half, dtype=np.float32) * np.float32(-2.0 * math.log(10000.0) / 64)).astype(np.float32)
    t = np.zeros((P, 13, 128), np.float32)
    for n in range(13):
        pos = tile_positions(n // 4, n % 4) if n < 12 else np.full(P, PAST_LEN)
        ang = (pos.astype(np.float32)[:, None] * inv[None, :]).astype(np.float32)
        cos, sin = np.cos(ang), np.sin(ang)
        t[:, n] = np.concatenate([cos, cos, -sin, sin], axis=1)
    return t.reshape(P, 13 * 128)


def rows_of(n):
    return P if n < 4 else N_S


def stage_semaphores(nc, stack, prefix, names):
    sems = {n: nc.alloc_semaphore(prefix + n) for n in names}

    def release():
        nc.clear_and_free_semaphores(list(sems.values()))
        nc.all_engine_barrier()

    stack.callback(release)
    return sems


class Chain:

    def __init__(self, sem):
        self.sem, self.count = sem, 0

    def __call__(self, eng, ins):
        self.count += 1
        ins.then_inc(self.sem, 1)
        eng.wait_ge(self.sem, self.count)


def hybrid_decoder_step(nc, ins, outs):
    ctx = ExitStack()
    with ctx:
        sem = lambda name: ctx.enter_context(nc.semaphore(name))
        mem = ctx.enter_context(nc.sbuf_tensor("mem", [P, 53200], F32))
        bank = [ctx.enter_context(nc.psum_tensor(f"bank{i}", [P, 512], F32)) for i in range(8)]
        head_out = nc.dram_tensor("head_out", [3, SEQ, 528], F32, kind="Internal").ap()
        m = Memory(mem)
        s = {}
        for name in SEMS:
            s[name] = sem(name)
        shared = Shared(nc, ins, outs, m, bank, s, head_out)
        attention_prompt(shared)
        attention_sample(shared)
        ssd_branch(shared)
        merge_branches(shared)
        peer_and_ple(shared)


SEMS = ["consts_in", "x_in", "ring_in0", "ring_in1", "sync_step", "act_step", "dve_step", "pool_step", "pe_step",
        "proj_ready", "proj_free0", "proj_free1", "proj_free2"]


class Memory:

    def __init__(self, mem):
        self.mem = mem
        self.const = mem[:, 0:N_CONST]
        at = N_CONST
        self.cols = mem[:, at:at + 200]
        self.norm_mix, self.norm_ffn, self.norm_ple = (self.cols[:, 8 * i:8 * i + 8] for i in range(3))
        self.norm_ssd = self.cols[:, 24:40]
        self.conv_w = self.cols[:, 40:168].rearrange("p (c w) -> p c w", w=4)
        self.conv_b = self.cols[:, 168:200]
        at += 200
        self.head_rows = mem[:, at:at + 96]
        self.head_cols = mem[0:32, at + 96:at + 99]
        self.small = mem[:, at + 100:at + 228]
        at += 228
        assert at <= 4360
        self.hT = mem[:, 4360:8520].rearrange("p (c t) -> p c t", t=T_ALL)
        self.attT = mem[:, 8520:10600].rearrange("p (c t) -> p c t", t=T_ALL)
        self.slot = [mem[:, 10600 + 4096 * i:10600 + 4096 * (i + 1)] for i in range(2)]
        self.phase = 18792
        self.end = 53200
        self.q_s = mem[0:8, 48592:50128].rearrange("p (g n) -> p g n", g=3)
        self.kv_s = mem[0:8, 50128:53200].rearrange("p (g n) -> p g n", g=3)

    def at(self, offset, n, parts=P):
        assert self.phase + offset + n <= self.end
        return self.mem[0:parts, self.phase + offset:self.phase + offset + n]

    def c(self, at, n=P, parts=P):
        return self.const[0:parts, at:at + n]


class Shared:
    def __init__(self, nc, ins, outs, m, bank, s, head_out):
        self.nc, self.ins, self.outs, self.m, self.bank, self.s = nc, ins, outs, m, bank, s
        self.head_out = head_out
        self.act = Chain(s["act_step"])
        self.dve = Chain(s["dve_step"])
        self.pool = Chain(s["pool_step"])


def transposed_norm(sh, name, x, xn, tiles, banks, ctx):
    nc, m = sh.nc, sh.m
    squares, inverse, roots, scaled, turned, columns = (
        ctx.enter_context(nc.semaphore(f"{name}_{k}"))
        for k in ("squares", "inverse", "roots", "scaled", "turned", "columns"))
    stat = m.small
    return squares, inverse, roots, scaled, turned, columns, stat


def attention_prompt(sh):
    nc, ins, outs, m, bank, s = sh.nc, sh.ins, sh.outs, sh.m, sh.bank, sh.s
    ident = m.c(C_IDENT)
    x = m.at(0, 5120).rearrange("p (n d) -> p n d", n=N_T)
    xn = m.at(5120, 5120).rearrange("p (n d) -> p n d", n=N_T)
    q_buf = [m.at(2048 * i, 2048).rearrange("p (s n) -> p s n", s=4) for i in range(2)]
    kv_buf = [m.at(4096 + 4096 * i, 4096).rearrange("p (s n) -> p s n", s=4) for i in range(2)]
    qT = m.at(12288, 2048).rearrange("p (c t) -> p c t", c=4)
    kT = m.at(14336, 2048).rearrange("p (c t) -> p c t", c=4)
    score = [m.at(16384 + 1024 * i, 1024).rearrange("p (h w k) -> p h w k", h=4, w=2) for i in range(2)]
    probT = [m.at(18432 + 1024 * i, 1024).rearrange("p (w h q) -> p w h q", w=2, h=4) for i in range(2)]
    head_rows = m.at(20480, 2112).rearrange("p (s h c) -> p s h c", s=4, h=8)
    rope_a, rope_b = m.at(22592, 512), m.at(23104, 512)
    merge_in = [m.at(23616 + 1584 * i, 1584).rearrange("p (g h c) -> p g h c", g=3, h=8) for i in range(2)]
    rope = m.at(26784, 1664).rearrange("p (n c) -> p n c", n=13)
    neg_max = [m.at(28448 + 4 * i, 4) for i in range(2)]
    merge_max = m.at(28456, 8)
    merge_w = m.at(28464, 24).rearrange("p (g h) -> p g h", g=3)
    merge_den = m.at(28488, 24).rearrange("p (g h) -> p g h", g=3)
    merge_sum = m.at(28512, 8)
    stat = m.small

    turns = []
    for g in range(3):
        for t in range(4):
            turns += [("q", g, t), ("k", g, t)]
        for v in range(8):
            turns += [("p", g, v, w) for w in range(2 if g == 0 and v >= 2 else 1)]
    turns += [("att", n) for n in range(4)]
    turn_at = {k: i for i, k in enumerate(turns)}

    def token_columns(k, g, t):
        if t == 4:
            return m.hT[:, k, SEQ:T_ALL]
        if g == 0:
            return m.hT[:, k, P * t:P * t + P]
        return m.hT[:, k, t:SEQ:4]

    with ExitStack() as c:
        names = ("squares", "inverse", "roots", "scaled", "turned", "columns", "qk_rows", "v_rows", "kv_stored0", "kv_stored1", "kv_stored2",
                 "turn_ready", "turn_free", "score_ready", "score_free", "max_ready", "prob_ready", "out_ready",
                 "out_kept", "group_done", "head_stored", "merge_in0", "merge_in1", "merge_exp", "merge_max",
                 "merge_rows")
        a = stage_semaphores(nc, c, "a_", names)
        block = c.enter_context(nc.Block())

        @block.sync
        def _(sp):
            sp.dma_start(x[0:N_S, 4, :], ins["x_sample"]).then_inc(s["x_in"], 16)
            sp.dma_start(x[:, 0:4, :], ins["x_prompt"].rearrange("(n p) d -> p n d", p=P)).then_inc(s["x_in"], 16)
            for b in range(9):
                if b >= 2:
                    sp.wait_ge(s["proj_ready"], 5 * (b - 1))
                sp.dma_start(m.slot[b % 2], ins["stream"][b]).then_inc(s[f"ring_in{b % 2}"], 16)
            for b in (9, 10):
                sp.wait_ge(s["proj_ready"], 5 * (b - 1))
                sp.dma_start(m.slot[b % 2], ins["stream"][b]).then_inc(s[f"ring_in{b % 2}"], 16)

        @block.gpsimd
        def _(pool):
            def store_kv(g):
                pool.wait_ge(a["qk_rows"], 10 * (g + 1))
                pool.wait_ge(a["v_rows"], 5 * (g + 1))
                for t in range(4):
                    src = kv_buf[g % 2][:, t]
                    if g == 0:
                        if t == 3:
                            pool.dma_start(outs["kv0"], src).then_inc(a[f"kv_stored{g}"], 16)
                    else:
                        dst = outs[f"kv{g}"].rearrange("(i r) c -> r i c", r=4)[t]
                        pool.dma_start(dst, src).then_inc(a[f"kv_stored{g}"], 16)
                pool.dma_start(outs[f"kvs{g}"], m.kv_s[:, g]).then_inc(a[f"kv_stored{g}"], 16)

            def store_heads(g):
                for t in range(4):
                    pool.wait_ge(a["out_kept"], 8 * g + 2 * t + 2)
                    src = head_rows[:, t].rearrange("p h c -> p (h c)")
                    if g == 0:
                        pool.dma_start(sh.head_out[0, P * t:P * t + P], src).then_inc(a["head_stored"], 16)
                    else:
                        dst = sh.head_out[g].rearrange("(i r) c -> r i c", r=4)[t]
                        pool.dma_start(dst, src).then_inc(a["head_stored"], 16)

            store_kv(0)
            store_kv(1)
            store_heads(0)
            store_kv(2)
            store_heads(1)
            store_heads(2)
            pool.wait_ge(a["head_stored"], 16 * 12)
            for n in range(4):
                if n >= 2:
                    pool.wait_ge(a["merge_rows"], n - 1)
                src = sh.head_out[:, P * n:P * n + P, :].rearrange("g p c -> p g c")
                dst = merge_in[n % 2].rearrange("p g h c -> p g (h c)")
                pool.dma_start(dst, src).then_inc(a[f"merge_in{n % 2}"], 16)
            for g in range(3):
                pool.wait_ge(a[f"kv_stored{g}"], 16 * (5 if g else 2))

        @block.scalar
        def _(act):
            act.dma_start(m.const, ins["consts"]).then_inc(s["consts_in"], 16)
            act.dma_start(rope.rearrange("p n c -> p (n c)"), ins["rope_table"]).then_inc(s["consts_in"], 16)
            act.dma_start(m.cols, ins["cols"]).then_inc(s["consts_in"], 16)
            act.dma_start(m.head_rows, ins["head_rows"][0].partition_broadcast(P)).then_inc(s["consts_in"], 16)
            act.dma_start(m.head_cols, ins["head_cols"]).then_inc(s["consts_in"], 16)
            act.wait_ge(s["x_in"], 32)
            act.wait_ge(a["squares"], 1)
            for n in range(N_T):
                r = rows_of(n)
                nc.scalar.activation(xn[0:r, n], x[0:r, n], ACT.Square,
                                     accum_out=stat[0:r, n:n + 1]).then_inc(a["squares"], 1)
            act.wait_ge(a["inverse"], 1)
            nc.scalar.activation(stat[:, 16:21], stat[:, 8:13], ACT.Sqrt).then_inc(a["roots"], 1)

            def keep_v(g):
                for t in range(5):
                    unit = 15 * g + 10 + t
                    act.wait_ge(s["proj_ready"], unit + 1)
                    if g == 2 and t == 0:
                        act.wait_ge(a["group_done"], 1)
                        act.wait_ge(a["kv_stored0"], 32)
                    dst = m.kv_s[:, g, 512:1024] if t == 4 else kv_buf[g % 2][:, t, 512:1024]
                    r = rows_of(t)
                    nc.scalar.copy(dst, bank[unit % 3][0:r, :]).then_inc(s[f"proj_free{unit % 3}"], 1)
                    act.wait_ge(s[f"proj_free{unit % 3}"], unit // 3 + 1)
                    act.sem_inc(a["v_rows"], 1)

            def turned(key, dst):
                i = turn_at[key]
                act.wait_ge(a["turn_ready"], i + 1)
                src = bank[5 + i % 2][:, :].rearrange("p (c t) -> p c t", c=4)
                nc.scalar.copy(dst, src).then_inc(a["turn_free"], 1)

            def exps(g, v):
                w = 2 if g == 0 and v >= 2 else 1
                act.wait_ge(a["max_ready"], 8 * g + v + 1)
                for hh in range(4):
                    last = nc.scalar.activation(
                        score[v % 2][:, hh, 0:w], score[v % 2][:, hh, 0:w], ACT.Exp, scale=SCALE,
                        bias=neg_max[v % 2][:, hh:hh + 1],
                        accum_out=head_rows[:, v // 2, 2 * hh + v % 2, 64:65])
                last.then_inc(a["prob_ready"], 1)

            def attend(g):
                for t in range(4):
                    turned(("q", g, t), qT[:, :, P * t:P * t + P])
                    turned(("k", g, t), kT[:, :, P * t:P * t + P])
                if g:
                    act.wait_ge(a["head_stored"], 64 * g)
                exps(g, 0)
                for v in range(8):
                    if 8 * g + v >= 2:
                        act.wait_ge(a["out_ready"], 8 * g + v - 1)
                    for w in range(2 if g == 0 and v >= 2 else 1):
                        turned(("p", g, v, w), probT[v % 2][:, w])
                    if v < 7:
                        exps(g, v + 1)
                    act.wait_ge(a["out_ready"], 8 * g + v + 1)
                    nc.scalar.copy(head_rows[:, v // 2, v % 2:8:2, 0:64],
                                   bank[7][:, 0:256].rearrange("p (h c) -> p h c", h=4)).then_inc(a["out_kept"], 1)

            keep_v(0)
            keep_v(1)
            attend(0)
            keep_v(2)
            attend(1)
            attend(2)
            for n in range(4):
                act.wait_ge(a["merge_max"], n + 1)
                nc.scalar.activation(merge_w, merge_w, ACT.Exp, scale=SCALE).then_inc(a["merge_exp"], 1)
                turned(("att", n), m.attT[:, :, P * n:P * n + P])
            act.wait_ge(a["turn_free"], len(turns))

        @block.vector
        def _(dve):
            link = lambda i: sh.dve(dve, i)
            link(nc.vector.memset(stat[:, :], 1.0))
            dve.sem_inc(a["squares"], 1)
            dve.wait_ge(s["x_in"], 32)
            dve.wait_ge(a["squares"], 1 + N_T)
            link(nc.vector.tensor_scalar(stat[:, 0:5], stat[:, 0:5], 1.0 / D_MODEL, EPS, ALU.mult, ALU.add))
            nc.vector.reciprocal(stat[:, 8:13], stat[:, 0:5]).then_inc(a["inverse"], 1)
            dve.wait_ge(a["roots"], 1)
            for n in range(N_T):
                r = rows_of(n)
                nc.vector.tensor_scalar(xn[0:r, n], x[0:r, n], stat[0:r, 16 + n:17 + n], None,
                                        ALU.mult).then_inc(a["scaled"], 1)
            dve.wait_ge(s["consts_in"], 80)
            for n in range(N_T):
                r = rows_of(n)
                for half in range(2):
                    dve.wait_ge(a["turned"], 2 * n + half + 1)
                    src = bank[5 + half][:, :].rearrange("p (c t) -> p c t", c=4)[:, :, 0:r]
                    g = m.norm_mix[:, 4 * half:4 * half + 4].unsqueeze(2).to_broadcast([P, 4, r])
                    nc.vector.tensor_tensor(m.hT[:, 4 * half:4 * half + 4, P * n:P * n + r], src, g,
                                            ALU.mult).then_inc(a["columns"], 1)

            def rope_rows(g):
                for j in range(2):
                    for t in range(5):
                        unit = 15 * g + 5 * j + t
                        r = rows_of(t)
                        dve.wait_ge(s["proj_ready"], unit + 1)
                        if g == 2 and j == 0 and t == 0:
                            dve.wait_ge(a["group_done"], 1)
                            dve.wait_ge(a["kv_stored0"], 32)
                        tab = rope[0:r, 12 if t == 4 else 4 * g + t]
                        src = bank[unit % 3][0:r, :].rearrange("p (h c) -> p h c", h=8)
                        ra = rope_a[0:r].rearrange("p (h c) -> p h c", h=8)
                        rb = rope_b[0:r].rearrange("p (h c) -> p h c", h=8)
                        cos = tab[:, 0:64].unsqueeze(1).to_broadcast([r, 8, 64])
                        neg_sin = tab[:, 64:96].unsqueeze(1).to_broadcast([r, 8, 32])
                        sin = tab[:, 96:128].unsqueeze(1).to_broadcast([r, 8, 32])
                        nc.vector.tensor_tensor(ra, src, cos, ALU.mult)
                        nc.vector.tensor_tensor(rb[:, :, 0:32], src[:, :, 32:64], neg_sin, ALU.mult)
                        nc.vector.tensor_tensor(rb[:, :, 32:64], src[:, :, 0:32], sin,
                                                ALU.mult).then_inc(s[f"proj_free{unit % 3}"], 1)
                        dve.wait_ge(s[f"proj_free{unit % 3}"], unit // 3 + 1)
                        if t == 4:
                            dst = m.q_s[:, g] if j == 0 else m.kv_s[:, g, 0:512]
                        else:
                            dst = q_buf[g % 2][:, t] if j == 0 else kv_buf[g % 2][:, t, 0:512]
                        nc.vector.tensor_tensor(dst, rope_a[0:r], rope_b[0:r], ALU.add).then_inc(a["qk_rows"], 1)
                        dve.wait_ge(a["qk_rows"], 10 * g + 5 * j + t + 1)

            def maxima(g):
                for v in range(8):
                    w = 2 if g == 0 and v >= 2 else 1
                    dve.wait_ge(a["score_ready"], 8 * g + v + 1)
                    if v >= 2:
                        dve.wait_ge(a["turn_ready"], turn_at[("p", g, v - 2, 1 if g == 0 and v >= 4 else 0)] + 1)
                    elif g:
                        dve.wait_ge(a["turn_ready"], turn_at[("p", g - 1, v + 6, 1 if g == 1 else 0)] + 1)
                    buf = score[v % 2]
                    mask = m.c(C_CAUSAL if g < 2 else C_RES)
                    srcs = [(3, mask), (4, m.c(C_PREV))][:w]
                    for i, (b, mk) in enumerate(srcs):
                        last = nc.vector.tensor_tensor(buf[:, :, i, :], bank[b][:, :].rearrange("p (h k) -> p h k", h=4),
                                                       mk.unsqueeze(1).to_broadcast([P, 4, P]), ALU.add)
                    last.then_inc(a["score_free"], 1)
                    dve.wait_ge(a["score_free"], 8 * g + v + 1)
                    top = head_rows[:, v // 2, v % 2:8:2, 65]
                    if g and v == 0:
                        dve.wait_ge(a["head_stored"], 64 * g)
                    link(nc.vector.tensor_reduce(top, buf[:, :, 0:w, :], XY_AXIS, ALU.max))
                    nc.vector.tensor_scalar(neg_max[v % 2], top, -SCALE, None, ALU.mult).then_inc(a["max_ready"], 1)

            def merge(n):
                dve.wait_ge(a[f"merge_in{n % 2}"], 16 * (n // 2 + 1))
                rows = merge_in[n % 2]
                link(nc.vector.tensor_tensor(merge_max, rows[:, 0, :, 65], rows[:, 1, :, 65], ALU.max))
                link(nc.vector.tensor_tensor(merge_max, merge_max, rows[:, 2, :, 65], ALU.max))
                nc.vector.tensor_tensor(merge_w, rows[:, :, :, 65], merge_max.unsqueeze(1).to_broadcast([P, 3, 8]),
                                        ALU.subtract).then_inc(a["merge_max"], 1)
                dve.wait_ge(a["merge_exp"], n + 1)
                link(nc.vector.tensor_tensor(merge_den, merge_w, rows[:, :, :, 64], ALU.mult))
                link(nc.vector.tensor_reduce(merge_sum, merge_den.rearrange("p g h -> p h g"), X_AXIS, ALU.add))
                link(nc.vector.reciprocal(merge_sum, merge_sum))
                link(nc.vector.tensor_tensor(merge_w, merge_w, merge_sum.unsqueeze(1).to_broadcast([P, 3, 8]), ALU.mult))
                if n:
                    dve.wait_ge(a["turn_ready"], turn_at[("att", n - 1)] + 1)
                for g in range(3):
                    out = (rope_a, rope_b, rope_b)[g].rearrange("p (h c) -> p h c", h=8)
                    link(nc.vector.tensor_tensor(out, rows[:, g, :, 0:64],
                                                 merge_w[:, g].unsqueeze(2).to_broadcast([P, 8, 64]), ALU.mult))
                    if g == 1:
                        link(nc.vector.tensor_tensor(rope_a, rope_a, rope_b, ALU.add))
                nc.vector.tensor_tensor(rope_a, rope_a, rope_b, ALU.add).then_inc(a["merge_rows"], 1)

            rope_rows(0)
            rope_rows(1)
            maxima(0)
            rope_rows(2)
            maxima(1)
            maxima(2)
            for n in range(4):
                merge(n)

        @block.tensor
        def _(pe):
            pe.wait_ge(s["consts_in"], 80)
            for n in range(N_T):
                r = rows_of(n)
                pe.wait_ge(a["scaled"], n + 1)
                for half in range(2):
                    if n:
                        pe.wait_ge(a["columns"], 2 * n + half - 1)
                    for cc in range(4):
                        k = 4 * half + cc
                        last = nc.tensor.transpose(bank[5 + half][:, P * cc:P * cc + r], xn[0:r, n, P * k:P * k + P],
                                                   ident[0:r, 0:r])
                    last.then_inc(a["turned"], 1)
            pe.wait_ge(a["columns"], 2 * N_T)

            def project(g):
                for j in range(3):
                    b = 3 * g + j
                    pe.wait_ge(s[f"ring_in{b % 2}"], 16 * (b // 2 + 1))
                    for t in range(5):
                        unit = 5 * b + t
                        if unit >= 3:
                            pe.wait_ge(s[f"proj_free{unit % 3}"], unit // 3)
                        for k in range(8):
                            last = nc.tensor.matmul(bank[unit % 3][0:rows_of(t), :], token_columns(k, g, t),
                                                    m.slot[b % 2][:, 512 * k:512 * k + 512],
                                                    start=(k == 0), stop=(k == 7))
                        last.then_inc(s["proj_ready"], 1)

            def turn(key, srcs):
                i = turn_at[key]
                if i >= 2:
                    pe.wait_ge(a["turn_free"], i - 1)
                for cc in range(4):
                    last = nc.tensor.transpose(bank[5 + i % 2][:, P * cc:P * cc + P], srcs(cc), ident)
                last.then_inc(a["turn_ready"], 1)

            def scores(g, v):
                t, u = v // 2, v % 2
                if 8 * g + v:
                    pe.wait_ge(a["score_free"], 8 * g + v)
                for w in range(2 if g == 0 and t else 1):
                    for hh in range(4):
                        h = 2 * hh + u
                        lo = 64 * u
                        last = nc.tensor.matmul(bank[3 + w][:, P * hh:P * hh + P],
                                                qT[lo:lo + 64, h // 2, P * t:P * t + P],
                                                kT[lo:lo + 64, h // 2, P * (t - w):P * (t - w) + P],
                                                start=True, stop=True)
                last.then_inc(a["score_ready"], 1)

            def attend(g):
                pe.wait_ge(a["qk_rows"], 10 * g + 10)
                for t in range(4):
                    turn(("q", g, t), lambda cc: q_buf[g % 2][:, t, P * cc:P * cc + P])
                    turn(("k", g, t), lambda cc: kv_buf[g % 2][:, t, P * cc:P * cc + P])
                pe.wait_ge(a["turn_free"], turn_at[("k", g, 3)] + 1)
                pe.wait_ge(a["v_rows"], 5 * g + 5)
                scores(g, 0)
                for v in range(8):
                    t, u = v // 2, v % 2
                    wide = range(2 if g == 0 and t else 1)
                    if v < 7:
                        scores(g, v + 1)
                    pe.wait_ge(a["prob_ready"], 8 * g + v + 1)
                    for w in wide:
                        turn(("p", g, v, w), lambda cc: score[v % 2][:, cc, w, :])
                    pe.wait_ge(a["turn_free"], turn_at[("p", g, v, wide[-1])] + 1)
                    if 8 * g + v:
                        pe.wait_ge(a["out_kept"], 8 * g + v)
                    for hh in range(4):
                        h = 2 * hh + u
                        for w in wide:
                            last = nc.tensor.matmul(bank[7][:, 64 * hh:64 * hh + 64], probT[v % 2][:, w, hh],
                                                    kv_buf[g % 2][:, t - w, 512 + 64 * h:576 + 64 * h],
                                                    start=(w == 0), stop=(w == wide[-1]))
                    last.then_inc(a["out_ready"], 1)
                pe.wait_ge(a["out_ready"], 8 * g + 8)
                pe.sem_inc(a["group_done"], 1)

            project(0)
            project(1)
            attend(0)
            project(2)
            attend(1)
            attend(2)
            for n in range(4):
                pe.wait_ge(a["merge_rows"], n + 1)
                turn(("att", n), lambda cc: rope_a[:, P * cc:P * cc + P])


def attention_sample(sh):
    nc, ins, m, bank, s = sh.nc, sh.ins, sh.m, sh.bank, sh.s
    keys = (128, 128, 64)
    cache = m.at(0, 24576).rearrange("p (g b n) -> p g b n", g=3, b=N_S)
    product = [m.at(24576 + 512 * i, 512) for i in range(2)]
    by_key = m.at(25600, 192).rearrange("p (g r) -> p g r", g=3)
    score_rows = m.at(25792, 323, 64)
    prob_cols = m.at(26120, 192).rearrange("p (g r) -> p g r", g=3)
    new_diag = m.at(26312, 192, 64).rearrange("p (g r) -> p g r", g=3)
    new_cols = m.at(26504, 192, 8).rearrange("p (g r) -> p g r", g=3)
    new_score = m.at(26696, 24, 8).rearrange("p (g h) -> p g h", g=3)
    new_spread = m.at(26720, 192, 8).rearrange("p (g r) -> p g r", g=3)
    row_max, neg_max, row_sum, row_inv = (m.at(26912 + i, 1, 64) for i in range(4))
    new_prod = m.at(26920, 1536, 8).rearrange("p (g n) -> p g n", g=3)
    ident = m.c(C_IDENT)

    with ExitStack() as c:
        names = ("query_ready", "query_free", "key_cols", "new_ready", "rows_ready", "max_ready", "exps", "probs",
                 "cols_ready", "cols_kept", "diag_ready", "new_turned", "out_ready", "out_kept")
        a = stage_semaphores(nc, c, "b_", names)
        cache_in = list(stage_semaphores(nc, c, "b_cache_in", [str(i) for i in range(24)]).values())
        block = c.enter_context(nc.Block())

        def load(eng, b):
            for g in range(3):
                stride = (1, 4, 16)[g]
                eng.dma_start(cache[0:keys[g], g, b], ins[f"cache{g}"][b, 0::stride]).then_inc(
                    cache_in[8 * g + b], 16)

        @block.sync
        def _(sp):
            for b in range(N_S):
                load(sp, b)

        @block.scalar
        def _(act):
            act.wait_ge(a["max_ready"], 1)
            nc.scalar.activation(score_rows, score_rows, ACT.Exp, scale=SCALE, bias=neg_max,
                                 accum_out=row_sum).then_inc(a["exps"], 1)
            act.wait_ge(a["cols_ready"], 1)
            nc.scalar.copy(prob_cols[:, 0:2], bank[3][:, 0:128].rearrange("p (g r) -> p g r", g=2))
            nc.scalar.copy(prob_cols[0:64, 2], bank[3][0:64, 128:192]).then_inc(a["cols_kept"], 1)
            act.wait_ge(a["new_turned"], 1)
            nc.scalar.copy(new_cols, bank[4][0:8, 0:192].rearrange("p (g r) -> p g r", g=3)).then_inc(a["cols_kept"], 1)

        @block.vector
        def _(dve):
            link = lambda i: sh.dve(dve, i)
            link(nc.vector.tensor_tensor(new_prod, m.q_s, m.kv_s[:, :, 0:512], ALU.mult))
            link(nc.vector.tensor_reduce(new_score, new_prod.rearrange("p g (h c) -> p g h c", h=8), X_AXIS, ALU.add))
            for g in range(3):
                last = nc.vector.tensor_tensor(
                    new_spread[:, g].rearrange("p (b h) -> p b h", b=8),
                    m.c(C_DELTA, 64, 8).rearrange("p (b h) -> p b h", b=8),
                    new_score[:, g].unsqueeze(1).to_broadcast([8, 8, 8]), ALU.mult)
            last.then_inc(a["new_ready"], 1)
            i = 0
            for b in range(N_S):
                for g in range(3):
                    dve.wait_ge(cache_in[8 * g + b], 16)
                    dve.wait_ge(a["query_ready"], i + 1)
                    k = keys[g]
                    nc.vector.tensor_tensor(product[i % 2][0:k], cache[0:k, g, b, 0:512], bank[i % 2][0:k, :],
                                            ALU.mult).then_inc(a["query_free"], 1)
                    dve.wait_ge(a["query_free"], i + 1)
                    nc.vector.tensor_reduce(by_key[0:k, g, 8 * b:8 * b + 8],
                                            product[i % 2][0:k].rearrange("p (h c) -> p h c", h=8), X_AXIS,
                                            ALU.add).then_inc(a["key_cols"], 1)
                    i += 1
            dve.wait_ge(a["rows_ready"], 1)
            nc.vector.tensor_copy(score_rows[:, 0:320], bank[2][0:64, 0:320])
            link(nc.vector.tensor_copy(score_rows[:, 320:323], bank[2][0:64, 320:323]))
            link(nc.vector.tensor_reduce(row_max, score_rows, X_AXIS, ALU.max))
            nc.vector.tensor_scalar(neg_max, row_max, -SCALE, None, ALU.mult).then_inc(a["max_ready"], 1)
            dve.wait_ge(a["exps"], 1)
            link(nc.vector.reciprocal(row_inv, row_sum))
            nc.vector.tensor_scalar(score_rows, score_rows, row_inv, None, ALU.mult).then_inc(a["probs"], 1)
            dve.wait_ge(a["probs"], 1)
            for g in range(3):
                last = nc.vector.tensor_scalar(new_diag[:, g], m.c(C_IDENT, 64, 64), score_rows[:, 320 + g:321 + g],
                                               None, ALU.mult)
            last.then_inc(a["diag_ready"], 1)
            dve.wait_ge(a["out_ready"], 1)
            out = bank[5][:, 0:64].rearrange("p (b c w) -> p w c b", b=8, w=2)
            nc.vector.tensor_copy(m.attT[0:64, :, SEQ:T_ALL], out[0:64, 0])
            link(nc.vector.tensor_copy(m.attT[64:128, :, SEQ:T_ALL], out[64:128, 1]))

        @block.tensor
        def _(pe):
            i = 0
            for b in range(N_S):
                for g in range(3):
                    if i >= 2:
                        pe.wait_ge(a["query_free"], i - 1)
                    nc.tensor.matmul(bank[i % 2][:, :], m.c(C_SEL + P * b, P, 8), m.q_s[:, g],
                                     start=True, stop=True).then_inc(a["query_ready"], 1)
                    i += 1
            pe.wait_ge(a["key_cols"], 24)
            pe.wait_ge(a["new_ready"], 1)
            for g in range(3):
                k = keys[g]
                nc.tensor.transpose(bank[2][0:64, P * g:P * g + k], by_key[0:k, g], ident[0:k, 0:k])
            for g in range(3):
                last = nc.tensor.matmul(bank[2][0:64, 320 + g:321 + g], new_spread[:, g], m.c(C_ONES, 1, 8),
                                        start=True, stop=True)
            last.then_inc(a["rows_ready"], 1)
            pe.wait_ge(a["probs"], 1)
            for g in range(3):
                k = keys[g]
                last = nc.tensor.transpose(bank[3][0:k, 64 * g:64 * g + 64], score_rows[:, P * g:P * g + k],
                                           ident[0:64, 0:64])
            last.then_inc(a["cols_ready"], 1)
            pe.wait_ge(a["diag_ready"], 1)
            nc.tensor.matmul(bank[4][0:8, 0:192], m.c(C_IND, 8, 64), new_diag, start=True,
                             stop=True).then_inc(a["new_turned"], 1)
            pe.wait_ge(a["cols_kept"], 2)
            for b in range(N_S):
                for pair in range(4):
                    at = 8 * b + 2 * pair
                    dst = bank[5][:, at:at + 2]
                    for g in range(3):
                        k = keys[g]
                        nc.tensor.matmul(dst, cache[0:k, g, b, 512 + P * pair:640 + P * pair],
                                         prob_cols[0:k, g, at:at + 2], start=(g == 0), stop=False)
                    for g in range(3):
                        last = nc.tensor.matmul(dst, m.kv_s[:, g, 512 + P * pair:640 + P * pair],
                                                new_cols[:, g, at:at + 2], start=False, stop=(g == 2))
            last.then_inc(a["out_ready"], 1)


def ssd_branch(sh):
    nc, ins, outs, m, bank, s = sh.nc, sh.ins, sh.outs, sh.m, sh.bank, sh.s
    NCK, G = 4, SSD_GROUPS
    xpad = [m.at(2060 * i, 2060).rearrange("p (c t) -> p c t", c=4) for i in range(2)]
    xc = [m.at(4120 + 2080 * i, 2080).rearrange("p (c t) -> p c t", c=4) for i in range(2)]
    tanh = m.at(8280, 2080).rearrange("p (c t) -> p c t", c=4)
    update = m.at(8280, 2048).rearrange("p (c b n) -> p c b n", c=2, b=8)
    z_tanh = m.at(10360, 512)
    rows = [m.at(10872 + 1536 * i, 1536).rearrange("p (k c) -> p k c", k=4) for i in range(2)]
    xdt = m.at(13944, 1024).rearrange("p (k e c) -> p k e c", k=4, e=4)
    xdt_end = m.at(14968, 1024).rearrange("p (k e c) -> p k e c", k=4, e=4)
    y = sh.y = m.at(26216, 8192).rearrange("p (k c) -> p k c", k=4)
    z = m.at(15992, 2048).rearrange("p (k c) -> p k c", k=4)
    decay = [m.at(18040 + 512 * i, 512).rearrange("p (e t) -> p e t", e=4) for i in range(2)]
    cb = [m.at(19064 + 128 * i, 128) for i in range(2)]
    hT = [m.at(19320 + 256 * i, 256) for i in range(2)]
    off = m.at(19832, 256)
    at = 20088
    per_head = [m.at(at + 128 * i, 128) for i in range(6)]
    dt, dta, acs, to_end, from_start, chunk_decay = per_head
    by_head = lambda t: t.rearrange("p (k h) -> p k h", k=4)
    at += 768
    state = m.at(at, 2048).rearrange("p (c b n) -> p c b n", c=2, b=8)
    at += 2048
    conv_state = m.at(at, 768).rearrange("p (c b w) -> p c b w", c=32, b=8)
    at += 768
    conv_tail = m.at(at, 96).rearrange("p (c w) -> p c w", c=32)
    at += 96
    s_cols = m.at(at, 17, 32)
    at += 20
    s_head = m.at(at, 272).rearrange("p (c j) -> p c j", c=16)
    at += 272
    ys = sh.ys = m.small[:, 0:128].rearrange("p (c b) -> p c b", c=16)
    zs = m.at(at, 128).rearrange("p (c b) -> p c b", c=16)
    at += 128
    zs_tanh = m.at(at, 32).rearrange("p (c b) -> p c b", c=4)
    at += 32
    h_out = m.at(at, 256).rearrange("p (c n) -> p c n", c=2)
    at += 256
    window = m.at(at, 128).rearrange("p (c b w) -> p c b w", c=4, b=8)
    at += 128
    window_w = m.at(at, 128).rearrange("p (c b w) -> p c b w", c=4, b=8)
    at += 128
    half_w = m.at(at, 128).rearrange("p (c w) -> p c w", c=32)
    at += 128
    half_b = m.at(at, 32)
    at += 32
    w_dt = m.at(at, 256)
    at += 256
    soft_a, soft_b, soft_c = (m.at(at + 136 * i, 136) for i in range(3))
    at += 408
    exp_a = m.at(at, 33)
    at += 36
    xdt_s = m.at(at, 16).rearrange("p (c b) -> p c b", c=2)
    at += 16
    skip_s = m.at(at, 16).rearrange("p (c b) -> p c b", c=2)
    at += 16
    assert at <= 26216

    seq = [("x", 0), ("x", 1)]
    for g in range(1, G):
        if g % 2:
            seq.append(("z", g // 2))
        if g + 1 < G:
            seq.append(("x", g + 1))
    place = {k: i for i, k in enumerate(seq)}

    turns = [(w, g, k) for g in range(G) for w, n in (("rows", 4), ("state", 4), ("last", 1)) for k in range(n)]
    turn_at = {k: i for i, k in enumerate(turns)}

    with ExitStack() as c:
        names = ("proj_ready", "proj_free0", "proj_free1", "small_ready", "small_free", "small_in", "dt_ready",
                 "dt_a", "dt_b", "dt_c", "dt_done", "sums_ready", "sums_kept", "expand_ready", "expand_kept",
                 "pad_ready", "conv_ready", "tanh_ready", "xc_ready", "z_tanh", "z_ready", "turn_ready",
                 "turn_free", "xdt_ready", "acs_ready", "acs_free", "cb_ready", "cb_free", "diff_ready",
                 "exp_ready", "mix_ready", "y_ready", "y_free", "skip_ready", "h_ready", "bc_ready", "bc_free",
                 "state_in", "state_decayed", "state_new", "state_out", "h_stored", "conv_in", "conv_rows",
                 "window_ready", "window_used", "pads", "conv_stored", "y_gated", "wide_free")
        a = stage_semaphores(nc, c, "c_", names)
        block = c.enter_context(nc.Block())

        @block.sync
        def _(sp):
            sp.dma_start(w_dt, ins["w_dt"]).then_inc(a["small_in"], 16)
            sp.dma_start(conv_state.rearrange("p c b w -> p (c b w)"), ins["state_conv"]).then_inc(a["conv_in"], 16)
            loaded = 2
            for g in range(G):
                upto = min(place[("x", min(g + 1, G - 1))] + 3, len(seq) + 2)
                if g == G - 1:
                    upto = len(seq) + 2
                if g:
                    sp.wait_ge(a["state_out"], 32 * g)
                    sp.wait_ge(a["bc_free"], 4 * g)
                for half in range(2):
                    r = 256 * g + P * half
                    sp.dma_start(state[:, half], ins["state_ssm"][:, r:r + P].rearrange("b p n -> p b n")).then_inc(
                        a["state_in"], 16)
                while loaded < upto:
                    sp.wait_ge(a["proj_ready"], 4 * (loaded - 1))
                    b = B_SSD + loaded
                    sp.dma_start(m.slot[b % 2], ins["stream"][b]).then_inc(s[f"ring_in{b % 2}"], 16)
                    loaded += 1
                sp.wait_ge(a["turn_free"], turn_at[("last", g, 0)] + 1)
                sp.dma_start(outs["ssm_prompt"][256 * g:256 * g + 256].rearrange("(c p) n -> p c n", p=P),
                             h_out).then_inc(a["h_stored"], 16)
                sp.wait_ge(a["state_new"], g + 1)
                for half in range(2):
                    r = 256 * g + P * half
                    sp.dma_start(outs["ssm_sample"][:, r:r + P].rearrange("b p n -> p b n"),
                                 state[:, half]).then_inc(a["state_out"], 16)
            sp.wait_ge(a["conv_rows"], 2 * G)
            sp.dma_start(outs["conv_prompt"], conv_tail.rearrange("p c w -> p (c w)")).then_inc(a["conv_stored"], 16)
            sp.dma_start(outs["conv_sample"], conv_state.rearrange("p c b w -> p (c b w)")).then_inc(
                a["conv_stored"], 16)
            sp.wait_ge(a["conv_stored"], 32)
            sp.wait_ge(a["state_out"], 32 * G)
            sp.wait_ge(a["h_stored"], 16 * G)

        @block.gpsimd
        def _(pool):
            for i in range(2):
                nc.gpsimd.memset(xpad[i][:, :, 0:3], 0.0).then_inc(a["pads"], 1)

            def tails(g):
                pool.wait_ge(a["pad_ready"], 4 * g + 4)
                nc.gpsimd.tensor_copy(conv_tail[:, 4 * g:4 * g + 4], xpad[g % 2][:, :, 512:515]).then_inc(
                    a["conv_rows"], 1)
                pool.wait_ge(a["window_ready"], g + 1)
                nc.gpsimd.tensor_copy(conv_state[:, 4 * g:4 * g + 4], window[:, :, :, 1:4]).then_inc(a["conv_rows"], 1)

            tails(0)
            for g in range(G):
                if g + 1 < G:
                    tails(g + 1)
                pool.wait_ge(a["turn_free"], turn_at[("rows", g, 3)] + 1)
                x_rows = rows[g % 2][:, :, 0:256].rearrange("p k (e c) -> p k e c", e=4)
                for k in range(NCK):
                    last = nc.gpsimd.tensor_tensor(
                        y[:, k, 256 * g:256 * g + 256].rearrange("p (e c) -> p e c", e=4), x_rows[:, k],
                        m.head_rows[:, 64 + 4 * g:68 + 4 * g].unsqueeze(2).to_broadcast([P, 4, 64]), ALU.mult)
                last.then_inc(a["skip_ready"], 1)
                for k in range(NCK):
                    i = NCK * g + k
                    if k == 1:
                        pool.wait_ge(a["state_in"], 32 * (g + 1))
                        if g == 0:
                            pool.wait_ge(a["expand_kept"], 1)
                        for half in range(2):
                            last = nc.gpsimd.tensor_tensor(
                                state[:, half], state[:, half],
                                s_head[:, 2 * g + half, 8:16].unsqueeze(2).to_broadcast([P, 8, P]), ALU.mult)
                        last.then_inc(a["state_decayed"], 1)
                    pool.wait_ge(a["exp_ready"], i + 1)
                    pool.wait_ge(a["cb_free"], i + 1)
                    nc.gpsimd.tensor_tensor(decay[i % 2], decay[i % 2], cb[i % 2].unsqueeze(1).to_broadcast([P, 4, P]),
                                            ALU.mult).then_inc(a["mix_ready"], 1)

        @block.scalar
        def _(act):
            act.wait_ge(a["dt_a"], 1)
            nc.scalar.activation(soft_b, soft_b, ACT.Exp, scale=-1.0).then_inc(a["dt_b"], 1)
            nc.scalar.activation(exp_a[:, 0:32], m.head_rows[:, 32:64], ACT.Exp)
            nc.scalar.activation(exp_a[0:32, 32:33], m.head_cols[:, 1:2], ACT.Exp).then_inc(a["dt_b"], 1)
            act.wait_ge(a["dt_c"], 1)
            nc.scalar.activation(soft_b, soft_b, ACT.Ln).then_inc(a["dt_b"], 1)
            act.wait_ge(a["dt_done"], 1)
            nc.scalar.activation(s_cols[:, 8:16], s_cols[:, 8:16], ACT.Exp).then_inc(a["dt_b"], 1)
            act.wait_ge(a["sums_kept"], 1)
            nc.scalar.activation(from_start, acs, ACT.Exp)
            nc.scalar.activation(to_end, to_end, ACT.Exp)
            nc.scalar.activation(chunk_decay, chunk_decay, ACT.Exp).then_inc(a["dt_b"], 1)
            act.wait_ge(a["pads"], 2)

            def pads(g):
                for t in range(4):
                    unit = 4 * place[("x", g)] + t
                    act.wait_ge(a["proj_ready"], unit + 1)
                    if g >= 2 and t == 0:
                        act.wait_ge(a["conv_ready"], g - 1)
                        act.wait_ge(a["conv_rows"], 2 * (g - 1))
                    nc.scalar.copy(xpad[g % 2][:, t, 3:515], bank[unit % 2][:, :]).then_inc(
                        a[f"proj_free{unit % 2}"], 1)
                    act.wait_ge(a[f"proj_free{unit % 2}"], unit // 2 + 1)
                    act.sem_inc(a["pad_ready"], 1)

            def gate(j):
                for t in range(4):
                    unit = 4 * place[("z", j)] + t
                    act.wait_ge(a["proj_ready"], unit + 1)
                    if 4 * j + t:
                        act.wait_ge(a["z_ready"], 5 * j + t)
                    nc.scalar.activation(z_tanh, bank[unit % 2][:, :], ACT.Tanh, scale=0.5).then_inc(a["z_tanh"], 1)
                act.wait_ge(a["small_ready"], place[("z", j)] + 1)
                nc.scalar.activation(zs_tanh, bank[2][:, 0:32].rearrange("p (c b) -> p c b", c=4), ACT.Tanh,
                                     scale=0.5).then_inc(a["z_tanh"], 1)

            def silu(g):
                act.wait_ge(a["conv_ready"], g + 1)
                nc.scalar.activation(tanh, xc[g % 2], ACT.Tanh).then_inc(a["tanh_ready"], 1)

            pads(0)
            silu(0)
            for g in range(G):
                if g % 2:
                    gate(g // 2)
                if g + 1 < G:
                    pads(g + 1)
                for k in range(NCK):
                    i = turn_at[("rows", g, k)]
                    act.wait_ge(a["turn_ready"], i + 1)
                    if g >= 2 and k == 0:
                        act.wait_ge(a["y_free"], NCK * (g - 1))
                        act.wait_ge(a["skip_ready"], g - 1)
                    nc.scalar.copy(rows[g % 2][:, k], bank[3][:, 0:384]).then_inc(a["turn_free"], 1)
                if g + 1 < G:
                    silu(g + 1)
                for k in range(NCK):
                    i = NCK * g + k
                    act.wait_ge(a["diff_ready"], i + 1)
                    nc.scalar.activation(decay[i % 2], decay[i % 2], ACT.Exp).then_inc(a["exp_ready"], 1)
                act.wait_ge(a["turn_ready"], turn_at[("last", g, 0)] + 1)
                if g:
                    act.wait_ge(a["h_stored"], 16 * g)
                nc.scalar.copy(h_out, bank[3][:, 0:256].rearrange("p (c n) -> p c n", c=2)).then_inc(a["turn_free"], 1)

        @block.vector
        def _(dve):
            link = lambda i: sh.dve(dve, i)
            nc.vector.tensor_scalar(half_w, m.conv_w, 0.5, None, ALU.mult)
            link(nc.vector.tensor_scalar(half_b, m.conv_b, 0.5, None, ALU.mult))
            link(nc.vector.memset(soft_a, 0.0))
            dve.wait_ge(a["dt_ready"], 1)
            nc.vector.tensor_tensor(by_head(soft_a[:, 0:128]), by_head(bank[5][:, 0:128]),
                                    m.head_rows[:, 0:32].unsqueeze(1).to_broadcast([P, 4, 32]), ALU.add)
            link(nc.vector.tensor_scalar(soft_a[0:32, 128:136], bank[6][0:32, 0:8], m.head_cols[:, 0:1], None, ALU.add))
            link(nc.vector.tensor_scalar(soft_b, soft_a, -1.0, None, ALU.mult))
            nc.vector.tensor_tensor(soft_b, soft_b, soft_a, ALU.max).then_inc(a["dt_a"], 1)
            dve.wait_ge(a["dt_b"], 2)
            nc.vector.tensor_scalar(soft_b, soft_b, 1.0, None, ALU.add).then_inc(a["dt_c"], 1)
            dve.wait_ge(a["dt_b"], 3)
            link(nc.vector.scalar_tensor_tensor(soft_c, soft_a, 0.0, soft_b, ALU.max, ALU.add))
            nc.vector.tensor_copy(dt, soft_c[:, 0:128])
            nc.vector.tensor_copy(s_cols[:, 0:8], soft_c[0:32, 128:136])
            nc.vector.tensor_copy(s_cols[:, 16:17], m.head_cols[:, 2:3])
            nc.vector.tensor_scalar(s_cols[:, 8:16], soft_c[0:32, 128:136], exp_a[0:32, 32:33], -1.0, ALU.mult, ALU.mult)
            nc.vector.scalar_tensor_tensor(by_head(dta), by_head(soft_c[:, 0:128]), -1.0,
                                           exp_a[:, 0:32].unsqueeze(1).to_broadcast([P, 4, 32]), ALU.mult,
                                           ALU.mult).then_inc(a["dt_done"], 1)
            dve.wait_ge(a["sums_ready"], 1)
            nc.vector.tensor_copy(acs, bank[4][:, 0:128])
            link(nc.vector.tensor_copy(chunk_decay, bank[4][:, 128:256]))
            nc.vector.tensor_tensor(to_end, chunk_decay, acs, ALU.subtract).then_inc(a["sums_kept"], 1)
            dve.wait_ge(a["expand_ready"], 1)
            nc.vector.tensor_copy(s_head, bank[6][:, 0:272].rearrange("p (c j) -> p c j", c=16)).then_inc(
                a["expand_kept"], 1)
            dve.wait_ge(a["dt_b"], 5)
            dve.wait_ge(a["conv_in"], 16)

            def conv(g):
                dve.wait_ge(a["small_ready"], place[("x", g)] + 1)
                if g:
                    dve.wait_ge(a["conv_rows"], 2 * g)
                nc.vector.tensor_copy(window[:, :, :, 0:3], conv_state[:, 4 * g:4 * g + 4])
                nc.vector.tensor_copy(window[:, :, :, 3], bank[2][:, 0:32].rearrange("p (c b) -> p c b", c=4)).then_inc(
                    a["small_free"], 1)
                dve.wait_ge(a["small_free"], place[("x", g)] + 1)
                dve.sem_inc(a["window_ready"], 1)
                out = xc[g % 2]
                link(nc.vector.tensor_tensor(window_w, window,
                                             half_w[:, 4 * g:4 * g + 4].unsqueeze(2).to_broadcast([P, 4, 8, 4]),
                                             ALU.mult))
                if g >= 2:
                    dve.wait_ge(a["y_ready"], NCK * (g - 1))
                    dve.wait_ge(a["bc_ready"], 4 * (g - 1))
                link(nc.vector.tensor_reduce(out[:, :, 512:520], window_w, X_AXIS, ALU.add))
                nc.vector.tensor_tensor(out[:, :, 512:520], out[:, :, 512:520],
                                        half_b[:, 4 * g:4 * g + 4].unsqueeze(2).to_broadcast([P, 4, 8]), ALU.add)
                dve.wait_ge(a["pad_ready"], 4 * g + 4)
                for t in range(4):
                    w = half_w[:, 4 * g + t]
                    last = nc.vector.tensor_scalar(out[:, t, 0:512], xpad[g % 2][:, t, 0:512], w[:, 0:1],
                                                   half_b[:, 4 * g + t:4 * g + t + 1], ALU.mult, ALU.add)
                link(last)
                for j in range(1, 4):
                    for t in range(4):
                        last = nc.vector.scalar_tensor_tensor(out[:, t, 0:512], xpad[g % 2][:, t, j:j + 512],
                                                              half_w[:, 4 * g + t, j:j + 1], out[:, t, 0:512],
                                                              ALU.mult, ALU.add)
                    if j < 3:
                        link(last)
                last.then_inc(a["conv_ready"], 1)
                dve.wait_ge(a["tanh_ready"], g + 1)
                link(nc.vector.scalar_tensor_tensor(out, tanh, 1.0, out, ALU.add, ALU.mult))
                dve.sem_inc(a["xc_ready"], 1)

            def gate_values(j):
                for t in range(4):
                    unit = 4 * place[("z", j)] + t
                    dve.wait_ge(a["z_tanh"], 5 * j + t + 1)
                    nc.vector.scalar_tensor_tensor(z[:, t], z_tanh, 1.0, bank[unit % 2][:, :], ALU.add,
                                                   ALU.mult).then_inc(a[f"proj_free{unit % 2}"], 1)
                    dve.wait_ge(a[f"proj_free{unit % 2}"], unit // 2 + 1)
                    dve.sem_inc(a["z_ready"], 1)
                dve.wait_ge(a["z_tanh"], 5 * j + 5)
                nc.vector.scalar_tensor_tensor(zs[:, 4 * j:4 * j + 4], zs_tanh, 1.0,
                                               bank[2][:, 0:32].rearrange("p (c b) -> p c b", c=4), ALU.add,
                                               ALU.mult).then_inc(a["small_free"], 1)
                dve.wait_ge(a["small_free"], place[("z", j)] + 1)
                dve.sem_inc(a["z_ready"], 1)

            def decays(g, k):
                i = NCK * g + k
                dve.wait_ge(a["cb_ready"], i + 1)
                if i >= 2:
                    dve.wait_ge(a["mix_ready"], i - 1)
                    dve.wait_ge(a["y_ready"], i - 1)
                nc.vector.tensor_tensor(cb[i % 2], bank[5][:, 0:128], m.c(C_TRI), ALU.mult).then_inc(a["cb_free"], 1)
                dve.wait_ge(a["acs_ready"], i + 1)
                for e in range(4):
                    h = 32 * k + 4 * g + e
                    last = nc.vector.tensor_scalar(decay[i % 2][:, e], bank[4][:, P * e:P * e + P], acs[:, h:h + 1], 0.0,
                                                   ALU.subtract, ALU.min)
                last.then_inc(a["diff_ready"], 1)

            def ssd(g):
                dve.wait_ge(a["turn_free"], turn_at[("rows", g, 3)] + 1)
                if g:
                    dve.wait_ge(a["turn_ready"], turn_at[("state", g - 1, 3)] + 1)
                x_rows = rows[g % 2][:, :, 0:256].rearrange("p k (e c) -> p k e c", e=4)
                heads = slice(4 * g, 4 * g + 4)
                link(nc.vector.tensor_tensor(xdt, x_rows, by_head(dt)[:, :, heads].unsqueeze(3).to_broadcast([P, 4, 4, 64]),
                                             ALU.mult))
                nc.vector.tensor_tensor(xdt_end, xdt, by_head(to_end)[:, :, heads].unsqueeze(3).to_broadcast([P, 4, 4, 64]),
                                        ALU.mult).then_inc(a["xdt_ready"], 1)
                decays(g, 0)
                dve.wait_ge(a["skip_ready"], g + 1)
                for k in range(NCK):
                    i = NCK * g + k
                    if k + 1 < NCK:
                        decays(g, k + 1)
                    dve.wait_ge(a["y_ready"], i + 1)
                    yk = y[:, k, 256 * g:256 * g + 256]
                    if k:
                        nc.vector.tensor_tensor(off.rearrange("p (e c) -> p e c", e=4),
                                                bank[6][:, 256:512].rearrange("p (e c) -> p e c", e=4),
                                                by_head(from_start)[:, k, heads].unsqueeze(2).to_broadcast([P, 4, 64]),
                                                ALU.mult)
                    nc.vector.tensor_tensor(yk, yk, bank[6][:, 0:256], ALU.add).then_inc(a["y_free"], 1)
                    dve.wait_ge(a["y_free"], i + 1)
                    if k:
                        nc.vector.tensor_tensor(yk, yk, off, ALU.add)
                    if k:
                        link(nc.vector.tensor_tensor(
                            hT[k % 2].rearrange("p (e c) -> p e c", e=4), hT[(k - 1) % 2].rearrange("p (e c) -> p e c", e=4),
                            by_head(chunk_decay)[:, k, heads].unsqueeze(2).to_broadcast([P, 4, 64]), ALU.mult))
                    t = turn_at[("state", g, k)]
                    dve.wait_ge(a["turn_ready"], t + 1)
                    if k:
                        last = nc.vector.tensor_tensor(hT[k % 2], hT[k % 2], bank[3][:, 0:256], ALU.add)
                    else:
                        last = nc.vector.tensor_copy(hT[0], bank[3][:, 0:256])
                    last.then_inc(a["turn_free"], 1)
                    dve.wait_ge(a["turn_free"], t + 1)
                    dve.sem_inc(a["h_ready"], 1)

            def sample(g):
                xs = xc[g % 2][:, 0:2, 512:520]
                nc.vector.tensor_tensor(skip_s, xs, s_head[:, 2 * g:2 * g + 2, 16:17].to_broadcast([P, 2, 8]), ALU.mult)
                link(nc.vector.tensor_tensor(xdt_s, xs, s_head[:, 2 * g:2 * g + 2, 0:8], ALU.mult))
                for q in range(4):
                    i = 4 * g + q
                    part = slice(4 * (q % 2), 4 * (q % 2) + 4)
                    dve.wait_ge(a["bc_ready"], i + 1)
                    wide = bank[7][:, :].rearrange("p (b n) -> p b n", b=4)
                    for half in range(2):
                        other = state[:, half, part] if q >= 2 else \
                            xdt_s[:, half, part].unsqueeze(2).to_broadcast([P, 4, P])
                        last = nc.vector.tensor_tensor(update[:, half, part], wide, other, ALU.mult)
                    last.then_inc(a["bc_free"], 1)
                    dve.wait_ge(a["bc_free"], i + 1)
                    if q == 1:
                        dve.wait_ge(a["state_decayed"], g + 1)
                        nc.vector.tensor_tensor(state, state, update, ALU.add).then_inc(a["state_new"], 1)
                        dve.wait_ge(a["state_new"], g + 1)
                link(nc.vector.tensor_reduce(ys[:, 2 * g:2 * g + 2], update, X_AXIS, ALU.add))
                link(nc.vector.tensor_tensor(ys[:, 2 * g:2 * g + 2], ys[:, 2 * g:2 * g + 2], skip_s, ALU.add))

            conv(0)
            for g in range(G):
                if g % 2:
                    gate_values(g // 2)
                if g + 1 < G:
                    conv(g + 1)
                ssd(g)
                sample(g)
                if g % 2:
                    j = g // 2
                    link(nc.vector.scalar_tensor_tensor(y[:, :, 512 * j:512 * j + 512], z, 0.5,
                                                        y[:, :, 512 * j:512 * j + 512], ALU.mult, ALU.mult))
            link(nc.vector.scalar_tensor_tensor(ys, zs, 0.5, ys, ALU.mult, ALU.mult))

        @block.tensor
        def _(pe):
            pe.wait_ge(a["small_in"], 16)
            for k4 in range(4):
                for k in range(8):
                    nc.tensor.matmul(bank[5][:, 32 * k4:32 * k4 + 32], m.hT[:, k, P * k4:P * k4 + P],
                                     w_dt[:, 32 * k:32 * k + 32], start=(k == 0), stop=(k == 7))
            for k in range(8):
                last = nc.tensor.matmul(bank[6][0:32, 0:8], w_dt[:, 32 * k:32 * k + 32], m.hT[:, k, SEQ:T_ALL],
                                        start=(k == 0), stop=(k == 7))
            last.then_inc(a["dt_ready"], 1)

            def project(key):
                i = place[key]
                b = B_SSD + i
                w = m.slot[b % 2]
                pe.wait_ge(s[f"ring_in{b % 2}"], 16 * (b // 2 + 1))
                if i:
                    pe.wait_ge(a["small_free"], i)
                for t in range(4):
                    unit = 4 * i + t
                    if unit >= 2:
                        pe.wait_ge(a[f"proj_free{unit % 2}"], unit // 2)
                    for k in range(8):
                        cols = w[:, 512 * k + P * t:512 * k + P * t + P]
                        if key[0] == "x":
                            last = nc.tensor.matmul(bank[unit % 2][:, :], cols, m.hT[:, k, 0:SEQ], start=(k == 0),
                                                    stop=(k == 7))
                        else:
                            last = nc.tensor.matmul(bank[unit % 2][:, :], m.hT[:, k, P * t:P * t + P],
                                                    w[:, 512 * k:512 * k + 512], start=(k == 0), stop=(k == 7))
                        small = nc.tensor.matmul(bank[2][:, 8 * t:8 * t + 8], cols, m.hT[:, k, SEQ:T_ALL],
                                                 start=(k == 0), stop=(k == 7))
                    small.then_inc(a["proj_ready"], 1)
                pe.wait_ge(a["proj_ready"], 4 * i + 4)
                pe.sem_inc(a["small_ready"], 1)

            pe.wait_ge(a["dt_done"], 1)
            nc.tensor.matmul(bank[4][:, 0:128], m.c(C_TRI), dta, start=True, stop=True)
            nc.tensor.matmul(bank[4][:, 128:256], m.c(C_ONES), dta, start=True, stop=True).then_inc(a["sums_ready"], 1)
            pe.wait_ge(a["dt_b"], 4)
            for pair in range(16):
                last = nc.tensor.matmul(bank[6][:, 17 * pair:17 * pair + 17], m.c(C_EXPAND + P * pair, P, 32), s_cols,
                                        start=True, stop=True)
            last.then_inc(a["expand_ready"], 1)
            pe.wait_ge(a["sums_kept"], 1)
            pe.wait_ge(a["expand_kept"], 1)
            project(("x", 0))

            def own_turn(key):
                i = turn_at[key]
                if i:
                    pe.wait_ge(a["turn_free"], i)

            def weigh(g, k):
                i = NCK * g + k
                x = xc[g % 2]
                if i:
                    pe.wait_ge(a["cb_free"], i)
                nc.tensor.matmul(bank[5][:, 0:128], x[:, 2, P * k:P * k + P], x[:, 3, P * k:P * k + P], start=True,
                                 stop=True).then_inc(a["cb_ready"], 1)
                if i:
                    pe.wait_ge(a["diff_ready"], i)
                for e in range(4):
                    h = 32 * k + 4 * g + e
                    last = nc.tensor.matmul(bank[4][:, P * e:P * e + P], dta[:, h:h + 1].to_broadcast([P, P]),
                                            m.c(C_TRI), start=True, stop=True)
                last.then_inc(a["acs_ready"], 1)

            def spread(g, q):
                i = 4 * g + q
                if i:
                    pe.wait_ge(a["bc_free"], i)
                for b in range(4):
                    at_b = SEQ + 4 * (q % 2) + b
                    last = nc.tensor.matmul(bank[7][:, P * b:P * b + P],
                                            xc[g % 2][:, 2 + q // 2, at_b:at_b + 1].to_broadcast([P, P]),
                                            m.c(C_IDENT), start=True, stop=True)
                last.then_inc(a["bc_ready"], 1)

            for g in range(G):
                if g % 2:
                    project(("z", g // 2))
                if g + 1 < G:
                    project(("x", g + 1))
                x = xc[g % 2]
                pe.wait_ge(a["xc_ready"], g + 1)
                for k in range(NCK):
                    own_turn(("rows", g, k))
                    for j in range(3):
                        last = nc.tensor.transpose(bank[3][:, P * j:P * j + P], x[:, j, P * k:P * k + P], m.c(C_IDENT))
                    last.then_inc(a["turn_ready"], 1)
                weigh(g, 0)
                for k in range(NCK):
                    i = NCK * g + k
                    if k + 1 < NCK:
                        weigh(g, k + 1)
                    if k == 0:
                        pe.wait_ge(a["xdt_ready"], g + 1)
                    pe.wait_ge(a["mix_ready"], i + 1)
                    if i:
                        pe.wait_ge(a["y_free"], i)
                    if k:
                        pe.wait_ge(a["h_ready"], i)
                        nc.tensor.matmul(bank[6][:, 256:512], x[:, 3, P * k:P * k + P], hT[(k - 1) % 2], start=True,
                                         stop=True)
                    for e in range(4):
                        last = nc.tensor.matmul(bank[6][:, 64 * e:64 * e + 64], decay[i % 2][:, e], xdt[:, k, e],
                                                start=True, stop=True)
                    last.then_inc(a["y_ready"], 1)
                    own_turn(("state", g, k))
                    nc.tensor.matmul(bank[3][:, 0:256], rows[g % 2][:, k, 256:384], xdt_end[:, k], start=True,
                                     stop=True).then_inc(a["turn_ready"], 1)
                own_turn(("last", g, 0))
                for half in range(2):
                    last = nc.tensor.transpose(bank[3][:, P * half:P * half + P], hT[1][:, P * half:P * half + P],
                                               m.c(C_IDENT))
                last.then_inc(a["turn_ready"], 1)
                for q in range(4):
                    spread(g, q)


def merge_branches(sh):
    nc, ins, m, bank, s = sh.nc, sh.ins, sh.m, sh.bank, sh.s
    x = sh.x = m.at(0, 5120).rearrange("p (n d) -> p n d", n=N_T)
    gates = m.at(5120, 8320).rearrange("p (c t) -> p c t", t=T_ALL)
    yT = m.at(13440, 8320).rearrange("p (c t) -> p c t", t=T_ALL)
    squares = m.at(13440, 8192).rearrange("p (k c) -> p k c", k=4)
    merged = m.at(21760, 4160).rearrange("p (c t) -> p c t", t=T_ALL)
    y, ys = sh.y, sh.ys
    parts = [m.at(26216 + 512 * i, 512) for i in range(2)]
    stat = m.at(25920, 32)
    part_s = m.at(25952, 128)
    n_units = [4] * 4 + [8] + [2] * 4 + [5] * 2
    upto = [sum(n_units[:i + 1]) for i in range(len(n_units))]
    first = [u - n for u, n in zip(upto, n_units)]

    with ExitStack() as c:
        names = ("x_in", "squares", "inverse", "roots", "scaled", "turned", "turn_free", "s_square", "s_sum",
                 "s_inverse", "s_scaled", "proj_ready", "proj_free0", "proj_free1", "small_free", "gates", "merged",
                 "done")
        a = stage_semaphores(nc, c, "d_", names)
        block = c.enter_context(nc.Block())

        @block.sync
        def _(sp):
            sp.dma_start(x[:, 0:4, :], ins["x_prompt"].rearrange("(n p) d -> p n d", p=P)).then_inc(a["x_in"], 16)
            sp.dma_start(x[0:N_S, 4, :], ins["x_sample"]).then_inc(a["x_in"], 16)
            for i in range(2, 13):
                b = B_GATE + i
                sp.wait_ge(a["proj_ready"], upto[i - 2])
                sp.dma_start(m.slot[b % 2], ins["stream"][b]).then_inc(s[f"ring_in{b % 2}"], 16)

        @block.scalar
        def _(act):
            for k in range(4):
                nc.scalar.activation(squares[:, k], y[:, k], ACT.Square, accum_out=stat[:, k:k + 1]).then_inc(a["squares"], 1)
            act.wait_ge(a["inverse"], 1)
            nc.scalar.activation(stat[:, 8:12], stat[:, 4:8], ACT.Sqrt).then_inc(a["roots"], 1)
            act.wait_ge(a["s_inverse"], 1)
            nc.scalar.activation(stat[:, 24:32], stat[:, 16:24], ACT.Sqrt).then_inc(a["roots"], 1)
            for i in range(4):
                for t in range(4):
                    unit = first[i] + t
                    act.wait_ge(a["proj_ready"], unit + 1)
                    nc.scalar.activation(gates[:, 4 * i + t, 0:SEQ], bank[unit % 2][:, :], ACT.Tanh,
                                         scale=0.5).then_inc(a[f"proj_free{unit % 2}"], 1)
                nc.scalar.activation(gates[:, 4 * i:4 * i + 4, SEQ:T_ALL],
                                     bank[2][:, 0:32].rearrange("p (c b) -> p c b", c=4), ACT.Tanh,
                                     scale=0.5).then_inc(a["small_free"], 1)
            act.wait_ge(a["small_free"], 4)
            act.sem_inc(a["gates"], 1)

        @block.vector
        def _(dve):
            link = lambda i: sh.dve(dve, i)
            dve.wait_ge(a["squares"], 4)
            link(nc.vector.tensor_scalar(stat[:, 0:4], stat[:, 0:4], 1.0 / D_INNER, EPS, ALU.mult, ALU.add))
            nc.vector.reciprocal(stat[:, 4:8], stat[:, 0:4]).then_inc(a["inverse"], 1)
            nc.vector.tensor_tensor(part_s, ys.rearrange("p c b -> p (c b)"), ys.rearrange("p c b -> p (c b)"),
                                    ALU.mult).then_inc(a["s_square"], 1)
            dve.wait_ge(a["s_sum"], 1)
            link(nc.vector.tensor_reduce(stat[:, 16:24], bank[7][:, 0:128].rearrange("p (c b) -> p b c", c=16), X_AXIS,
                                         ALU.add))
            link(nc.vector.tensor_scalar(stat[:, 16:24], stat[:, 16:24], 1.0 / D_INNER, EPS, ALU.mult, ALU.add))
            nc.vector.reciprocal(stat[:, 16:24], stat[:, 16:24]).then_inc(a["s_inverse"], 1)
            dve.wait_ge(a["roots"], 1)
            for k in range(4):
                nc.vector.tensor_scalar(y[:, k], y[:, k], stat[:, 8 + k:9 + k], None, ALU.mult).then_inc(a["scaled"], 1)
            dve.wait_ge(a["roots"], 2)
            link(nc.vector.tensor_tensor(ys, ys, stat[:, 24:32].unsqueeze(1).to_broadcast([P, 16, 8]), ALU.mult))
            nc.vector.tensor_tensor(yT[:, :, SEQ:T_ALL], ys, m.norm_ssd.unsqueeze(2).to_broadcast([P, 16, 8]),
                                    ALU.mult).then_inc(a["s_scaled"], 1)
            for k in range(4):
                for q in range(4):
                    i = 4 * k + q
                    dve.wait_ge(a["turned"], i + 1)
                    nc.vector.tensor_tensor(yT[:, 4 * q:4 * q + 4, P * k:P * k + P],
                                            bank[5 + i % 2][:, :].rearrange("p (c t) -> p c t", c=4),
                                            m.norm_ssd[:, 4 * q:4 * q + 4].unsqueeze(2).to_broadcast([P, 4, P]),
                                            ALU.mult).then_inc(a["turn_free"], 1)
            dve.wait_ge(a["turn_free"], 16)
            dve.wait_ge(a["gates"], 1)
            for t in range(8):
                unit = first[4] + t
                dve.wait_ge(a["proj_ready"], unit + 1)
                nc.vector.scalar_tensor_tensor(merged[:, t, 0:SEQ], gates[:, t, 0:SEQ], 1.0, bank[unit % 2][:, :],
                                               ALU.add, ALU.mult).then_inc(a[f"proj_free{unit % 2}"], 1)
            nc.vector.scalar_tensor_tensor(merged[:, :, SEQ:T_ALL], gates[:, 0:8, SEQ:T_ALL], 1.0,
                                           bank[2][:, 0:64].rearrange("p (c b) -> p c b", c=8),
                                           ALU.add, ALU.mult).then_inc(a["small_free"], 1)
            dve.wait_ge(a["small_free"], 5)
            for j in range(4):
                for t in range(2):
                    unit = first[5 + j] + t
                    row = 2 * j + t
                    part = parts[t]
                    dve.wait_ge(a["proj_ready"], unit + 1)
                    nc.vector.scalar_tensor_tensor(part, gates[:, 8 + row, 0:SEQ], 1.0, bank[unit % 2][:, :],
                                                   ALU.add, ALU.mult).then_inc(a[f"proj_free{unit % 2}"], 1)
                    dve.wait_ge(a[f"proj_free{unit % 2}"], unit // 2 + 1)
                    nc.vector.tensor_tensor(merged[:, row, 0:SEQ], merged[:, row, 0:SEQ], part, ALU.add)
                small = part_s[:, 0:16].rearrange("p (c b) -> p c b", c=2)
                nc.vector.scalar_tensor_tensor(small, gates[:, 8 + 2 * j:10 + 2 * j, SEQ:T_ALL], 1.0,
                                               bank[2][:, 0:16].rearrange("p (c b) -> p c b", c=2),
                                               ALU.add, ALU.mult).then_inc(a["small_free"], 1)
                dve.wait_ge(a["small_free"], 6 + j)
                nc.vector.tensor_tensor(merged[:, 2 * j:2 * j + 2, SEQ:T_ALL], merged[:, 2 * j:2 * j + 2, SEQ:T_ALL],
                                        small, ALU.add).then_inc(a["merged"], 1)
                dve.wait_ge(a["merged"], j + 1)
            for j in range(2):
                for t in range(5):
                    unit = first[9 + j] + t
                    r = rows_of(t)
                    dve.wait_ge(a["proj_ready"], unit + 1)
                    xs = x[0:r, t, 512 * j:512 * j + 512]
                    if unit == first[9]:
                        dve.wait_ge(a["x_in"], 32)
                    nc.vector.scalar_tensor_tensor(xs, bank[unit % 2][0:r, :], 0.5, xs, ALU.mult,
                                                   ALU.add).then_inc(a[f"proj_free{unit % 2}"], 1)
            dve.wait_ge(a["proj_free0"], upto[-1] // 2)

        @block.tensor
        def _(pe):
            def unit_free(unit):
                if unit >= 2:
                    pe.wait_ge(a[f"proj_free{unit % 2}"], unit // 2)

            def columns(i, n_k, width, src):
                b = B_GATE + i
                w = m.slot[b % 2]
                pe.wait_ge(s[f"ring_in{b % 2}"], 16 * (b // 2 + 1))
                if i:
                    pe.wait_ge(a["small_free"], i)
                for t in range(n_units[i]):
                    unit = first[i] + t
                    unit_free(unit)
                    for k in range(n_k):
                        cols = w[:, width * k + P * t:width * k + P * t + P]
                        nc.tensor.matmul(bank[unit % 2][:, :], cols, src[:, k, 0:SEQ], start=(k == 0),
                                         stop=(k == n_k - 1))
                        last = nc.tensor.matmul(bank[2][:, 8 * t:8 * t + 8], cols, src[:, k, SEQ:T_ALL],
                                                start=(k == 0), stop=(k == n_k - 1))
                    last.then_inc(a["proj_ready"], 1)

            pe.wait_ge(a["s_square"], 1)
            nc.tensor.matmul(bank[7][:, 0:128], m.c(C_ONES), part_s, start=True, stop=True).then_inc(a["s_sum"], 1)
            for i in range(4):
                columns(i, 8, 512, m.hT)
            for k in range(4):
                pe.wait_ge(a["scaled"], k + 1)
                for q in range(4):
                    i = 4 * k + q
                    if i >= 2:
                        pe.wait_ge(a["turn_free"], i - 1)
                    for j in range(4):
                        at = P * (4 * q + j)
                        last = nc.tensor.transpose(bank[5 + i % 2][:, P * j:P * j + P], y[:, k, at:at + P],
                                                   m.c(C_IDENT))
                    last.then_inc(a["turned"], 1)
            columns(4, 4, 1024, m.attT)
            pe.wait_ge(a["turn_free"], 16)
            pe.wait_ge(a["s_scaled"], 1)
            for i in range(5, 9):
                columns(i, 16, 256, yT)
            pe.wait_ge(a["merged"], 4)
            for i in range(9, 11):
                b = B_GATE + i
                pe.wait_ge(s[f"ring_in{b % 2}"], 16 * (b // 2 + 1))
                for t in range(5):
                    unit = first[i] + t
                    r = rows_of(t)
                    unit_free(unit)
                    for k in range(8):
                        last = nc.tensor.matmul(bank[unit % 2][0:r, :], merged[:, k, P * t:P * t + r],
                                                m.slot[b % 2][:, 512 * k:512 * k + 512], start=(k == 0), stop=(k == 7))
                    last.then_inc(a["proj_ready"], 1)


class LoopChain:

    def __init__(self, sem, turn, length, passed, start=0):
        self.sem, self.turn, self.length, self.start, self.count = sem, turn, length, start, 0
        self.passed = passed

    def __call__(self, eng, ins):
        self.count += 1
        ins.then_inc(self.sem, 1)
        eng.wait_ge(self.sem, self.turn * self.length + (self.start + self.count))
        eng.sem_inc(self.passed, 1)

    def close(self):
        assert self.count == self.length


U_BUFS, V_BUFS = 8, 4


def peer_and_ple(sh):
    nc, ins, outs, m, bank, s = sh.nc, sh.ins, sh.outs, sh.m, sh.bank, sh.s
    x = sh.x
    hx = m.at(5120, 5120).rearrange("p (n d) -> p n d", n=N_T)
    query = m.at(10240, 8320).rearrange("p (c t) -> p c t", t=T_ALL)
    scores_of = lambda n: query[:, :, P * n:P * n + rows_of(n)]
    keys = m.at(18560, 2048).rearrange("p (c k) -> p c k", c=16)
    ple_x = m.at(20608, 1024).rearrange("p (k t) -> p k t", k=8)
    diag = [m.at(21632 + P * i, P) for i in range(V_BUFS)]
    stage = m.at(22144, 512).rearrange("p (a w k) -> p a w k", a=2, w=2)
    p_cols = m.at(22656, 1040).rearrange("p (k t) -> p k t", k=2)
    w_proj = m.at(23696, 2048).rearrange("p (k n) -> p k n", k=2)
    row_tmp = m.at(25744, 1024)
    index_f = m.at(26768, 128)
    index = [m.at(26896 + 128 * i, 128).bitcast(U32) for i in range(2)]
    gate = [m.at(27152 + 128 * i, 128) for i in range(2)]
    top_at = 27408
    val = m.at(top_at, 32).rearrange("p (w k) -> p w k", w=2)
    pos = m.at(top_at + 32, 32).bitcast(U32).rearrange("p (w k) -> p w k", w=2)
    best = m.at(top_at + 64, 16)
    best_at = m.at(top_at + 80, 16).bitcast(U32)
    all_pos = m.at(top_at + 96, 256).rearrange("p (h w k) -> p h w k", h=8, w=2)
    all_best = m.at(top_at + 352, 128).rearrange("p (h k) -> p h k", h=8)
    all_at = m.at(top_at + 480, 128).bitcast(U32)
    digit_u = m.at(top_at + 608, 128).bitcast(U32)
    digit = m.at(top_at + 736, 128)
    picked = [m.at(top_at + 864 + 128 * i, 128) for i in range(2)]
    stat = m.at(top_at + 1120, 64)
    now_index = [m.at(at, 16).bitcast(U32) for at in (top_at + 1184, 33360)]
    dots = m.at(top_at + 1200, 16)
    acts = m.at(top_at + 1216, 16)
    coef = m.at(top_at + 1232, 16)
    index_s = m.at(top_at + 1248, 8).bitcast(U32)
    gate_s = m.at(top_at + 1256, 8)
    assert top_at + 1264 <= 28672
    cand = m.at(28672, 256).rearrange("p (a b) -> p a b", a=16)
    cand_rest = m.at(28928, 256)
    v_buf = [m.at(29184 + 1024 * i, 1024) for i in range(V_BUFS)]
    coef_s = m.at(33280, 64, P).rearrange("p (b c) -> p b c", b=8)
    dots_s = m.at(33344, 16).rearrange("p (b w) -> p b w", b=8)
    u_buf = [m.slot[i // 4][:, 1024 * (i % 4):1024 * (i % 4) + 1024] for i in range(U_BUFS)]
    w_gate_low = [m.at(18560, 2048), m.mem[:, 4360:6408]]
    w_gate_high = [scores_of(n) for n in range(2)]

    def w_gate(k, j):
        if j == 0:
            return w_gate_low[k // 4][:, 512 * (k % 4):512 * (k % 4) + 512]
        return w_gate_high[k // 4][:, 4 * (k % 4):4 * (k % 4) + 4]
    one_hot = m.mem[:, 6408:8456].rearrange("p (h k a) -> p h k a", h=8, k=16)
    norm_rows = m.mem[:, 8520:10568].rearrange("p (w d) -> p w d", w=2)
    sample_scores = m.c(C_EXPAND, 2048, N_S).rearrange("p (c k) -> p c k", c=16)
    ident = m.c(C_IDENT)
    acc = [(bank[0], bank[1]), (bank[2], bank[7])]
    TOP_LINKS = 14
    n_banks = 4
    score_banks = ((3, 4, 5, 6), (0, 1, 2, 7))

    with ExitStack() as c:
        names = ["small_in", "rows_in", "squares", "inverse", "roots", "scaled", "turned", "columns", "proj_ready",
                 "proj_free0", "proj_free1", "small_free", "score_ready", "score_kept", "query_read", "top_step",
                 "top_done", "gate_max", "gate_exp", "index_ready", "dot_done", "dots_ready", "acts_ready",
                 "coef_ready", "diag_ready", "v_used", "stage_step", "acc_open", "acc_done", "acc_kept",
                 "ple_square", "ple_inverse", "ple_root", "ple_scaled", "ple_turned", "ple_columns", "ple_gate",
                 "ple_gated", "ple_proj", "ple_used", "end_square", "end_inverse", "end_root", "end_rows",
                 "stored", "w_gate_in", "s_turned", "s_kept", "s_wide", "s_read", "gathered_s", "top_passed", "gather_passed"]
        a = stage_semaphores(nc, c, "e_", names)
        u_in = list(stage_semaphores(nc, c, "e_u_in", [str(i) for i in range(U_BUFS)]).values())
        v_in = list(stage_semaphores(nc, c, "e_v_in", [str(i) for i in range(V_BUFS)]).values())
        block = c.enter_context(nc.Block())

        @block.sync
        def _(sp):
            sp.dma_start(norm_rows.rearrange("p w d -> p (w d)"),
                         ins["norm_rows"].rearrange("w d -> (w d)").partition_broadcast(P)).then_inc(a["rows_in"], 16)
            sp.dma_start(keys.rearrange("p c k -> p (c k)"), ins["keys"]).then_inc(a["small_in"], 16)
            sp.dma_start(p_cols.rearrange("p k t -> p (k t)"), ins["p_cols"]).then_inc(a["small_in"], 16)
            sp.dma_start(w_proj.rearrange("p k n -> p (k n)"), ins["w_ple_proj"]).then_inc(a["small_in"], 16)
            for i in (2, 3):
                b = B_PQ + i
                sp.wait_ge(a["proj_ready"], 4 * (i - 1))
                sp.dma_start(m.slot[b % 2], ins["stream"][b]).then_inc(s[f"ring_in{b % 2}"], 16)
            sp.wait_ge(a["score_ready"], 4 * N_T)
            for i in range(2):
                sp.dma_start(w_gate_low[i], ins["stream"][B_PLE][:, 2048 * i:2048 * i + 2048]).then_inc(
                    a["w_gate_in"], 16)
            sp.wait_ge(a["top_done"], 2)
            for i in range(2):
                src = ins["stream"][B_PLE + 1][:, 2048 * i:2048 * i + 2048].rearrange("p (c k) -> p c k", c=16)
                sp.dma_start(w_gate_high[i], src).then_inc(a["w_gate_in"], 16)
            for n in range(N_T):
                sp.wait_ge(a["end_rows"], n + 1)
                if n == 4:
                    sp.dma_start(outs["y_sample"], x[0:N_S, 4]).then_inc(a["stored"], 16)
                else:
                    sp.dma_start(outs["y_prompt"][P * n:P * n + P], x[:, n]).then_inc(a["stored"], 16)
            sp.wait_ge(a["stored"], 16 * N_T)

        @block.gpsimd
        def _(pool):
            pool.wait_ge(a["proj_ready"], 16)

            def gather(table, idx, buf, arrived):
                nc.gpsimd.indirect_dma_start(buf, None, ins[table], bass.IndirectOffsetOnAxis(idx, 0)).then_inc(
                    arrived, 16)

            for n in range(4):
                pool.wait_ge(a["index_ready"], n + 1)
                with pool.Fori(0, 4) as two:
                    for odd in range(2):
                        pool.wait_ge(a["v_used"], two * 32 + (128 * n + 16 * odd + 1))
                        now = now_index[odd]
                        nc.gpsimd.tensor_copy(now, index[n % 2][:, bass.ds(two * 32 + 16 * odd, 16)]).then_inc(
                            a["stage_step"], 1)
                        pool.wait_ge(a["stage_step"], two * 2 + (8 * n + odd + 1))
                        for k in range(TOPK):
                            pool.wait_ge(a["dot_done"], two * 32 + (128 * n + 16 * odd + k + 1))
                            pool.sem_inc(a["gather_passed"], 1)
                            gather("peer_u", now[:, k:k + 1], u_buf[k % U_BUFS], u_in[k % U_BUFS])
                        for k in range(TOPK):
                            pool.wait_ge(a["v_used"], two * 32 + (128 * n + 16 * odd + k + 1))
                            pool.sem_inc(a["gather_passed"], 1)
                            gather("peer_v", now[:, k:k + 1], v_buf[k % V_BUFS], v_in[k % V_BUFS])
            pool.wait_ge(a["gather_passed"], 4 * 8 * 2 * TOPK)
            pool.wait_ge(a["s_kept"], 2)
            for table, buf, arrived, used in (("peer_u", u_buf, u_in, "dot_done"), ("peer_v", v_buf, v_in, "v_used")):
                for b in range(N_S):
                    pool.wait_ge(a[used], 512 + b + 1)
                    gather(table, index_s[:, b:b + 1], buf[b % len(buf)], arrived[b % len(buf)])

        @block.scalar
        def _(act):
            for n in range(N_T):
                r = rows_of(n)
                if n == 0:
                    act.wait_ge(a["squares"], 1)
                nc.scalar.activation(hx[0:r, n], x[0:r, n], ACT.Square, accum_out=stat[0:r, n:n + 1]).then_inc(
                    a["squares"], 1)
            act.wait_ge(a["inverse"], 1)
            nc.scalar.activation(stat[:, 16:21], stat[:, 8:13], ACT.Sqrt).then_inc(a["roots"], 1)
            for n in range(N_T):
                r = rows_of(n)
                for half in range(2):
                    act.wait_ge(a["turned"], 2 * n + half + 1)
                    nc.scalar.copy(m.hT[:, 4 * half:4 * half + 4, P * n:P * n + r],
                                   bank[5 + half][:, :].rearrange("p (c t) -> p c t", c=4)[:, :, 0:r]).then_inc(
                        a["columns"], 1)
            for i in range(4):
                for t in range(4):
                    unit = 4 * i + t
                    act.wait_ge(a["proj_ready"], unit + 1)
                    nc.scalar.copy(query[:, unit, 0:SEQ], bank[unit % 2][:, :]).then_inc(a[f"proj_free{unit % 2}"], 1)
                nc.scalar.copy(query[:, 4 * i:4 * i + 4, SEQ:T_ALL],
                               bank[2][:, 0:32].rearrange("p (c b) -> p c b", c=4)).then_inc(a["small_free"], 1)

            for n in range(N_T):
                r = rows_of(n)
                for q in range(n_banks):
                    act.wait_ge(a["score_ready"], 4 * n + 4)
                    src = bank[score_banks[n % 2][q]][0:r, :].rearrange("p (c k) -> p c k", c=4)
                    dst = query[0:r, 4 * q:4 * q + 4, P * n:P * n + P] if n < 4 else \
                        sample_scores[:, 4 * q:4 * q + 4]
                    nc.scalar.copy(dst, src).then_inc(a["score_kept"], 1)

            def gate_exp(n):
                r = rows_of(n)
                act.wait_ge(a["gate_max"], n + 1)
                nc.scalar.activation(gate[n % 2][0:r], gate[n % 2][0:r], ACT.Exp).then_inc(a["gate_exp"], 1)

            def ple(n):
                r = rows_of(n)
                act.wait_ge(a["acc_kept"], n + 1)
                nc.scalar.activation(row_tmp[0:r], x[0:r, n], ACT.Square, accum_out=stat[0:r, 24:25]).then_inc(
                    a["ple_square"], 1)
                act.wait_ge(a["ple_inverse"], n + 1)
                nc.scalar.activation(stat[0:r, 26:27], stat[0:r, 25:26], ACT.Sqrt).then_inc(a["ple_root"], 1)
                for j in range(2):
                    act.wait_ge(a["ple_gate"], 2 * n + j + 1)
                    nc.scalar.activation(row_tmp[0:r, 512 * j:512 * j + 512], bank[5 + j][0:r, :], ACT.Tanh,
                                         scale=0.5).then_inc(a["ple_gated"], 1)
                act.wait_ge(a["ple_used"], 2 * n + 2)
                nc.scalar.activation(row_tmp[0:r], x[0:r, n], ACT.Square, accum_out=stat[0:r, 28:29]).then_inc(
                    a["end_square"], 1)
                act.wait_ge(a["end_inverse"], n + 1)
                nc.scalar.activation(stat[0:r, 30:31], stat[0:r, 29:30], ACT.Sqrt).then_inc(a["end_root"], 1)

            gate_exp(0)
            for n in range(4):
                with act.Fori(0, 8) as hd:
                    act.wait_ge(a["dots_ready"], hd + (8 * n + 1))
                    nc.scalar.activation(acts, dots, ACT.Gelu_apprx_tanh).then_inc(a["acts_ready"], 1)
                    act.wait_ge(a["coef_ready"], hd + (8 * n + 1))
                    for k in range(TOPK):
                        act.wait_ge(a["v_used"], hd * 16 + (128 * n + k + 1))
                        nc.scalar.mul(diag[k % V_BUFS], ident, coef[:, k:k + 1]).then_inc(a["diag_ready"], 1)
                gate_exp(n + 1)
                ple(n)
            act.wait_ge(a["s_turned"], 1)
            nc.scalar.copy(gate_s, bank[3][:, 8:16]).then_inc(a["s_kept"], 1)
            act.wait_ge(a["dots_ready"], 33)
            nc.scalar.activation(acts[:, 0:8], dots[:, 0:8], ACT.Gelu_apprx_tanh).then_inc(a["acts_ready"], 1)
            ple(4)

        @block.vector
        def _(dve):
            link = lambda i: sh.dve(dve, i)
            link(nc.vector.memset(stat, 1.0))
            dve.sem_inc(a["squares"], 1)
            dve.sem_inc(a["dot_done"], U_BUFS)
            dve.sem_inc(a["v_used"], V_BUFS)
            dve.sem_inc(a["acts_ready"], 1)
            dve.sem_inc(a["diag_ready"], 1)
            nc.vector.memset(coef_s, 0.0)
            dve.wait_ge(a["squares"], 1 + N_T)
            link(nc.vector.tensor_scalar(stat[:, 0:5], stat[:, 0:5], 1.0 / D_MODEL, EPS, ALU.mult, ALU.add))
            nc.vector.reciprocal(stat[:, 8:13], stat[:, 0:5]).then_inc(a["inverse"], 1)
            dve.wait_ge(a["roots"], 1)
            dve.wait_ge(a["rows_in"], 16)
            for n in range(N_T):
                r = rows_of(n)
                nc.vector.scalar_tensor_tensor(hx[0:r, n], x[0:r, n], stat[0:r, 16 + n:17 + n], norm_rows[0:r, 0],
                                               ALU.mult, ALU.mult).then_inc(a["scaled"], 1)

            def top(n, hd, chain):
                r = rows_of(n)
                link = lambda i: chain(dve, i)
                src = sample_scores if n == 4 else query[:, :, P * n:P * n + P]
                link(nc.vector.tensor_copy(stage[0:r, 0], src[0:r, bass.ds(hd * 2, 2)]))
                for lo in (0, 8):
                    src = stage[0:r, 0 if lo == 0 else 1]
                    for w in range(2):
                        last = nc.vector.max(val[0:r, w, lo:lo + 8], src[:, w])
                    link(last)
                    for w in range(2):
                        last = nc.vector.max_index(pos[0:r, w, lo:lo + 8], val[0:r, w, lo:lo + 8], src[:, w])
                    if lo == 0:
                        for w in range(2):
                            last = nc.vector.match_replace(stage[0:r, 1, w], val[0:r, w, 0:8], src[:, w], NEG)
                    link(last)
                link(nc.vector.tensor_tensor(cand[0:r], val[0:r, 0].unsqueeze(2).to_broadcast([r, 16, 16]),
                                             val[0:r, 1].unsqueeze(1).to_broadcast([r, 16, 16]), ALU.add))
                flat = cand[0:r].rearrange("p a b -> p (a b)")
                link(nc.vector.max(best[0:r, 0:8], flat))
                nc.vector.max_index(best_at[0:r, 0:8], best[0:r, 0:8], flat)
                link(nc.vector.match_replace(cand_rest[0:r], best[0:r, 0:8], flat, NEG))
                link(nc.vector.max(best[0:r, 8:16], cand_rest[0:r]))
                link(nc.vector.max_index(best_at[0:r, 8:16], best[0:r, 8:16], cand_rest[0:r]))
                nc.vector.tensor_copy(all_pos[0:r, bass.ds(hd, 1)].rearrange("p h w k -> p (h w k)"),
                                      pos[0:r].rearrange("p w k -> p (w k)"))
                nc.vector.tensor_copy(all_best[0:r, bass.ds(hd, 1)].rearrange("p h k -> p (h k)"), best[0:r])
                link(nc.vector.tensor_copy(all_at[0:r, bass.ds(hd * 16, 16)], best_at[0:r]))

            N_LINKS = 11

            def decode(n):
                r = rows_of(n)
                dve.sem_inc(a["top_done"], 1)
                if n >= 2:
                    dve.wait_ge(a["coef_ready"], 8 * (n - 1))
                    dve.wait_ge(a["stage_step"], 8 * (n - 1))
                g = gate[n % 2][0:r].rearrange("p (h k) -> p h k", h=8)
                nc.vector.tensor_tensor(g, all_best[0:r], all_best[0:r, :, 0:1].to_broadcast([r, 8, 16]),
                                        ALU.subtract).then_inc(a["gate_max"], 1)
                for w in range(2):
                    if w == 0:
                        link(nc.vector.tensor_scalar(digit_u[0:r], all_at[0:r], 4, None, ALU.logical_shift_right))
                    else:
                        link(nc.vector.tensor_scalar(digit_u[0:r], all_at[0:r], 15, None, ALU.bitwise_and))
                    link(nc.vector.tensor_copy(digit[0:r], digit_u[0:r]))
                    hot = one_hot[0:r].rearrange("p h k a -> p (h k) a")
                    link(nc.vector.tensor_tensor(hot, digit[0:r].unsqueeze(2).to_broadcast([r, 128, 16]),
                                                 m.c(C_IOTA, 16, r).unsqueeze(1).to_broadcast([r, 128, 16]),
                                                 ALU.is_equal))
                    link(nc.vector.tensor_tensor(one_hot[0:r], one_hot[0:r],
                                                 all_pos[0:r, :, w].unsqueeze(2).to_broadcast([r, 8, 16, 16]), ALU.mult))
                    link(nc.vector.tensor_reduce(picked[w][0:r], hot, X_AXIS, ALU.add))
                link(nc.vector.scalar_tensor_tensor(index_f[0:r], picked[0][0:r], float(N_KEYS), picked[1][0:r],
                                                    ALU.mult, ALU.add))
                dve.wait_ge(a["gate_exp"], n + 1)
                link(nc.vector.tensor_reduce(stat[0:r, 32:40], g, X_AXIS, ALU.add))
                link(nc.vector.reciprocal(stat[0:r, 32:40], stat[0:r, 32:40]))
                link(nc.vector.tensor_tensor(g, g, stat[0:r, 32:40].unsqueeze(2).to_broadcast([r, 8, 16]), ALU.mult))
                nc.vector.tensor_copy(index[n % 2][0:r], index_f[0:r]).then_inc(a["index_ready"], 1)
                dve.wait_ge(a["index_ready"], n + 1)

            def ple(n):
                r = rows_of(n)
                xs = x[0:r, n]
                dve.wait_ge(a["acc_done"], n + 1)
                for j in range(2):
                    last = nc.vector.tensor_copy(xs[:, 512 * j:512 * j + 512], acc[n % 2][j][0:r, :])
                last.then_inc(a["acc_kept"], 1)
                dve.wait_ge(a["ple_square"], n + 1)
                link(nc.vector.tensor_scalar(stat[0:r, 24:25], stat[0:r, 24:25], 1.0 / D_MODEL, EPS, ALU.mult, ALU.add))
                nc.vector.reciprocal(stat[0:r, 25:26], stat[0:r, 24:25]).then_inc(a["ple_inverse"], 1)
                dve.wait_ge(a["ple_root"], n + 1)
                nc.vector.tensor_scalar(row_tmp[0:r], xs, stat[0:r, 26:27], None, ALU.mult).then_inc(a["ple_scaled"], 1)
                for half in range(2):
                    dve.wait_ge(a["ple_turned"], 2 * n + half + 1)
                    nc.vector.tensor_tensor(ple_x[:, 4 * half:4 * half + 4, 0:r],
                                            bank[3 + half][:, :].rearrange("p (c t) -> p c t", c=4)[:, :, 0:r],
                                            m.norm_ple[:, 4 * half:4 * half + 4].unsqueeze(2).to_broadcast([P, 4, r]),
                                            ALU.mult).then_inc(a["ple_columns"], 1)
                for j in range(2):
                    dve.wait_ge(a["ple_gated"], 2 * n + j + 1)
                    dve.wait_ge(a["ple_proj"], 2 * n + j + 1)
                    t = row_tmp[0:r, 512 * j:512 * j + 512]
                    link(nc.vector.scalar_tensor_tensor(t, t, 1.0, bank[3 + j][0:r, :], ALU.add, ALU.mult))
                    xj = xs[:, 512 * j:512 * j + 512]
                    nc.vector.scalar_tensor_tensor(xj, t, 0.5, xj, ALU.mult, ALU.add).then_inc(a["ple_used"], 1)
                dve.wait_ge(a["end_square"], n + 1)
                link(nc.vector.tensor_scalar(stat[0:r, 28:29], stat[0:r, 28:29], 1.0 / D_MODEL, EPS, ALU.mult, ALU.add))
                nc.vector.reciprocal(stat[0:r, 29:30], stat[0:r, 28:29]).then_inc(a["end_inverse"], 1)
                dve.wait_ge(a["end_root"], n + 1)
                nc.vector.scalar_tensor_tensor(xs, xs, stat[0:r, 30:31], norm_rows[0:r, 1], ALU.mult,
                                               ALU.mult).then_inc(a["end_rows"], 1)

            dve.wait_ge(a["score_kept"], 4 * N_T)
            with dve.Fori(0, 8) as hd:
                chain = LoopChain(a["top_step"], hd, N_LINKS, a["top_passed"])
                top(0, hd, chain)
                chain.close()
            decode(0)
            for n in range(4):
                with dve.Fori(0, 8) as hd:
                    dve.wait_ge(a["acts_ready"], hd + (8 * n + 1))
                    for k in range(TOPK):
                        use = 16 * (16 * n + k // U_BUFS + 1)
                        dve.wait_ge(u_in[k % U_BUFS], hd * 32 + use)
                        u = u_buf[k % U_BUFS]
                        ins_ = nc.vector.tensor_tensor_reduce(u, u, hx[:, n], 1.0, 0.0, ALU.mult, ALU.add,
                                                              dots[:, k:k + 1])
                        ins_.then_inc(a["dot_done"], 1)
                    dve.wait_ge(a["dot_done"], hd * 16 + (128 * n + 16 + U_BUFS))
                    dve.sem_inc(a["dots_ready"], 1)
                    chain = LoopChain(a["top_step"], hd, N_LINKS, a["top_passed"], 8 * N_LINKS * (n + 1))
                    top(n + 1, hd, chain)
                    chain.close()
                    dve.wait_ge(a["acts_ready"], hd + (8 * n + 2))
                    dve.wait_ge(a["diag_ready"], hd * 16 + (128 * n + 1))
                    nc.vector.tensor_tensor(coef, acts, gate[n % 2][:, bass.ds(hd * 16, 16)], ALU.mult).then_inc(
                        a["coef_ready"], 1)
                decode(n + 1)
                ple(n)
            dve.wait_ge(a["top_passed"], 40 * N_LINKS)
            dve.wait_ge(a["s_turned"], 1)
            nc.vector.tensor_copy(index_s, bank[4][:, 0:8]).then_inc(a["s_kept"], 1)
            for b in range(N_S):
                dve.wait_ge(a["s_wide"], b + 1)
                dve.wait_ge(u_in[b], 16 * (64 + 1))
                for j in range(2):
                    u = u_buf[b][:, 512 * j:512 * j + 512]
                    last = nc.vector.tensor_tensor_reduce(u, u, bank[5 + j][:, :], 1.0, 0.0, ALU.mult, ALU.add,
                                                          dots_s[:, b, j:j + 1])
                last.then_inc(a["s_read"], 1)
            dve.wait_ge(a["s_read"], N_S)
            nc.vector.tensor_tensor(dots[:, 0:8], dots_s[:, :, 0], dots_s[:, :, 1], ALU.add).then_inc(
                a["dots_ready"], 1)
            dve.wait_ge(a["acts_ready"], 34)
            dve.wait_ge(a["s_kept"], 2)
            nc.vector.tensor_tensor(coef_s.rearrange("p b c -> p (b c)")[:, 0:64:9], acts[:, 0:8], gate_s,
                                    ALU.mult).then_inc(a["coef_ready"], 1)
            ple(4)

        @block.tensor
        def _(pe):
            for n in range(N_T):
                r = rows_of(n)
                pe.wait_ge(a["scaled"], n + 1)
                for half in range(2):
                    if n:
                        pe.wait_ge(a["columns"], 2 * n + half - 1)
                    for j in range(4):
                        at = P * (4 * half + j)
                        last = nc.tensor.transpose(bank[5 + half][:, P * j:P * j + r], hx[0:r, n, at:at + P],
                                                   ident[0:r, 0:r])
                    last.then_inc(a["turned"], 1)
            pe.wait_ge(a["columns"], 2 * N_T)
            for i in range(4):
                b = B_PQ + i
                w = m.slot[b % 2]
                pe.wait_ge(s[f"ring_in{b % 2}"], 16 * (b // 2 + 1))
                if i:
                    pe.wait_ge(a["small_free"], i)
                for t in range(4):
                    unit = 4 * i + t
                    if unit >= 2:
                        pe.wait_ge(a[f"proj_free{unit % 2}"], unit // 2)
                    for k in range(8):
                        cols = w[:, 512 * k + P * t:512 * k + P * t + P]
                        nc.tensor.matmul(bank[unit % 2][:, :], cols, m.hT[:, k, 0:SEQ], start=(k == 0), stop=(k == 7))
                        last = nc.tensor.matmul(bank[2][:, 8 * t:8 * t + 8], cols, m.hT[:, k, SEQ:T_ALL],
                                                start=(k == 0), stop=(k == 7))
                    last.then_inc(a["proj_ready"], 1)
            pe.wait_ge(a["small_free"], 4)
            pe.wait_ge(a["proj_free0"], 8)
            pe.wait_ge(a["proj_free1"], 8)
            pe.wait_ge(a["small_in"], 48)

            for n in range(N_T):
                r = rows_of(n)
                for q in range(n_banks):
                    if n >= 2:
                        pe.wait_ge(a["score_kept"], 4 * (n - 2) + q + 1)
                    for j in range(4):
                        cc = 4 * q + j
                        last = nc.tensor.matmul(bank[score_banks[n % 2][q]][0:r, P * j:P * j + P],
                                                query[:, cc, P * n:P * n + r], keys[:, cc], start=True, stop=True)
                    last.then_inc(a["score_ready"], 1)
            pe.wait_ge(a["score_kept"], 4 * N_T)

            def open_acc(n):
                r = rows_of(n)
                if n >= 2:
                    pe.wait_ge(a["acc_kept"], n - 1)
                for j in range(2):
                    nc.tensor.matmul(acc[n % 2][j][0:r, :], ident[0:r, 0:r], x[0:r, n, 512 * j:512 * j + 512],
                                     start=True, stop=False, skip_group_check=True)

            def ple(n):
                r = rows_of(n)
                if n == 0:
                    pe.wait_ge(a["w_gate_in"], 64)
                pe.wait_ge(a["ple_scaled"], n + 1)
                if n == 4:
                    pe.wait_ge(a["s_kept"], 2)
                    pe.wait_ge(a["s_read"], N_S)
                for half in range(2):
                    for j in range(4):
                        at = P * (4 * half + j)
                        last = nc.tensor.transpose(bank[3 + half][:, P * j:P * j + r], row_tmp[0:r, at:at + P],
                                                   ident[0:r, 0:r])
                    last.then_inc(a["ple_turned"], 1)
                pe.wait_ge(a["ple_columns"], 2 * n + 2)
                for j in range(2):
                    for k in range(8):
                        last = nc.tensor.matmul(bank[5 + j][0:r, :], ple_x[:, k, 0:r], w_gate(k, j), start=(k == 0),
                                                stop=(k == 7))
                    last.then_inc(a["ple_gate"], 1)
                for j in range(2):
                    for k in range(2):
                        last = nc.tensor.matmul(bank[3 + j][0:r, :], p_cols[:, k, P * n:P * n + r],
                                                w_proj[:, k, 512 * j:512 * j + 512], start=(k == 0), stop=(k == 1))
                    last.then_inc(a["ple_proj"], 1)

            for n in range(4):
                open_acc(n)
                with pe.Fori(0, 8) as hd:
                    for k in range(TOPK):
                        use = 16 * (32 * n + k // V_BUFS + 1)
                        pe.wait_ge(v_in[k % V_BUFS], hd * 64 + use)
                        pe.wait_ge(a["diag_ready"], hd * 16 + (128 * n + k + 2))
                        for j in range(2):
                            last = nc.tensor.matmul(acc[n % 2][j][:, :], diag[k % V_BUFS],
                                                    v_buf[k % V_BUFS][:, 512 * j:512 * j + 512], start=False,
                                                    stop=False, skip_group_check=True)
                        last.then_inc(a["v_used"], 1)
                pe.wait_ge(a["v_used"], 128 * (n + 1) + V_BUFS)
                pe.sem_inc(a["acc_done"], 1)
                if n:
                    pe.wait_ge(a["ple_used"], 2 * n)
                ple(n)
            pe.wait_ge(a["ple_used"], 8)
            pe.wait_ge(a["index_ready"], N_T)
            nc.tensor.transpose(bank[4][:, 0:8], index_f[0:8], ident[0:8, 0:8])
            nc.tensor.transpose(bank[3][:, 8:16], gate[0][0:8], ident[0:8, 0:8]).then_inc(a["s_turned"], 1)
            open_acc(4)
            for b in range(N_S):
                if b:
                    pe.wait_ge(a["s_read"], b)
                for j in range(2):
                    last = nc.tensor.matmul(bank[5 + j][:, :], m.c(C_SEL + P * b, P, 8), hx[0:8, 4, 512 * j:512 * j + 512],
                                            start=True, stop=True)
                last.then_inc(a["s_wide"], 1)
            pe.wait_ge(a["coef_ready"], 33)
            for b in range(N_S):
                pe.wait_ge(v_in[b % V_BUFS], 16 * (128 + b // V_BUFS + 1))
                for j in range(2):
                    last = nc.tensor.matmul(acc[0][j][0:8, :], coef_s[:, b], v_buf[b % V_BUFS][:, 512 * j:512 * j + 512],
                                            start=False, stop=False, skip_group_check=True)
                last.then_inc(a["v_used"], 1)
            pe.wait_ge(a["v_used"], 512 + N_S + V_BUFS)
            pe.sem_inc(a["acc_done"], 1)
            ple(4)


def kernel(**inputs):
    import numpy as np
    import concourse.bacc as bacc
    from concourse import mybir as _mybir
    from concourse.bass_utils import run_bass_kernel_spmd as run

    a = {k: np.asarray(v) for k, v in inputs.items()}

    def chunks(w):
        return np.ascontiguousarray(w.reshape(w.shape[0] // P, P, w.shape[1]).transpose(1, 0, 2))

    def column(v):
        return np.ascontiguousarray(v.reshape(-1, P).T)

    w_in = chunks(a["w_in"][0])
    q0, k0, v0 = 0, Q_COLS, 2 * Q_COLS
    z0 = 3 * Q_COLS
    x0 = z0 + D_INNER
    b0 = x0 + D_INNER
    c0 = b0 + SSD_GROUPS * D_STATE
    dt0 = x0 + CONV_CH
    gate0 = dt0 + SSD_HEADS
    blocks = []
    for g in range(3):
        for base in (q0, k0, v0):
            blocks.append(w_in[:, :, base + g * ATT_W:base + (g + 1) * ATT_W])
    for g in range(SSD_GROUPS):
        blocks.append(np.concatenate([w_in[:, :, x0 + 256 * g:x0 + 256 * (g + 1)],
                                      w_in[:, :, b0 + 128 * g:b0 + 128 * (g + 1)],
                                      w_in[:, :, c0 + 128 * g:c0 + 128 * (g + 1)]], axis=2))
        if g % 2:
            blocks.append(w_in[:, :, z0 + 512 * (g // 2):z0 + 512 * (g // 2 + 1)])
    for j in range(4):
        blocks.append(w_in[:, :, gate0 + 512 * j:gate0 + 512 * (j + 1)])
    blocks.append(chunks(a["w_att_out"][0]))
    w_ssd = chunks(a["w_ssd_out"][0])
    for j in range(4):
        blocks.append(w_ssd[:, :, 256 * j:256 * (j + 1)])
    w_out = chunks(a["w_out"][0])
    blocks += [w_out[:, :, 512 * j:512 * (j + 1)] for j in range(2)]
    w_pq = chunks(a["w_peer_q"][0])
    blocks += [w_pq[:, :, 512 * j:512 * (j + 1)] for j in range(4)]
    w_pg = chunks(a["w_ple_gate"][0])
    blocks += [w_pg[:, :, 512 * j:512 * (j + 1)] for j in range(2)]
    stream = np.stack([b.reshape(P, 4096) for b in blocks])
    assert stream.shape[0] == N_BLOCKS

    tile_order = [t for g in range(SSD_GROUPS) for t in (2 * g, 2 * g + 1, 16 + g, 24 + g)]
    conv_w = a["conv_w"][0].reshape(CONV_W, 32, P).transpose(2, 1, 0)[:, tile_order]
    conv_b = column(a["conv_b"][0])[:, tile_order]
    state_conv = a["state_conv"][0].reshape(N_S, 3, 32, P).transpose(3, 2, 0, 1)[:, tile_order]
    keys = np.stack([a["peer_keys1"][0], a["peer_keys2"][0]], axis=1)
    keys = keys.transpose(3, 0, 1, 2).reshape(P, 2048)
    p_all = np.concatenate([a["p_prompt"][0, 0], a["p_sample"][0, :, 0]], axis=0)
    cols = np.concatenate([column(a["norm_mix"][0]), column(a["norm_ffn"][0]), column(a["norm_ple"][0]),
                           column(a["ssd_norm"][0]), conv_w.reshape(P, 128), conv_b], axis=1)
    head_rows = np.concatenate([a["dt_bias"][0], a["a_log"][0], a["d_skip"][0]]).reshape(1, 96)
    head_cols = np.stack([a["dt_bias"][0], a["a_log"][0], a["d_skip"][0]], axis=1)
    arrays = {
        "x_prompt": a["x_prompt"][0], "x_sample": a["x_sample"][:, 0],
        "cache0": a["cache_kv_w128"][0].reshape(N_S, -1, 1024),
        "cache1": a["cache_kv_w512"][0].reshape(N_S, -1, 1024),
        "cache2": a["cache_kv_w2048"][0].reshape(N_S, -1, 1024),
        "state_conv": state_conv.reshape(P, 32 * 24),
        "state_ssm": a["state_ssm"][0].reshape(N_S, SSD_HEADS * 64, D_STATE),
        "stream": stream, "w_dt": w_in[:, :, dt0:dt0 + SSD_HEADS].reshape(P, 256),
        "w_ple_proj": chunks(a["w_ple_proj"][0]).reshape(P, 2048),
        "p_cols": chunks(p_all.T).reshape(P, 2 * T_ALL),
        "keys": keys, "cols": cols, "head_rows": head_rows, "head_cols": head_cols,
        "norm_rows": np.stack([a["norm_ffn"][0], a["norm_final"]]),
        "peer_u": a["peer_u"][0], "peer_v": a["peer_v"][0],
        "consts": shape_constants(), "rope_table": rope_table(),
    }
    outs = {
        "y_prompt": (SEQ, D_MODEL), "y_sample": (N_S, D_MODEL),
        "kv0": (128, 1024), "kv1": (SEQ, 1024), "kv2": (SEQ, 1024),
        "conv_prompt": (P, 96), "ssm_prompt": (SSD_HEADS * 64, D_STATE),
        "kvs0": (N_S, 1024), "kvs1": (N_S, 1024), "kvs2": (N_S, 1024),
        "conv_sample": (P, 32 * 24), "ssm_sample": (N_S, SSD_HEADS * 64, D_STATE),
    }
    nc = bacc.Bacc("TRN2", target_bir_lowering=False, num_devices=1)
    arrays = {"in_" + k: np.ascontiguousarray(v) for k, v in arrays.items()}
    ins = {k[3:]: nc.dram_tensor(k, v.shape, _mybir.dt.from_np(v.dtype), kind="ExternalInput").ap()
           for k, v in arrays.items()}
    out_aps = {k: nc.dram_tensor("out_" + k, s, F32, kind="ExternalOutput").ap() for k, s in outs.items()}
    hybrid_decoder_step(nc, ins, out_aps)
    r = run(nc, [arrays], core_ids=[0]).results[0]
    o = {k: r["out_" + k] for k in outs}

    inverse = np.argsort(tile_order)

    def conv_rows(x, n):
        x = x.reshape(P, 32, n, 3)[:, inverse]
        return np.ascontiguousarray(x.transpose(2, 3, 1, 0)).reshape(1, n, 3, CONV_CH)

    kv_shape = (2, 8, 64)
    return (o["y_prompt"].reshape(1, SEQ, D_MODEL), o["y_sample"].reshape(N_S, 1, D_MODEL),
            o["kv0"].reshape(1, 1, 128, *kv_shape), o["kv1"].reshape(1, 1, SEQ, *kv_shape),
            o["kv2"].reshape(1, 1, SEQ, *kv_shape),
            conv_rows(o["conv_prompt"], 1), o["ssm_prompt"].reshape(1, 1, SSD_HEADS, 64, D_STATE),
            o["kvs0"].reshape(1, N_S, 1, *kv_shape), o["kvs1"].reshape(1, N_S, 1, *kv_shape),
            o["kvs2"].reshape(1, N_S, 1, *kv_shape),
            conv_rows(o["conv_sample"], N_S), o["ssm_sample"].reshape(1, N_S, SSD_HEADS, 64, D_STATE))
```

```python
import math
from contextlib import ExitStack

import numpy as np
import concourse.bass as bass
from concourse import mybir

P = 128
D_MODEL, SEQ, N_S, PAST_LEN = 1024, 512, 8, 1024
T_ALL = SEQ + N_S
N_T = 5
ATT_W, Q_COLS = 512, 1536
D_INNER, SSD_HEADS, SSD_GROUPS, D_STATE, CONV_W = 2048, 32, 8, 128, 4
CONV_CH = D_INNER + 2 * SSD_GROUPS * D_STATE
N_KEYS, TOPK = 128, 16
EPS = 1e-6
SCALE = 0.125
NEG = -1.0e30
F32 = mybir.dt.float32
U32 = mybir.dt.uint32
ALU = mybir.AluOpType
ACT = mybir.ActivationFunctionType
X_AXIS = mybir.AxisListType.X
XY_AXIS = mybir.AxisListType.XY

B_QKV = 0
B_SSD = 9
B_GATE = 21
B_ATT = 25
B_YOUT = 26
B_OUT = 30
B_PQ = 32
B_PLE = 36
N_BLOCKS = 38

C_IDENT, C_TRI, C_ONES, C_CAUSAL, C_PREV, C_RES, C_EXPAND = 0, 128, 256, 384, 512, 640, 768
C_SEL, C_DELTA, C_IND, C_IOTA, N_CONST = 2816, 3840, 3904, 3912, 3928


def shape_constants():
    c = np.zeros((P, N_CONST), np.float32)
    row, col = np.arange(P)[:, None], np.arange(P)[None, :]
    c[:, C_IDENT:C_IDENT + P] = row == col
    c[:, C_TRI:C_TRI + P] = row <= col
    c[:, C_ONES:C_ONES + P] = 1.0
    c[:, C_CAUSAL:C_CAUSAL + P] = np.where(col <= row, 0.0, NEG)
    c[:, C_PREV:C_PREV + P] = np.where(col >= row, 0.0, NEG)
    c[:, C_RES:C_RES + P] = np.where((col <= row) & (col % 4 == row % 4), 0.0, NEG)
    for pair in range(16):
        c[:32, C_EXPAND + P * pair:C_EXPAND + P * (pair + 1)] = np.arange(32)[:, None] == 2 * pair + col // 64
    c[:8, C_SEL:C_SEL + 1024] = np.arange(8)[:, None] == np.arange(1024)[None, :] // P
    c[:8, C_DELTA:C_DELTA + 64] = np.arange(8)[:, None] == np.arange(64)[None, :] // 8
    c[:64, C_IND:C_IND + 8] = np.arange(64)[:, None] // 8 == np.arange(8)[None, :]
    c[:, C_IOTA:C_IOTA + 16] = np.arange(16)[None, :]
    return c


def tile_positions(g, s):
    i = np.arange(P)
    return P * s + i if g == 0 else 4 * i + s


def rope_table():
    half = 32
    inv = np.exp(np.arange(half, dtype=np.float32) * np.float32(-2.0 * math.log(10000.0) / 64)).astype(np.float32)
    t = np.zeros((P, 13, 128), np.float32)
    for n in range(13):
        pos = tile_positions(n // 4, n % 4) if n < 12 else np.full(P, PAST_LEN)
        ang = (pos.astype(np.float32)[:, None] * inv[None, :]).astype(np.float32)
        cos, sin = np.cos(ang), np.sin(ang)
        t[:, n] = np.concatenate([cos, cos, -sin, sin], axis=1)
    return t.reshape(P, 13 * 128)


def rows_of(n):
    return P if n < 4 else N_S


def stage_semaphores(nc, stack, prefix, names):
    sems = {n: nc.alloc_semaphore(prefix + n) for n in names}

    def release():
        nc.clear_and_free_semaphores(list(sems.values()))
        nc.all_engine_barrier()

    stack.callback(release)
    return sems


class Chain:

    def __init__(self, sem):
        self.sem, self.count = sem, 0

    def __call__(self, eng, ins):
        self.count += 1
        ins.then_inc(self.sem, 1)
        eng.wait_ge(self.sem, self.count)


def hybrid_decoder_step(nc, ins, outs):
    ctx = ExitStack()
    with ctx:
        sem = lambda name: ctx.enter_context(nc.semaphore(name))
        mem = ctx.enter_context(nc.sbuf_tensor("mem", [P, 53200], F32))
        bank = [ctx.enter_context(nc.psum_tensor(f"bank{i}", [P, 512], F32)) for i in range(8)]
        head_out = nc.dram_tensor("head_out", [3, SEQ, 528], F32, kind="Internal").ap()
        m = Memory(mem)
        s = {}
        for name in SEMS:
            s[name] = sem(name)
        shared = Shared(nc, ins, outs, m, bank, s, head_out)
        attention_prompt(shared)
        attention_sample(shared)
        ssd_branch(shared)
        merge_branches(shared)
        peer_and_ple(shared)


SEMS = ["consts_in", "x_in", "ring_in0", "ring_in1", "sync_step", "act_step", "dve_step", "pool_step", "pe_step",
        "proj_ready", "proj_free0", "proj_free1", "proj_free2"]


class Memory:

    def __init__(self, mem):
        self.mem = mem
        self.const = mem[:, 0:N_CONST]
        at = N_CONST
        self.cols = mem[:, at:at + 200]
        self.norm_mix, self.norm_ffn, self.norm_ple = (self.cols[:, 8 * i:8 * i + 8] for i in range(3))
        self.norm_ssd = self.cols[:, 24:40]
        self.conv_w = self.cols[:, 40:168].rearrange("p (c w) -> p c w", w=4)
        self.conv_b = self.cols[:, 168:200]
        at += 200
        self.head_rows = mem[:, at:at + 96]
        self.head_cols = mem[0:32, at + 96:at + 99]
        self.small = mem[:, at + 100:at + 228]
        at += 228
        assert at <= 4360
        self.hT = mem[:, 4360:8520].rearrange("p (c t) -> p c t", t=T_ALL)
        self.attT = mem[:, 8520:10600].rearrange("p (c t) -> p c t", t=T_ALL)
        self.slot = [mem[:, 10600 + 4096 * i:10600 + 4096 * (i + 1)] for i in range(2)]
        self.phase = 18792
        self.end = 53200
        self.q_s = mem[0:8, 48592:50128].rearrange("p (g n) -> p g n", g=3)
        self.kv_s = mem[0:8, 50128:53200].rearrange("p (g n) -> p g n", g=3)

    def at(self, offset, n, parts=P):
        assert self.phase + offset + n <= self.end
        return self.mem[0:parts, self.phase + offset:self.phase + offset + n]

    def c(self, at, n=P, parts=P):
        return self.const[0:parts, at:at + n]


class Shared:
    def __init__(self, nc, ins, outs, m, bank, s, head_out):
        self.nc, self.ins, self.outs, self.m, self.bank, self.s = nc, ins, outs, m, bank, s
        self.head_out = head_out
        self.act = Chain(s["act_step"])
        self.dve = Chain(s["dve_step"])
        self.pool = Chain(s["pool_step"])


def transposed_norm(sh, name, x, xn, tiles, banks, ctx):
    nc, m = sh.nc, sh.m
    squares, inverse, roots, scaled, turned, columns = (
        ctx.enter_context(nc.semaphore(f"{name}_{k}"))
        for k in ("squares", "inverse", "roots", "scaled", "turned", "columns"))
    stat = m.small
    return squares, inverse, roots, scaled, turned, columns, stat


def attention_prompt(sh):
    nc, ins, outs, m, bank, s = sh.nc, sh.ins, sh.outs, sh.m, sh.bank, sh.s
    ident = m.c(C_IDENT)
    x = m.at(0, 5120).rearrange("p (n d) -> p n d", n=N_T)
    xn = m.at(5120, 5120).rearrange("p (n d) -> p n d", n=N_T)
    q_buf = [m.at(2048 * i, 2048).rearrange("p (s n) -> p s n", s=4) for i in range(2)]
    kv_buf = [m.at(4096 + 4096 * i, 4096).rearrange("p (s n) -> p s n", s=4) for i in range(2)]
    qT = m.at(12288, 2048).rearrange("p (c t) -> p c t", c=4)
    kT = m.at(14336, 2048).rearrange("p (c t) -> p c t", c=4)
    score = [m.at(16384 + 1024 * i, 1024).rearrange("p (h w k) -> p h w k", h=4, w=2) for i in range(2)]
    probT = [m.at(18432 + 1024 * i, 1024).rearrange("p (w h q) -> p w h q", w=2, h=4) for i in range(2)]
    head_rows = m.at(20480, 2112).rearrange("p (s h c) -> p s h c", s=4, h=8)
    rope_a, rope_b = m.at(22592, 512), m.at(23104, 512)
    merge_in = [m.at(23616 + 1584 * i, 1584).rearrange("p (g h c) -> p g h c", g=3, h=8) for i in range(2)]
    rope = m.at(26784, 1664).rearrange("p (n c) -> p n c", n=13)
    neg_max = [m.at(28448 + 4 * i, 4) for i in range(2)]
    merge_max = m.at(28456, 8)
    merge_w = m.at(28464, 24).rearrange("p (g h) -> p g h", g=3)
    merge_den = m.at(28488, 24).rearrange("p (g h) -> p g h", g=3)
    merge_sum = m.at(28512, 8)
    stat = m.small

    turns = []
    for g in range(3):
        for t in range(4):
            turns += [("q", g, t), ("k", g, t)]
        for v in range(8):
            turns += [("p", g, v, w) for w in range(2 if g == 0 and v >= 2 else 1)]
    turns += [("att", n) for n in range(4)]
    turn_at = {k: i for i, k in enumerate(turns)}

    def token_columns(k, g, t):
        if t == 4:
            return m.hT[:, k, SEQ:T_ALL]
        if g == 0:
            return m.hT[:, k, P * t:P * t + P]
        return m.hT[:, k, t:SEQ:4]

    with ExitStack() as c:
        names = ("squares", "inverse", "roots", "scaled", "turned", "columns", "qk_rows", "v_rows", "kv_stored0", "kv_stored1", "kv_stored2",
                 "turn_ready", "turn_free", "score_ready", "score_free", "max_ready", "prob_ready", "out_ready",
                 "out_kept", "group_done", "head_stored", "merge_in0", "merge_in1", "merge_exp", "merge_max",
                 "merge_rows")
        a = stage_semaphores(nc, c, "a_", names)
        block = c.enter_context(nc.Block())

        @block.sync
        def _(sp):
            sp.dma_start(x[0:N_S, 4, :], ins["x_sample"]).then_inc(s["x_in"], 16)
            sp.dma_start(x[:, 0:4, :], ins["x_prompt"].rearrange("(n p) d -> p n d", p=P)).then_inc(s["x_in"], 16)
            for b in range(9):
                if b >= 2:
                    sp.wait_ge(s["proj_ready"], 5 * (b - 1))
                sp.dma_start(m.slot[b % 2], ins["stream"][b]).then_inc(s[f"ring_in{b % 2}"], 16)
            for b in (9, 10):
                sp.wait_ge(s["proj_ready"], 5 * (b - 1))
                sp.dma_start(m.slot[b % 2], ins["stream"][b]).then_inc(s[f"ring_in{b % 2}"], 16)

        @block.gpsimd
        def _(pool):
            def store_kv(g):
                pool.wait_ge(a["qk_rows"], 10 * (g + 1))
                pool.wait_ge(a["v_rows"], 5 * (g + 1))
                for t in range(4):
                    src = kv_buf[g % 2][:, t]
                    if g == 0:
                        if t == 3:
                            pool.dma_start(outs["kv0"], src).then_inc(a[f"kv_stored{g}"], 16)
                    else:
                        dst = outs[f"kv{g}"].rearrange("(i r) c -> r i c", r=4)[t]
                        pool.dma_start(dst, src).then_inc(a[f"kv_stored{g}"], 16)
                pool.dma_start(outs[f"kvs{g}"], m.kv_s[:, g]).then_inc(a[f"kv_stored{g}"], 16)

            def store_heads(g):
                for t in range(4):
                    pool.wait_ge(a["out_kept"], 8 * g + 2 * t + 2)
                    src = head_rows[:, t].rearrange("p h c -> p (h c)")
                    if g == 0:
                        pool.dma_start(sh.head_out[0, P * t:P * t + P], src).then_inc(a["head_stored"], 16)
                    else:
                        dst = sh.head_out[g].rearrange("(i r) c -> r i c", r=4)[t]
                        pool.dma_start(dst, src).then_inc(a["head_stored"], 16)

            store_kv(0)
            store_kv(1)
            store_heads(0)
            store_kv(2)
            store_heads(1)
            store_heads(2)
            pool.wait_ge(a["head_stored"], 16 * 12)
            for n in range(4):
                if n >= 2:
                    pool.wait_ge(a["merge_rows"], n - 1)
                src = sh.head_out[:, P * n:P * n + P, :].rearrange("g p c -> p g c")
                dst = merge_in[n % 2].rearrange("p g h c -> p g (h c)")
                pool.dma_start(dst, src).then_inc(a[f"merge_in{n % 2}"], 16)
            for g in range(3):
                pool.wait_ge(a[f"kv_stored{g}"], 16 * (5 if g else 2))

        @block.scalar
        def _(act):
            act.dma_start(m.const, ins["consts"]).then_inc(s["consts_in"], 16)
            act.dma_start(rope.rearrange("p n c -> p (n c)"), ins["rope_table"]).then_inc(s["consts_in"], 16)
            act.dma_start(m.cols, ins["cols"]).then_inc(s["consts_in"], 16)
            act.dma_start(m.head_rows, ins["head_rows"][0].partition_broadcast(P)).then_inc(s["consts_in"], 16)
            act.dma_start(m.head_cols, ins["head_cols"]).then_inc(s["consts_in"], 16)
            act.wait_ge(s["x_in"], 32)
            act.wait_ge(a["squares"], 1)
            for n in range(N_T):
                r = rows_of(n)
                nc.scalar.activation(xn[0:r, n], x[0:r, n], ACT.Square,
                                     accum_out=stat[0:r, n:n + 1]).then_inc(a["squares"], 1)
            act.wait_ge(a["inverse"], 1)
            nc.scalar.activation(stat[:, 16:21], stat[:, 8:13], ACT.Sqrt).then_inc(a["roots"], 1)

            def keep_v(g):
                for t in range(5):
                    unit = 15 * g + 10 + t
                    act.wait_ge(s["proj_ready"], unit + 1)
                    if g == 2 and t == 0:
                        act.wait_ge(a["group_done"], 1)
                        act.wait_ge(a["kv_stored0"], 32)
                    dst = m.kv_s[:, g, 512:1024] if t == 4 else kv_buf[g % 2][:, t, 512:1024]
                    r = rows_of(t)
                    nc.scalar.copy(dst, bank[unit % 3][0:r, :]).then_inc(s[f"proj_free{unit % 3}"], 1)
                    act.wait_ge(s[f"proj_free{unit % 3}"], unit // 3 + 1)
                    act.sem_inc(a["v_rows"], 1)

            def turned(key, dst):
                i = turn_at[key]
                act.wait_ge(a["turn_ready"], i + 1)
                src = bank[5 + i % 2][:, :].rearrange("p (c t) -> p c t", c=4)
                nc.scalar.copy(dst, src).then_inc(a["turn_free"], 1)

            def exps(g, v):
                w = 2 if g == 0 and v >= 2 else 1
                act.wait_ge(a["max_ready"], 8 * g + v + 1)
                for hh in range(4):
                    last = nc.scalar.activation(
                        score[v % 2][:, hh, 0:w], score[v % 2][:, hh, 0:w], ACT.Exp, scale=SCALE,
                        bias=neg_max[v % 2][:, hh:hh + 1],
                        accum_out=head_rows[:, v // 2, 2 * hh + v % 2, 64:65])
                last.then_inc(a["prob_ready"], 1)

            def attend(g):
                for t in range(4):
                    turned(("q", g, t), qT[:, :, P * t:P * t + P])
                    turned(("k", g, t), kT[:, :, P * t:P * t + P])
                if g:
                    act.wait_ge(a["head_stored"], 64 * g)
                exps(g, 0)
                for v in range(8):
                    if 8 * g + v >= 2:
                        act.wait_ge(a["out_ready"], 8 * g + v - 1)
                    for w in range(2 if g == 0 and v >= 2 else 1):
                        turned(("p", g, v, w), probT[v % 2][:, w])
                    if v < 7:
                        exps(g, v + 1)
                    act.wait_ge(a["out_ready"], 8 * g + v + 1)
                    nc.scalar.copy(head_rows[:, v // 2, v % 2:8:2, 0:64],
                                   bank[7][:, 0:256].rearrange("p (h c) -> p h c", h=4)).then_inc(a["out_kept"], 1)

            keep_v(0)
            keep_v(1)
            attend(0)
            keep_v(2)
            attend(1)
            attend(2)
            for n in range(4):
                act.wait_ge(a["merge_max"], n + 1)
                nc.scalar.activation(merge_w, merge_w, ACT.Exp, scale=SCALE).then_inc(a["merge_exp"], 1)
                turned(("att", n), m.attT[:, :, P * n:P * n + P])
            act.wait_ge(a["turn_free"], len(turns))

        @block.vector
        def _(dve):
            link = lambda i: sh.dve(dve, i)
            link(nc.vector.memset(stat[:, :], 1.0))
            dve.sem_inc(a["squares"], 1)
            dve.wait_ge(s["x_in"], 32)
            dve.wait_ge(a["squares"], 1 + N_T)
            link(nc.vector.tensor_scalar(stat[:, 0:5], stat[:, 0:5], 1.0 / D_MODEL, EPS, ALU.mult, ALU.add))
            nc.vector.reciprocal(stat[:, 8:13], stat[:, 0:5]).then_inc(a["inverse"], 1)
            dve.wait_ge(a["roots"], 1)
            for n in range(N_T):
                r = rows_of(n)
                nc.vector.tensor_scalar(xn[0:r, n], x[0:r, n], stat[0:r, 16 + n:17 + n], None,
                                        ALU.mult).then_inc(a["scaled"], 1)
            dve.wait_ge(s["consts_in"], 80)
            for n in range(N_T):
                r = rows_of(n)
                for half in range(2):
                    dve.wait_ge(a["turned"], 2 * n + half + 1)
                    src = bank[5 + half][:, :].rearrange("p (c t) -> p c t", c=4)[:, :, 0:r]
                    g = m.norm_mix[:, 4 * half:4 * half + 4].unsqueeze(2).to_broadcast([P, 4, r])
                    nc.vector.tensor_tensor(m.hT[:, 4 * half:4 * half + 4, P * n:P * n + r], src, g,
                                            ALU.mult).then_inc(a["columns"], 1)

            def rope_rows(g):
                for j in range(2):
                    for t in range(5):
                        unit = 15 * g + 5 * j + t
                        r = rows_of(t)
                        dve.wait_ge(s["proj_ready"], unit + 1)
                        if g == 2 and j == 0 and t == 0:
                            dve.wait_ge(a["group_done"], 1)
                            dve.wait_ge(a["kv_stored0"], 32)
                        tab = rope[0:r, 12 if t == 4 else 4 * g + t]
                        src = bank[unit % 3][0:r, :].rearrange("p (h c) -> p h c", h=8)
                        ra = rope_a[0:r].rearrange("p (h c) -> p h c", h=8)
                        rb = rope_b[0:r].rearrange("p (h c) -> p h c", h=8)
                        cos = tab[:, 0:64].unsqueeze(1).to_broadcast([r, 8, 64])
                        neg_sin = tab[:, 64:96].unsqueeze(1).to_broadcast([r, 8, 32])
                        sin = tab[:, 96:128].unsqueeze(1).to_broadcast([r, 8, 32])
                        nc.vector.tensor_tensor(ra, src, cos, ALU.mult)
                        nc.vector.tensor_tensor(rb[:, :, 0:32], src[:, :, 32:64], neg_sin, ALU.mult)
                        nc.vector.tensor_tensor(rb[:, :, 32:64], src[:, :, 0:32], sin,
                                                ALU.mult).then_inc(s[f"proj_free{unit % 3}"], 1)
                        dve.wait_ge(s[f"proj_free{unit % 3}"], unit // 3 + 1)
                        if t == 4:
                            dst = m.q_s[:, g] if j == 0 else m.kv_s[:, g, 0:512]
                        else:
                            dst = q_buf[g % 2][:, t] if j == 0 else kv_buf[g % 2][:, t, 0:512]
                        nc.vector.tensor_tensor(dst, rope_a[0:r], rope_b[0:r], ALU.add).then_inc(a["qk_rows"], 1)
                        dve.wait_ge(a["qk_rows"], 10 * g + 5 * j + t + 1)

            def maxima(g):
                for v in range(8):
                    w = 2 if g == 0 and v >= 2 else 1
                    dve.wait_ge(a["score_ready"], 8 * g + v + 1)
                    if v >= 2:
                        dve.wait_ge(a["turn_ready"], turn_at[("p", g, v - 2, 1 if g == 0 and v >= 4 else 0)] + 1)
                    elif g:
                        dve.wait_ge(a["turn_ready"], turn_at[("p", g - 1, v + 6, 1 if g == 1 else 0)] + 1)
                    buf = score[v % 2]
                    mask = m.c(C_CAUSAL if g < 2 else C_RES)
                    srcs = [(3, mask), (4, m.c(C_PREV))][:w]
                    for i, (b, mk) in enumerate(srcs):
                        last = nc.vector.tensor_tensor(buf[:, :, i, :], bank[b][:, :].rearrange("p (h k) -> p h k", h=4),
                                                       mk.unsqueeze(1).to_broadcast([P, 4, P]), ALU.add)
                    last.then_inc(a["score_free"], 1)
                    dve.wait_ge(a["score_free"], 8 * g + v + 1)
                    top = head_rows[:, v // 2, v % 2:8:2, 65]
                    if g and v == 0:
                        dve.wait_ge(a["head_stored"], 64 * g)
                    link(nc.vector.tensor_reduce(top, buf[:, :, 0:w, :], XY_AXIS, ALU.max))
                    nc.vector.tensor_scalar(neg_max[v % 2], top, -SCALE, None, ALU.mult).then_inc(a["max_ready"], 1)

            def merge(n):
                dve.wait_ge(a[f"merge_in{n % 2}"], 16 * (n // 2 + 1))
                rows = merge_in[n % 2]
                link(nc.vector.tensor_tensor(merge_max, rows[:, 0, :, 65], rows[:, 1, :, 65], ALU.max))
                link(nc.vector.tensor_tensor(merge_max, merge_max, rows[:, 2, :, 65], ALU.max))
                nc.vector.tensor_tensor(merge_w, rows[:, :, :, 65], merge_max.unsqueeze(1).to_broadcast([P, 3, 8]),
                                        ALU.subtract).then_inc(a["merge_max"], 1)
                dve.wait_ge(a["merge_exp"], n + 1)
                link(nc.vector.tensor_tensor(merge_den, merge_w, rows[:, :, :, 64], ALU.mult))
                link(nc.vector.tensor_reduce(merge_sum, merge_den.rearrange("p g h -> p h g"), X_AXIS, ALU.add))
                link(nc.vector.reciprocal(merge_sum, merge_sum))
                link(nc.vector.tensor_tensor(merge_w, merge_w, merge_sum.unsqueeze(1).to_broadcast([P, 3, 8]), ALU.mult))
                if n:
                    dve.wait_ge(a["turn_ready"], turn_at[("att", n - 1)] + 1)
                for g in range(3):
                    out = (rope_a, rope_b, rope_b)[g].rearrange("p (h c) -> p h c", h=8)
                    link(nc.vector.tensor_tensor(out, rows[:, g, :, 0:64],
                                                 merge_w[:, g].unsqueeze(2).to_broadcast([P, 8, 64]), ALU.mult))
                    if g == 1:
                        link(nc.vector.tensor_tensor(rope_a, rope_a, rope_b, ALU.add))
                nc.vector.tensor_tensor(rope_a, rope_a, rope_b, ALU.add).then_inc(a["merge_rows"], 1)

            rope_rows(0)
            rope_rows(1)
            maxima(0)
            rope_rows(2)
            maxima(1)
            maxima(2)
            for n in range(4):
                merge(n)

        @block.tensor
        def _(pe):
            pe.wait_ge(s["consts_in"], 80)
            for n in range(N_T):
                r = rows_of(n)
                pe.wait_ge(a["scaled"], n + 1)
                for half in range(2):
                    if n:
                        pe.wait_ge(a["columns"], 2 * n + half - 1)
                    for cc in range(4):
                        k = 4 * half + cc
                        last = nc.tensor.transpose(bank[5 + half][:, P * cc:P * cc + r], xn[0:r, n, P * k:P * k + P],
                                                   ident[0:r, 0:r])
                    last.then_inc(a["turned"], 1)
            pe.wait_ge(a["columns"], 2 * N_T)

            def project(g):
                for j in range(3):
                    b = 3 * g + j
                    pe.wait_ge(s[f"ring_in{b % 2}"], 16 * (b // 2 + 1))
                    for t in range(5):
                        unit = 5 * b + t
                        if unit >= 3:
                            pe.wait_ge(s[f"proj_free{unit % 3}"], unit // 3)
                        for k in range(8):
                            last = nc.tensor.matmul(bank[unit % 3][0:rows_of(t), :], token_columns(k, g, t),
                                                    m.slot[b % 2][:, 512 * k:512 * k + 512],
                                                    start=(k == 0), stop=(k == 7))
                        last.then_inc(s["proj_ready"], 1)

            def turn(key, srcs):
                i = turn_at[key]
                if i >= 2:
                    pe.wait_ge(a["turn_free"], i - 1)
                for cc in range(4):
                    last = nc.tensor.transpose(bank[5 + i % 2][:, P * cc:P * cc + P], srcs(cc), ident)
                last.then_inc(a["turn_ready"], 1)

            def scores(g, v):
                t, u = v // 2, v % 2
                if 8 * g + v:
                    pe.wait_ge(a["score_free"], 8 * g + v)
                for w in range(2 if g == 0 and t else 1):
                    for hh in range(4):
                        h = 2 * hh + u
                        lo = 64 * u
                        last = nc.tensor.matmul(bank[3 + w][:, P * hh:P * hh + P],
                                                qT[lo:lo + 64, h // 2, P * t:P * t + P],
                                                kT[lo:lo + 64, h // 2, P * (t - w):P * (t - w) + P],
                                                start=True, stop=True)
                last.then_inc(a["score_ready"], 1)

            def attend(g):
                pe.wait_ge(a["qk_rows"], 10 * g + 10)
                for t in range(4):
                    turn(("q", g, t), lambda cc: q_buf[g % 2][:, t, P * cc:P * cc + P])
                    turn(("k", g, t), lambda cc: kv_buf[g % 2][:, t, P * cc:P * cc + P])
                pe.wait_ge(a["turn_free"], turn_at[("k", g, 3)] + 1)
                pe.wait_ge(a["v_rows"], 5 * g + 5)
                scores(g, 0)
                for v in range(8):
                    t, u = v // 2, v % 2
                    wide = range(2 if g == 0 and t else 1)
                    if v < 7:
                        scores(g, v + 1)
                    pe.wait_ge(a["prob_ready"], 8 * g + v + 1)
                    for w in wide:
                        turn(("p", g, v, w), lambda cc: score[v % 2][:, cc, w, :])
                    pe.wait_ge(a["turn_free"], turn_at[("p", g, v, wide[-1])] + 1)
                    if 8 * g + v:
                        pe.wait_ge(a["out_kept"], 8 * g + v)
                    for hh in range(4):
                        h = 2 * hh + u
                        for w in wide:
                            last = nc.tensor.matmul(bank[7][:, 64 * hh:64 * hh + 64], probT[v % 2][:, w, hh],
                                                    kv_buf[g % 2][:, t - w, 512 + 64 * h:576 + 64 * h],
                                                    start=(w == 0), stop=(w == wide[-1]))
                    last.then_inc(a["out_ready"], 1)
                pe.wait_ge(a["out_ready"], 8 * g + 8)
                pe.sem_inc(a["group_done"], 1)

            project(0)
            project(1)
            attend(0)
            project(2)
            attend(1)
            attend(2)
            for n in range(4):
                pe.wait_ge(a["merge_rows"], n + 1)
                turn(("att", n), lambda cc: rope_a[:, P * cc:P * cc + P])


def attention_sample(sh):
    nc, ins, m, bank, s = sh.nc, sh.ins, sh.m, sh.bank, sh.s
    keys = (128, 128, 64)
    cache = m.at(0, 24576).rearrange("p (g b n) -> p g b n", g=3, b=N_S)
    product = [m.at(24576 + 512 * i, 512) for i in range(2)]
    by_key = m.at(25600, 192).rearrange("p (g r) -> p g r", g=3)
    score_rows = m.at(25792, 323, 64)
    prob_cols = m.at(26120, 192).rearrange("p (g r) -> p g r", g=3)
    new_diag = m.at(26312, 192, 64).rearrange("p (g r) -> p g r", g=3)
    new_cols = m.at(26504, 192, 8).rearrange("p (g r) -> p g r", g=3)
    new_score = m.at(26696, 24, 8).rearrange("p (g h) -> p g h", g=3)
    new_spread = m.at(26720, 192, 8).rearrange("p (g r) -> p g r", g=3)
    row_max, neg_max, row_sum, row_inv = (m.at(26912 + i, 1, 64) for i in range(4))
    new_prod = m.at(26920, 1536, 8).rearrange("p (g n) -> p g n", g=3)
    ident = m.c(C_IDENT)

    with ExitStack() as c:
        names = ("query_ready", "query_free", "key_cols", "new_ready", "rows_ready", "max_ready", "exps", "probs",
                 "cols_ready", "cols_kept", "diag_ready", "new_turned", "out_ready", "out_kept")
        a = stage_semaphores(nc, c, "b_", names)
        cache_in = list(stage_semaphores(nc, c, "b_cache_in", [str(i) for i in range(24)]).values())
        block = c.enter_context(nc.Block())

        def load(eng, b):
            for g in range(3):
                stride = (1, 4, 16)[g]
                eng.dma_start(cache[0:keys[g], g, b], ins[f"cache{g}"][b, 0::stride]).then_inc(
                    cache_in[8 * g + b], 16)

        @block.sync
        def _(sp):
            for b in range(N_S):
                load(sp, b)

        @block.scalar
        def _(act):
            act.wait_ge(a["max_ready"], 1)
            nc.scalar.activation(score_rows, score_rows, ACT.Exp, scale=SCALE, bias=neg_max,
                                 accum_out=row_sum).then_inc(a["exps"], 1)
            act.wait_ge(a["cols_ready"], 1)
            nc.scalar.copy(prob_cols[:, 0:2], bank[3][:, 0:128].rearrange("p (g r) -> p g r", g=2))
            nc.scalar.copy(prob_cols[0:64, 2], bank[3][0:64, 128:192]).then_inc(a["cols_kept"], 1)
            act.wait_ge(a["new_turned"], 1)
            nc.scalar.copy(new_cols, bank[4][0:8, 0:192].rearrange("p (g r) -> p g r", g=3)).then_inc(a["cols_kept"], 1)

        @block.vector
        def _(dve):
            link = lambda i: sh.dve(dve, i)
            link(nc.vector.tensor_tensor(new_prod, m.q_s, m.kv_s[:, :, 0:512], ALU.mult))
            link(nc.vector.tensor_reduce(new_score, new_prod.rearrange("p g (h c) -> p g h c", h=8), X_AXIS, ALU.add))
            for g in range(3):
                last = nc.vector.tensor_tensor(
                    new_spread[:, g].rearrange("p (b h) -> p b h", b=8),
                    m.c(C_DELTA, 64, 8).rearrange("p (b h) -> p b h", b=8),
                    new_score[:, g].unsqueeze(1).to_broadcast([8, 8, 8]), ALU.mult)
            last.then_inc(a["new_ready"], 1)
            i = 0
            for b in range(N_S):
                for g in range(3):
                    dve.wait_ge(cache_in[8 * g + b], 16)
                    dve.wait_ge(a["query_ready"], i + 1)
                    k = keys[g]
                    nc.vector.tensor_tensor(product[i % 2][0:k], cache[0:k, g, b, 0:512], bank[i % 2][0:k, :],
                                            ALU.mult).then_inc(a["query_free"], 1)
                    dve.wait_ge(a["query_free"], i + 1)
                    nc.vector.tensor_reduce(by_key[0:k, g, 8 * b:8 * b + 8],
                                            product[i % 2][0:k].rearrange("p (h c) -> p h c", h=8), X_AXIS,
                                            ALU.add).then_inc(a["key_cols"], 1)
                    i += 1
            dve.wait_ge(a["rows_ready"], 1)
            nc.vector.tensor_copy(score_rows[:, 0:320], bank[2][0:64, 0:320])
            link(nc.vector.tensor_copy(score_rows[:, 320:323], bank[2][0:64, 320:323]))
            link(nc.vector.tensor_reduce(row_max, score_rows, X_AXIS, ALU.max))
            nc.vector.tensor_scalar(neg_max, row_max, -SCALE, None, ALU.mult).then_inc(a["max_ready"], 1)
            dve.wait_ge(a["exps"], 1)
            link(nc.vector.reciprocal(row_inv, row_sum))
            nc.vector.tensor_scalar(score_rows, score_rows, row_inv, None, ALU.mult).then_inc(a["probs"], 1)
            dve.wait_ge(a["probs"], 1)
            for g in range(3):
                last = nc.vector.tensor_scalar(new_diag[:, g], m.c(C_IDENT, 64, 64), score_rows[:, 320 + g:321 + g],
                                               None, ALU.mult)
            last.then_inc(a["diag_ready"], 1)
            dve.wait_ge(a["out_ready"], 1)
            out = bank[5][:, 0:64].rearrange("p (b c w) -> p w c b", b=8, w=2)
            nc.vector.tensor_copy(m.attT[0:64, :, SEQ:T_ALL], out[0:64, 0])
            link(nc.vector.tensor_copy(m.attT[64:128, :, SEQ:T_ALL], out[64:128, 1]))

        @block.tensor
        def _(pe):
            i = 0
            for b in range(N_S):
                for g in range(3):
                    if i >= 2:
                        pe.wait_ge(a["query_free"], i - 1)
                    nc.tensor.matmul(bank[i % 2][:, :], m.c(C_SEL + P * b, P, 8), m.q_s[:, g],
                                     start=True, stop=True).then_inc(a["query_ready"], 1)
                    i += 1
            pe.wait_ge(a["key_cols"], 24)
            pe.wait_ge(a["new_ready"], 1)
            for g in range(3):
                k = keys[g]
                nc.tensor.transpose(bank[2][0:64, P * g:P * g + k], by_key[0:k, g], ident[0:k, 0:k])
            for g in range(3):
                last = nc.tensor.matmul(bank[2][0:64, 320 + g:321 + g], new_spread[:, g], m.c(C_ONES, 1, 8),
                                        start=True, stop=True)
            last.then_inc(a["rows_ready"], 1)
            pe.wait_ge(a["probs"], 1)
            for g in range(3):
                k = keys[g]
                last = nc.tensor.transpose(bank[3][0:k, 64 * g:64 * g + 64], score_rows[:, P * g:P * g + k],
                                           ident[0:64, 0:64])
            last.then_inc(a["cols_ready"], 1)
            pe.wait_ge(a["diag_ready"], 1)
            nc.tensor.matmul(bank[4][0:8, 0:192], m.c(C_IND, 8, 64), new_diag, start=True,
                             stop=True).then_inc(a["new_turned"], 1)
            pe.wait_ge(a["cols_kept"], 2)
            for b in range(N_S):
                for pair in range(4):
                    at = 8 * b + 2 * pair
                    dst = bank[5][:, at:at + 2]
                    for g in range(3):
                        k = keys[g]
                        nc.tensor.matmul(dst, cache[0:k, g, b, 512 + P * pair:640 + P * pair],
                                         prob_cols[0:k, g, at:at + 2], start=(g == 0), stop=False)
                    for g in range(3):
                        last = nc.tensor.matmul(dst, m.kv_s[:, g, 512 + P * pair:640 + P * pair],
                                                new_cols[:, g, at:at + 2], start=False, stop=(g == 2))
            last.then_inc(a["out_ready"], 1)


def ssd_branch(sh):
    nc, ins, outs, m, bank, s = sh.nc, sh.ins, sh.outs, sh.m, sh.bank, sh.s
    NCK, G = 4, SSD_GROUPS
    xpad = [m.at(2060 * i, 2060).rearrange("p (c t) -> p c t", c=4) for i in range(2)]
    xc = [m.at(4120 + 2080 * i, 2080).rearrange("p (c t) -> p c t", c=4) for i in range(2)]
    tanh = m.at(8280, 2080).rearrange("p (c t) -> p c t", c=4)
    update = m.at(8280, 2048).rearrange("p (c b n) -> p c b n", c=2, b=8)
    z_tanh = m.at(10360, 512)
    rows = [m.at(10872 + 1536 * i, 1536).rearrange("p (k c) -> p k c", k=4) for i in range(2)]
    xdt = m.at(13944, 1024).rearrange("p (k e c) -> p k e c", k=4, e=4)
    xdt_end = m.at(14968, 1024).rearrange("p (k e c) -> p k e c", k=4, e=4)
    y = sh.y = m.at(26216, 8192).rearrange("p (k c) -> p k c", k=4)
    z = m.at(15992, 2048).rearrange("p (k c) -> p k c", k=4)
    decay = [m.at(18040 + 512 * i, 512).rearrange("p (e t) -> p e t", e=4) for i in range(2)]
    cb = [m.at(19064 + 128 * i, 128) for i in range(2)]
    hT = [m.at(19320 + 256 * i, 256) for i in range(2)]
    off = m.at(19832, 256)
    at = 20088
    per_head = [m.at(at + 128 * i, 128) for i in range(6)]
    dt, dta, acs, to_end, from_start, chunk_decay = per_head
    by_head = lambda t: t.rearrange("p (k h) -> p k h", k=4)
    at += 768
    state = m.at(at, 2048).rearrange("p (c b n) -> p c b n", c=2, b=8)
    at += 2048
    conv_state = m.at(at, 768).rearrange("p (c b w) -> p c b w", c=32, b=8)
    at += 768
    conv_tail = m.at(at, 96).rearrange("p (c w) -> p c w", c=32)
    at += 96
    s_cols = m.at(at, 17, 32)
    at += 20
    s_head = m.at(at, 272).rearrange("p (c j) -> p c j", c=16)
    at += 272
    ys = sh.ys = m.small[:, 0:128].rearrange("p (c b) -> p c b", c=16)
    zs = m.at(at, 128).rearrange("p (c b) -> p c b", c=16)
    at += 128
    zs_tanh = m.at(at, 32).rearrange("p (c b) -> p c b", c=4)
    at += 32
    h_out = m.at(at, 256).rearrange("p (c n) -> p c n", c=2)
    at += 256
    window = m.at(at, 128).rearrange("p (c b w) -> p c b w", c=4, b=8)
    at += 128
    window_w = m.at(at, 128).rearrange("p (c b w) -> p c b w", c=4, b=8)
    at += 128
    half_w = m.at(at, 128).rearrange("p (c w) -> p c w", c=32)
    at += 128
    half_b = m.at(at, 32)
    at += 32
    w_dt = m.at(at, 256)
    at += 256
    soft_a, soft_b, soft_c = (m.at(at + 136 * i, 136) for i in range(3))
    at += 408
    exp_a = m.at(at, 33)
    at += 36
    xdt_s = m.at(at, 16).rearrange("p (c b) -> p c b", c=2)
    at += 16
    skip_s = m.at(at, 16).rearrange("p (c b) -> p c b", c=2)
    at += 16
    assert at <= 26216

    of_step = [([("z", g // 2)] if g % 2 else []) + ([("x", g + 2)] if g + 2 < G else []) for g in range(G)]
    seq = [("x", 0), ("x", 1)] + [key for keys in of_step for key in keys]
    place = {k: i for i, k in enumerate(seq)}

    points = ("rows", "chunk0", "chunk1", "chunk2", "chunk3", "end0", "end1", "end2")

    def unit_at(g, point):
        units = [(key, t) for key in of_step[g] for t in range(4)]
        i = points.index(point) - (0 if len(units) == 8 else 1)
        return units[i] if 0 <= i < len(units) else None

    turns = [(w, g, k) for g in range(G) for w, n in (("rows", 4), ("state", 4), ("last", 1)) for k in range(n)]
    turn_at = {k: i for i, k in enumerate(turns)}

    with ExitStack() as c:
        names = ("proj_ready", "proj_free0", "proj_free1", "small_ready", "small_free", "small_in", "dt_ready",
                 "dt_a", "dt_b", "dt_c", "dt_done", "sums_ready", "sums_kept", "expand_ready", "expand_kept",
                 "pad_ready", "conv_ready", "tanh_ready", "xc_ready", "z_tanh", "z_ready", "turn_ready",
                 "turn_free", "xdt_ready", "acs_ready", "acs_free", "cb_ready", "cb_free", "diff_ready",
                 "exp_ready", "mix_ready", "y_ready", "y_free", "skip_ready", "h_ready", "bc_ready", "bc_free",
                 "state_in", "state_decayed", "state_new", "state_out", "h_stored", "conv_in", "conv_rows",
                 "window_ready", "window_used", "pads", "conv_stored", "y_gated", "wide_free")
        a = stage_semaphores(nc, c, "c_", names)
        block = c.enter_context(nc.Block())

        @block.sync
        def _(sp):
            sp.dma_start(w_dt, ins["w_dt"]).then_inc(a["small_in"], 16)
            sp.dma_start(conv_state.rearrange("p c b w -> p (c b w)"), ins["state_conv"]).then_inc(a["conv_in"], 16)
            loaded = 2
            for g in range(G):
                upto = 4 + sum(len(of_step[i]) for i in range(g + 1))
                if g:
                    sp.wait_ge(a["state_out"], 32 * g)
                    sp.wait_ge(a["bc_free"], 4 * g)
                for half in range(2):
                    r = 256 * g + P * half
                    sp.dma_start(state[:, half], ins["state_ssm"][:, r:r + P].rearrange("b p n -> p b n")).then_inc(
                        a["state_in"], 16)
                while loaded < upto:
                    sp.wait_ge(a["proj_ready"], 4 * (loaded - 1))
                    b = B_SSD + loaded
                    sp.dma_start(m.slot[b % 2], ins["stream"][b]).then_inc(s[f"ring_in{b % 2}"], 16)
                    loaded += 1
                sp.wait_ge(a["turn_free"], turn_at[("last", g, 0)] + 1)
                sp.dma_start(outs["ssm_prompt"][256 * g:256 * g + 256].rearrange("(c p) n -> p c n", p=P),
                             h_out).then_inc(a["h_stored"], 16)
                sp.wait_ge(a["state_new"], g + 1)
                for half in range(2):
                    r = 256 * g + P * half
                    sp.dma_start(outs["ssm_sample"][:, r:r + P].rearrange("b p n -> p b n"),
                                 state[:, half]).then_inc(a["state_out"], 16)
            sp.wait_ge(a["conv_rows"], 2 * G)
            sp.dma_start(outs["conv_prompt"], conv_tail.rearrange("p c w -> p (c w)")).then_inc(a["conv_stored"], 16)
            sp.dma_start(outs["conv_sample"], conv_state.rearrange("p c b w -> p (c b w)")).then_inc(
                a["conv_stored"], 16)
            sp.wait_ge(a["conv_stored"], 32)
            sp.wait_ge(a["state_out"], 32 * G)
            sp.wait_ge(a["h_stored"], 16 * G)

        @block.gpsimd
        def _(pool):
            for i in range(2):
                nc.gpsimd.memset(xpad[i][:, :, 0:3], 0.0).then_inc(a["pads"], 1)

            def tails(g):
                pool.wait_ge(a["pad_ready"], 4 * g + 4)
                nc.gpsimd.tensor_copy(conv_tail[:, 4 * g:4 * g + 4], xpad[g % 2][:, :, 512:515]).then_inc(
                    a["conv_rows"], 1)
                pool.wait_ge(a["window_ready"], g + 1)
                nc.gpsimd.tensor_copy(conv_state[:, 4 * g:4 * g + 4], window[:, :, :, 1:4]).then_inc(a["conv_rows"], 1)

            def mix(g, k):
                i = NCK * g + k
                pool.wait_ge(a["exp_ready"], i + 1)
                pool.wait_ge(a["cb_free"], i + 1)
                nc.gpsimd.tensor_tensor(decay[i % 2], decay[i % 2], cb[i % 2].unsqueeze(1).to_broadcast([P, 4, P]),
                                        ALU.mult).then_inc(a["mix_ready"], 1)

            tails(0)
            tails(1)
            for g in range(G):
                mix(g, 0)
                pool.wait_ge(a["turn_free"], turn_at[("rows", g, 3)] + 1)
                x_rows = rows[g % 2][:, :, 0:256].rearrange("p k (e c) -> p k e c", e=4)
                for k in range(NCK):
                    last = nc.gpsimd.tensor_tensor(
                        y[:, k, 256 * g:256 * g + 256].rearrange("p (e c) -> p e c", e=4), x_rows[:, k],
                        m.head_rows[:, 64 + 4 * g:68 + 4 * g].unsqueeze(2).to_broadcast([P, 4, 64]), ALU.mult)
                last.then_inc(a["skip_ready"], 1)
                mix(g, 1)
                pool.wait_ge(a["state_in"], 32 * (g + 1))
                if g == 0:
                    pool.wait_ge(a["expand_kept"], 1)
                for half in range(2):
                    last = nc.gpsimd.tensor_tensor(
                        state[:, half], state[:, half],
                        s_head[:, 2 * g + half, 8:16].unsqueeze(2).to_broadcast([P, 8, P]), ALU.mult)
                last.then_inc(a["state_decayed"], 1)
                mix(g, 2)
                mix(g, 3)
                if g + 2 < G:
                    tails(g + 2)

        @block.scalar
        def _(act):
            act.wait_ge(a["dt_a"], 1)
            nc.scalar.activation(soft_b, soft_b, ACT.Exp, scale=-1.0).then_inc(a["dt_b"], 1)
            nc.scalar.activation(exp_a[:, 0:32], m.head_rows[:, 32:64], ACT.Exp)
            nc.scalar.activation(exp_a[0:32, 32:33], m.head_cols[:, 1:2], ACT.Exp).then_inc(a["dt_b"], 1)
            act.wait_ge(a["dt_c"], 1)
            nc.scalar.activation(soft_b, soft_b, ACT.Ln).then_inc(a["dt_b"], 1)
            act.wait_ge(a["dt_done"], 1)
            nc.scalar.activation(s_cols[:, 8:16], s_cols[:, 8:16], ACT.Exp).then_inc(a["dt_b"], 1)
            act.wait_ge(a["pads"], 2)

            def pad(g, t):
                unit = 4 * place[("x", g)] + t
                act.wait_ge(a["proj_ready"], unit + 1)
                if g >= 2 and t == 0:
                    act.wait_ge(a["conv_ready"], g - 1)
                    act.wait_ge(a["conv_rows"], 2 * (g - 1))
                nc.scalar.copy(xpad[g % 2][:, t, 3:515], bank[unit % 2][:, :]).then_inc(
                    a[f"proj_free{unit % 2}"], 1)
                act.wait_ge(a[f"proj_free{unit % 2}"], unit // 2 + 1)
                act.sem_inc(a["pad_ready"], 1)

            def gate(j, t):
                unit = 4 * place[("z", j)] + t
                act.wait_ge(a["proj_ready"], unit + 1)
                if 4 * j + t:
                    act.wait_ge(a["z_ready"], 5 * j + t)
                nc.scalar.activation(z_tanh, bank[unit % 2][:, :], ACT.Tanh, scale=0.5).then_inc(a["z_tanh"], 1)
                if t == 3:
                    act.wait_ge(a["small_ready"], place[("z", j)] + 1)
                    nc.scalar.activation(zs_tanh, bank[2][:, 0:32].rearrange("p (c b) -> p c b", c=4), ACT.Tanh,
                                         scale=0.5).then_inc(a["z_tanh"], 1)

            def unit_of(g, point):
                found = unit_at(g, point)
                if found:
                    (kind, number), t = found
                    (pad if kind == "x" else gate)(number, t)

            def silu(g):
                act.wait_ge(a["conv_ready"], g + 1)
                nc.scalar.activation(tanh, xc[g % 2], ACT.Tanh).then_inc(a["tanh_ready"], 1)

            for t in range(4):
                pad(0, t)
            act.wait_ge(a["sums_kept"], 1)
            nc.scalar.activation(from_start, acs, ACT.Exp)
            nc.scalar.activation(to_end, to_end, ACT.Exp)
            nc.scalar.activation(chunk_decay, chunk_decay, ACT.Exp).then_inc(a["dt_b"], 1)
            silu(0)
            for t in range(4):
                pad(1, t)

            def keep_rows(g, k):
                act.wait_ge(a["turn_ready"], turn_at[("rows", g, k)] + 1)
                if g >= 2 and k == 0:
                    act.wait_ge(a["y_free"], NCK * (g - 1))
                    act.wait_ge(a["skip_ready"], g - 1)
                nc.scalar.copy(rows[g % 2][:, k], bank[3][:, 0:384]).then_inc(a["turn_free"], 1)

            for g in range(G):
                keep_rows(g, 0)
                keep_rows(g, 1)
                unit_of(g, "rows")
                keep_rows(g, 2)
                keep_rows(g, 3)
                for k in range(NCK):
                    i = NCK * g + k
                    act.wait_ge(a["diff_ready"], i + 1)
                    nc.scalar.activation(decay[i % 2], decay[i % 2], ACT.Exp).then_inc(a["exp_ready"], 1)
                    unit_of(g, f"chunk{k}")
                    if k == 0 and g + 1 < G:
                        silu(g + 1)
                unit_of(g, "end0")
                act.wait_ge(a["turn_ready"], turn_at[("last", g, 0)] + 1)
                if g:
                    act.wait_ge(a["h_stored"], 16 * g)
                nc.scalar.copy(h_out, bank[3][:, 0:256].rearrange("p (c n) -> p c n", c=2)).then_inc(a["turn_free"], 1)
                unit_of(g, "end1")
                unit_of(g, "end2")

        @block.vector
        def _(dve):
            link = lambda i: sh.dve(dve, i)
            nc.vector.tensor_scalar(half_w, m.conv_w, 0.5, None, ALU.mult)
            link(nc.vector.tensor_scalar(half_b, m.conv_b, 0.5, None, ALU.mult))
            link(nc.vector.memset(soft_a, 0.0))
            dve.wait_ge(a["conv_in"], 16)
            dve.wait_ge(a["dt_ready"], 1)
            nc.vector.tensor_tensor(by_head(soft_a[:, 0:128]), by_head(bank[5][:, 0:128]),
                                    m.head_rows[:, 0:32].unsqueeze(1).to_broadcast([P, 4, 32]), ALU.add)
            link(nc.vector.tensor_scalar(soft_a[0:32, 128:136], bank[6][0:32, 0:8], m.head_cols[:, 0:1], None, ALU.add))
            link(nc.vector.tensor_scalar(soft_b, soft_a, -1.0, None, ALU.mult))
            nc.vector.tensor_tensor(soft_b, soft_b, soft_a, ALU.max).then_inc(a["dt_a"], 1)
            dve.wait_ge(a["dt_b"], 2)
            nc.vector.tensor_scalar(soft_b, soft_b, 1.0, None, ALU.add).then_inc(a["dt_c"], 1)
            dve.wait_ge(a["dt_b"], 3)
            link(nc.vector.scalar_tensor_tensor(soft_c, soft_a, 0.0, soft_b, ALU.max, ALU.add))
            nc.vector.tensor_copy(dt, soft_c[:, 0:128])
            nc.vector.tensor_copy(s_cols[:, 0:8], soft_c[0:32, 128:136])
            nc.vector.tensor_copy(s_cols[:, 16:17], m.head_cols[:, 2:3])
            nc.vector.tensor_scalar(s_cols[:, 8:16], soft_c[0:32, 128:136], exp_a[0:32, 32:33], -1.0, ALU.mult, ALU.mult)
            nc.vector.scalar_tensor_tensor(by_head(dta), by_head(soft_c[:, 0:128]), -1.0,
                                           exp_a[:, 0:32].unsqueeze(1).to_broadcast([P, 4, 32]), ALU.mult,
                                           ALU.mult).then_inc(a["dt_done"], 1)
            def windows(g):
                dve.wait_ge(a["small_ready"], place[("x", g)] + 1)
                if g:
                    dve.wait_ge(a["conv_rows"], 2 * g)
                nc.vector.tensor_copy(window[:, :, :, 0:3], conv_state[:, 4 * g:4 * g + 4])
                nc.vector.tensor_copy(window[:, :, :, 3], bank[2][:, 0:32].rearrange("p (c b) -> p c b", c=4)).then_inc(
                    a["small_free"], 1)
                dve.wait_ge(a["small_free"], place[("x", g)] + 1)
                dve.sem_inc(a["window_ready"], 1)

            def conv(g):
                out = xc[g % 2]
                link(nc.vector.tensor_tensor(window_w, window,
                                             half_w[:, 4 * g:4 * g + 4].unsqueeze(2).to_broadcast([P, 4, 8, 4]),
                                             ALU.mult))
                if g >= 2:
                    dve.wait_ge(a["y_ready"], NCK * (g - 1))
                    dve.wait_ge(a["bc_ready"], 4 * (g - 1))
                link(nc.vector.tensor_reduce(out[:, :, 512:520], window_w, X_AXIS, ALU.add))
                nc.vector.tensor_tensor(out[:, :, 512:520], out[:, :, 512:520],
                                        half_b[:, 4 * g:4 * g + 4].unsqueeze(2).to_broadcast([P, 4, 8]), ALU.add)
                dve.wait_ge(a["pad_ready"], 4 * g + 4)
                for t in range(4):
                    w = half_w[:, 4 * g + t]
                    last = nc.vector.tensor_scalar(out[:, t, 0:512], xpad[g % 2][:, t, 0:512], w[:, 0:1],
                                                   half_b[:, 4 * g + t:4 * g + t + 1], ALU.mult, ALU.add)
                link(last)
                for j in range(1, 4):
                    for t in range(4):
                        last = nc.vector.scalar_tensor_tensor(out[:, t, 0:512], xpad[g % 2][:, t, j:j + 512],
                                                              half_w[:, 4 * g + t, j:j + 1], out[:, t, 0:512],
                                                              ALU.mult, ALU.add)
                    if j < 3:
                        link(last)
                last.then_inc(a["conv_ready"], 1)

            def conv_silu(g):
                dve.wait_ge(a["tanh_ready"], g + 1)
                link(nc.vector.scalar_tensor_tensor(xc[g % 2], tanh, 1.0, xc[g % 2], ALU.add, ALU.mult))
                dve.sem_inc(a["xc_ready"], 1)

            def gate_values(j, t):
                unit = 4 * place[("z", j)] + t
                dve.wait_ge(a["z_tanh"], 5 * j + t + 1)
                nc.vector.scalar_tensor_tensor(z[:, t], z_tanh, 1.0, bank[unit % 2][:, :], ALU.add,
                                               ALU.mult).then_inc(a[f"proj_free{unit % 2}"], 1)
                dve.wait_ge(a[f"proj_free{unit % 2}"], unit // 2 + 1)
                dve.sem_inc(a["z_ready"], 1)
                if t == 3:
                    dve.wait_ge(a["z_tanh"], 5 * j + 5)
                    nc.vector.scalar_tensor_tensor(zs[:, 4 * j:4 * j + 4], zs_tanh, 1.0,
                                                   bank[2][:, 0:32].rearrange("p (c b) -> p c b", c=4), ALU.add,
                                                   ALU.mult).then_inc(a["small_free"], 1)
                    dve.wait_ge(a["small_free"], place[("z", j)] + 1)
                    dve.sem_inc(a["z_ready"], 1)

            def unit_of(g, point):
                found = unit_at(g, point)
                if found:
                    (kind, number), t = found
                    if kind == "z":
                        gate_values(number, t)
                    elif t == 3:
                        windows(number)

            def decays(g, k):
                i = NCK * g + k
                dve.wait_ge(a["cb_ready"], i + 1)
                if i >= 2:
                    dve.wait_ge(a["mix_ready"], i - 1)
                    dve.wait_ge(a["y_ready"], i - 1)
                nc.vector.tensor_tensor(cb[i % 2], bank[5][:, 0:128], m.c(C_TRI), ALU.mult).then_inc(a["cb_free"], 1)
                dve.wait_ge(a["acs_ready"], i + 1)
                for e in range(4):
                    h = 32 * k + 4 * g + e
                    last = nc.vector.tensor_scalar(decay[i % 2][:, e], bank[4][:, P * e:P * e + P], acs[:, h:h + 1], 0.0,
                                                   ALU.subtract, ALU.min)
                last.then_inc(a["diff_ready"], 1)

            def start_chunks(g):
                dve.wait_ge(a["turn_free"], turn_at[("rows", g, 3)] + 1)
                if g:
                    dve.wait_ge(a["turn_ready"], turn_at[("state", g - 1, 3)] + 1)
                x_rows = rows[g % 2][:, :, 0:256].rearrange("p k (e c) -> p k e c", e=4)
                heads = slice(4 * g, 4 * g + 4)
                link(nc.vector.tensor_tensor(xdt, x_rows, by_head(dt)[:, :, heads].unsqueeze(3).to_broadcast([P, 4, 4, 64]),
                                             ALU.mult))
                nc.vector.tensor_tensor(xdt_end, xdt, by_head(to_end)[:, :, heads].unsqueeze(3).to_broadcast([P, 4, 4, 64]),
                                        ALU.mult).then_inc(a["xdt_ready"], 1)
                decays(g, 0)

            def chunk(g, k):
                heads = slice(4 * g, 4 * g + 4)
                i = NCK * g + k
                if k == 0:
                    dve.wait_ge(a["skip_ready"], g + 1)
                dve.wait_ge(a["y_ready"], i + 1)
                yk = y[:, k, 256 * g:256 * g + 256]
                if k:
                    nc.vector.tensor_tensor(off.rearrange("p (e c) -> p e c", e=4),
                                            bank[6][:, 256:512].rearrange("p (e c) -> p e c", e=4),
                                            by_head(from_start)[:, k, heads].unsqueeze(2).to_broadcast([P, 4, 64]),
                                            ALU.mult)
                nc.vector.tensor_tensor(yk, yk, bank[6][:, 0:256], ALU.add).then_inc(a["y_free"], 1)
                dve.wait_ge(a["y_free"], i + 1)
                if k:
                    nc.vector.tensor_tensor(yk, yk, off, ALU.add)
                if k:
                    link(nc.vector.tensor_tensor(
                        hT[k % 2].rearrange("p (e c) -> p e c", e=4), hT[(k - 1) % 2].rearrange("p (e c) -> p e c", e=4),
                        by_head(chunk_decay)[:, k, heads].unsqueeze(2).to_broadcast([P, 4, 64]), ALU.mult))
                t = turn_at[("state", g, k)]
                dve.wait_ge(a["turn_ready"], t + 1)
                if k:
                    last = nc.vector.tensor_tensor(hT[k % 2], hT[k % 2], bank[3][:, 0:256], ALU.add)
                else:
                    last = nc.vector.tensor_copy(hT[0], bank[3][:, 0:256])
                last.then_inc(a["turn_free"], 1)
                dve.wait_ge(a["turn_free"], t + 1)
                dve.sem_inc(a["h_ready"], 1)

            def sample(g, q):
                if q == 0:
                    xs = xc[g % 2][:, 0:2, 512:520]
                    nc.vector.tensor_tensor(skip_s, xs, s_head[:, 2 * g:2 * g + 2, 16:17].to_broadcast([P, 2, 8]),
                                            ALU.mult)
                    link(nc.vector.tensor_tensor(xdt_s, xs, s_head[:, 2 * g:2 * g + 2, 0:8], ALU.mult))
                i = 4 * g + q
                part = slice(4 * (q % 2), 4 * (q % 2) + 4)
                dve.wait_ge(a["bc_ready"], i + 1)
                wide = bank[7][:, :].rearrange("p (b n) -> p b n", b=4)
                for half in range(2):
                    other = state[:, half, part] if q >= 2 else \
                        xdt_s[:, half, part].unsqueeze(2).to_broadcast([P, 4, P])
                    last = nc.vector.tensor_tensor(update[:, half, part], wide, other, ALU.mult)
                last.then_inc(a["bc_free"], 1)
                dve.wait_ge(a["bc_free"], i + 1)
                if q == 1:
                    dve.wait_ge(a["state_decayed"], g + 1)
                    nc.vector.tensor_tensor(state, state, update, ALU.add).then_inc(a["state_new"], 1)
                    dve.wait_ge(a["state_new"], g + 1)
                if q == 3:
                    link(nc.vector.tensor_reduce(ys[:, 2 * g:2 * g + 2], update, X_AXIS, ALU.add))
                    link(nc.vector.tensor_tensor(ys[:, 2 * g:2 * g + 2], ys[:, 2 * g:2 * g + 2], skip_s, ALU.add))

            windows(0)
            dve.wait_ge(a["sums_ready"], 1)
            nc.vector.tensor_copy(acs, bank[4][:, 0:128])
            link(nc.vector.tensor_copy(chunk_decay, bank[4][:, 128:256]))
            nc.vector.tensor_tensor(to_end, chunk_decay, acs, ALU.subtract).then_inc(a["sums_kept"], 1)
            dve.wait_ge(a["expand_ready"], 1)
            nc.vector.tensor_copy(s_head, bank[6][:, 0:272].rearrange("p (c j) -> p c j", c=16)).then_inc(
                a["expand_kept"], 1)
            conv(0)
            conv_silu(0)
            windows(1)
            dve.wait_ge(a["dt_b"], 5)
            for g in range(G):
                unit_of(g, "rows")
                start_chunks(g)
                if g + 1 < G:
                    conv(g + 1)
                unit_of(g, "chunk0")
                for k in range(NCK):
                    if k + 1 < NCK:
                        decays(g, k + 1)
                    chunk(g, k)
                    if k == 0:
                        if g + 1 < G:
                            conv_silu(g + 1)
                    else:
                        sample(g, k - 1)
                    if k + 1 < NCK:
                        unit_of(g, f"chunk{k + 1}")
                unit_of(g, "end0")
                sample(g, 3)
                unit_of(g, "end1")
                unit_of(g, "end2")
                if g % 2:
                    j = g // 2
                    link(nc.vector.scalar_tensor_tensor(y[:, :, 512 * j:512 * j + 512], z, 0.5,
                                                        y[:, :, 512 * j:512 * j + 512], ALU.mult, ALU.mult))
            link(nc.vector.scalar_tensor_tensor(ys, zs, 0.5, ys, ALU.mult, ALU.mult))

        @block.tensor
        def _(pe):
            pe.wait_ge(a["small_in"], 16)
            for k4 in range(4):
                for k in range(8):
                    nc.tensor.matmul(bank[5][:, 32 * k4:32 * k4 + 32], m.hT[:, k, P * k4:P * k4 + P],
                                     w_dt[:, 32 * k:32 * k + 32], start=(k == 0), stop=(k == 7))
            for k in range(8):
                last = nc.tensor.matmul(bank[6][0:32, 0:8], w_dt[:, 32 * k:32 * k + 32], m.hT[:, k, SEQ:T_ALL],
                                        start=(k == 0), stop=(k == 7))
            last.then_inc(a["dt_ready"], 1)

            def project(key, t):
                i = place[key]
                b = B_SSD + i
                w = m.slot[b % 2]
                if t == 0:
                    pe.wait_ge(s[f"ring_in{b % 2}"], 16 * (b // 2 + 1))
                    if i:
                        pe.wait_ge(a["small_free"], i)
                unit = 4 * i + t
                if unit >= 2:
                    pe.wait_ge(a[f"proj_free{unit % 2}"], unit // 2)
                for k in range(8):
                    cols = w[:, 512 * k + P * t:512 * k + P * t + P]
                    if key[0] == "x":
                        nc.tensor.matmul(bank[unit % 2][:, :], cols, m.hT[:, k, 0:SEQ], start=(k == 0), stop=(k == 7))
                    else:
                        nc.tensor.matmul(bank[unit % 2][:, :], m.hT[:, k, P * t:P * t + P],
                                         w[:, 512 * k:512 * k + 512], start=(k == 0), stop=(k == 7))
                    small = nc.tensor.matmul(bank[2][:, 8 * t:8 * t + 8], cols, m.hT[:, k, SEQ:T_ALL],
                                             start=(k == 0), stop=(k == 7))
                small.then_inc(a["proj_ready"], 1)
                if t == 3:
                    pe.wait_ge(a["proj_ready"], 4 * i + 4)
                    pe.sem_inc(a["small_ready"], 1)

            def unit_of(g, point):
                found = unit_at(g, point)
                if found:
                    project(*found)

            for t in range(4):
                project(("x", 0), t)
            pe.wait_ge(a["dt_done"], 1)
            nc.tensor.matmul(bank[4][:, 0:128], m.c(C_TRI), dta, start=True, stop=True)
            nc.tensor.matmul(bank[4][:, 128:256], m.c(C_ONES), dta, start=True, stop=True).then_inc(a["sums_ready"], 1)
            pe.wait_ge(a["dt_b"], 4)
            for pair in range(16):
                last = nc.tensor.matmul(bank[6][:, 17 * pair:17 * pair + 17], m.c(C_EXPAND + P * pair, P, 32), s_cols,
                                        start=True, stop=True)
            last.then_inc(a["expand_ready"], 1)
            for t in range(4):
                project(("x", 1), t)
            pe.wait_ge(a["sums_kept"], 1)
            pe.wait_ge(a["expand_kept"], 1)

            def own_turn(key):
                i = turn_at[key]
                if i:
                    pe.wait_ge(a["turn_free"], i)

            def weigh(g, k):
                i = NCK * g + k
                x = xc[g % 2]
                if i:
                    pe.wait_ge(a["cb_free"], i)
                nc.tensor.matmul(bank[5][:, 0:128], x[:, 2, P * k:P * k + P], x[:, 3, P * k:P * k + P], start=True,
                                 stop=True).then_inc(a["cb_ready"], 1)
                if i:
                    pe.wait_ge(a["diff_ready"], i)
                for e in range(4):
                    h = 32 * k + 4 * g + e
                    last = nc.tensor.matmul(bank[4][:, P * e:P * e + P], dta[:, h:h + 1].to_broadcast([P, P]),
                                            m.c(C_TRI), start=True, stop=True)
                last.then_inc(a["acs_ready"], 1)

            def spread(g, q):
                i = 4 * g + q
                if i:
                    pe.wait_ge(a["bc_free"], i)
                for b in range(4):
                    at_b = SEQ + 4 * (q % 2) + b
                    last = nc.tensor.matmul(bank[7][:, P * b:P * b + P],
                                            xc[g % 2][:, 2 + q // 2, at_b:at_b + 1].to_broadcast([P, P]),
                                            m.c(C_IDENT), start=True, stop=True)
                last.then_inc(a["bc_ready"], 1)

            def chunk_products(g, k):
                i = NCK * g + k
                x = xc[g % 2]
                if k == 0:
                    pe.wait_ge(a["xdt_ready"], g + 1)
                pe.wait_ge(a["mix_ready"], i + 1)
                if i:
                    pe.wait_ge(a["y_free"], i)
                if k:
                    pe.wait_ge(a["h_ready"], i)
                    nc.tensor.matmul(bank[6][:, 256:512], x[:, 3, P * k:P * k + P], hT[(k - 1) % 2], start=True,
                                     stop=True)
                for e in range(4):
                    last = nc.tensor.matmul(bank[6][:, 64 * e:64 * e + 64], decay[i % 2][:, e], xdt[:, k, e],
                                            start=True, stop=True)
                last.then_inc(a["y_ready"], 1)
                own_turn(("state", g, k))
                nc.tensor.matmul(bank[3][:, 0:256], rows[g % 2][:, k, 256:384], xdt_end[:, k], start=True,
                                 stop=True).then_inc(a["turn_ready"], 1)

            def turn_rows(g, k):
                own_turn(("rows", g, k))
                for j in range(3):
                    last = nc.tensor.transpose(bank[3][:, P * j:P * j + P], xc[g % 2][:, j, P * k:P * k + P],
                                               m.c(C_IDENT))
                last.then_inc(a["turn_ready"], 1)

            for g in range(G):
                pe.wait_ge(a["xc_ready"], g + 1)
                turn_rows(g, 0)
                turn_rows(g, 1)
                unit_of(g, "rows")
                turn_rows(g, 2)
                turn_rows(g, 3)
                weigh(g, 0)
                for k in range(NCK):
                    unit_of(g, f"chunk{k}")
                    if k + 1 < NCK:
                        weigh(g, k + 1)
                    chunk_products(g, k)
                    if k:
                        spread(g, k - 1)
                unit_of(g, "end0")
                spread(g, 3)
                own_turn(("last", g, 0))
                for half in range(2):
                    last = nc.tensor.transpose(bank[3][:, P * half:P * half + P], hT[1][:, P * half:P * half + P],
                                               m.c(C_IDENT))
                last.then_inc(a["turn_ready"], 1)
                unit_of(g, "end1")
                unit_of(g, "end2")


def merge_branches(sh):
    nc, ins, m, bank, s = sh.nc, sh.ins, sh.m, sh.bank, sh.s
    x = sh.x = m.at(0, 5120).rearrange("p (n d) -> p n d", n=N_T)
    gates = m.at(5120, 8320).rearrange("p (c t) -> p c t", t=T_ALL)
    yT = m.at(13440, 8320).rearrange("p (c t) -> p c t", t=T_ALL)
    squares = m.at(13440, 8192).rearrange("p (k c) -> p k c", k=4)
    merged = m.at(21760, 4160).rearrange("p (c t) -> p c t", t=T_ALL)
    y, ys = sh.y, sh.ys
    parts = [m.at(26216 + 512 * i, 512) for i in range(2)]
    stat = m.at(25920, 32)
    part_s = m.at(25952, 128)
    n_units = [4] * 4 + [8] + [2] * 4 + [5] * 2
    upto = [sum(n_units[:i + 1]) for i in range(len(n_units))]
    first = [u - n for u, n in zip(upto, n_units)]

    with ExitStack() as c:
        names = ("x_in", "squares", "inverse", "roots", "scaled", "turned", "turn_free", "s_square", "s_sum",
                 "s_inverse", "s_scaled", "proj_ready", "proj_free0", "proj_free1", "small_free", "gates", "merged",
                 "done")
        a = stage_semaphores(nc, c, "d_", names)
        block = c.enter_context(nc.Block())

        @block.sync
        def _(sp):
            sp.dma_start(x[:, 0:4, :], ins["x_prompt"].rearrange("(n p) d -> p n d", p=P)).then_inc(a["x_in"], 16)
            sp.dma_start(x[0:N_S, 4, :], ins["x_sample"]).then_inc(a["x_in"], 16)
            for i in range(2, 13):
                b = B_GATE + i
                sp.wait_ge(a["proj_ready"], upto[i - 2])
                sp.dma_start(m.slot[b % 2], ins["stream"][b]).then_inc(s[f"ring_in{b % 2}"], 16)

        @block.scalar
        def _(act):
            for k in range(4):
                nc.scalar.activation(squares[:, k], y[:, k], ACT.Square, accum_out=stat[:, k:k + 1]).then_inc(a["squares"], 1)
            act.wait_ge(a["inverse"], 1)
            nc.scalar.activation(stat[:, 8:12], stat[:, 4:8], ACT.Sqrt).then_inc(a["roots"], 1)
            act.wait_ge(a["s_inverse"], 1)
            nc.scalar.activation(stat[:, 24:32], stat[:, 16:24], ACT.Sqrt).then_inc(a["roots"], 1)
            for i in range(4):
                for t in range(4):
                    unit = first[i] + t
                    act.wait_ge(a["proj_ready"], unit + 1)
                    nc.scalar.activation(gates[:, 4 * i + t, 0:SEQ], bank[unit % 2][:, :], ACT.Tanh,
                                         scale=0.5).then_inc(a[f"proj_free{unit % 2}"], 1)
                nc.scalar.activation(gates[:, 4 * i:4 * i + 4, SEQ:T_ALL],
                                     bank[2][:, 0:32].rearrange("p (c b) -> p c b", c=4), ACT.Tanh,
                                     scale=0.5).then_inc(a["small_free"], 1)
            act.wait_ge(a["small_free"], 4)
            act.sem_inc(a["gates"], 1)

        @block.vector
        def _(dve):
            link = lambda i: sh.dve(dve, i)
            dve.wait_ge(a["squares"], 4)
            link(nc.vector.tensor_scalar(stat[:, 0:4], stat[:, 0:4], 1.0 / D_INNER, EPS, ALU.mult, ALU.add))
            nc.vector.reciprocal(stat[:, 4:8], stat[:, 0:4]).then_inc(a["inverse"], 1)
            nc.vector.tensor_tensor(part_s, ys.rearrange("p c b -> p (c b)"), ys.rearrange("p c b -> p (c b)"),
                                    ALU.mult).then_inc(a["s_square"], 1)
            dve.wait_ge(a["s_sum"], 1)
            link(nc.vector.tensor_reduce(stat[:, 16:24], bank[7][:, 0:128].rearrange("p (c b) -> p b c", c=16), X_AXIS,
                                         ALU.add))
            link(nc.vector.tensor_scalar(stat[:, 16:24], stat[:, 16:24], 1.0 / D_INNER, EPS, ALU.mult, ALU.add))
            nc.vector.reciprocal(stat[:, 16:24], stat[:, 16:24]).then_inc(a["s_inverse"], 1)
            dve.wait_ge(a["roots"], 1)
            for k in range(4):
                nc.vector.tensor_scalar(y[:, k], y[:, k], stat[:, 8 + k:9 + k], None, ALU.mult).then_inc(a["scaled"], 1)
            dve.wait_ge(a["roots"], 2)
            link(nc.vector.tensor_tensor(ys, ys, stat[:, 24:32].unsqueeze(1).to_broadcast([P, 16, 8]), ALU.mult))
            nc.vector.tensor_tensor(yT[:, :, SEQ:T_ALL], ys, m.norm_ssd.unsqueeze(2).to_broadcast([P, 16, 8]),
                                    ALU.mult).then_inc(a["s_scaled"], 1)
            for k in range(4):
                for q in range(4):
                    i = 4 * k + q
                    dve.wait_ge(a["turned"], i + 1)
                    nc.vector.tensor_tensor(yT[:, 4 * q:4 * q + 4, P * k:P * k + P],
                                            bank[5 + i % 2][:, :].rearrange("p (c t) -> p c t", c=4),
                                            m.norm_ssd[:, 4 * q:4 * q + 4].unsqueeze(2).to_broadcast([P, 4, P]),
                                            ALU.mult).then_inc(a["turn_free"], 1)
            dve.wait_ge(a["turn_free"], 16)
            dve.wait_ge(a["gates"], 1)
            for t in range(8):
                unit = first[4] + t
                dve.wait_ge(a["proj_ready"], unit + 1)
                nc.vector.scalar_tensor_tensor(merged[:, t, 0:SEQ], gates[:, t, 0:SEQ], 1.0, bank[unit % 2][:, :],
                                               ALU.add, ALU.mult).then_inc(a[f"proj_free{unit % 2}"], 1)
            nc.vector.scalar_tensor_tensor(merged[:, :, SEQ:T_ALL], gates[:, 0:8, SEQ:T_ALL], 1.0,
                                           bank[2][:, 0:64].rearrange("p (c b) -> p c b", c=8),
                                           ALU.add, ALU.mult).then_inc(a["small_free"], 1)
            dve.wait_ge(a["small_free"], 5)
            for j in range(4):
                for t in range(2):
                    unit = first[5 + j] + t
                    row = 2 * j + t
                    part = parts[t]
                    dve.wait_ge(a["proj_ready"], unit + 1)
                    nc.vector.scalar_tensor_tensor(part, gates[:, 8 + row, 0:SEQ], 1.0, bank[unit % 2][:, :],
                                                   ALU.add, ALU.mult).then_inc(a[f"proj_free{unit % 2}"], 1)
                    dve.wait_ge(a[f"proj_free{unit % 2}"], unit // 2 + 1)
                    nc.vector.tensor_tensor(merged[:, row, 0:SEQ], merged[:, row, 0:SEQ], part, ALU.add)
                small = part_s[:, 0:16].rearrange("p (c b) -> p c b", c=2)
                nc.vector.scalar_tensor_tensor(small, gates[:, 8 + 2 * j:10 + 2 * j, SEQ:T_ALL], 1.0,
                                               bank[2][:, 0:16].rearrange("p (c b) -> p c b", c=2),
                                               ALU.add, ALU.mult).then_inc(a["small_free"], 1)
                dve.wait_ge(a["small_free"], 6 + j)
                nc.vector.tensor_tensor(merged[:, 2 * j:2 * j + 2, SEQ:T_ALL], merged[:, 2 * j:2 * j + 2, SEQ:T_ALL],
                                        small, ALU.add).then_inc(a["merged"], 1)
                dve.wait_ge(a["merged"], j + 1)
            for j in range(2):
                for t in range(5):
                    unit = first[9 + j] + t
                    r = rows_of(t)
                    dve.wait_ge(a["proj_ready"], unit + 1)
                    xs = x[0:r, t, 512 * j:512 * j + 512]
                    if unit == first[9]:
                        dve.wait_ge(a["x_in"], 32)
                    nc.vector.scalar_tensor_tensor(xs, bank[unit % 2][0:r, :], 0.5, xs, ALU.mult,
                                                   ALU.add).then_inc(a[f"proj_free{unit % 2}"], 1)
            dve.wait_ge(a["proj_free0"], upto[-1] // 2)

        @block.tensor
        def _(pe):
            def unit_free(unit):
                if unit >= 2:
                    pe.wait_ge(a[f"proj_free{unit % 2}"], unit // 2)

            def columns(i, n_k, width, src):
                b = B_GATE + i
                w = m.slot[b % 2]
                pe.wait_ge(s[f"ring_in{b % 2}"], 16 * (b // 2 + 1))
                if i:
                    pe.wait_ge(a["small_free"], i)
                for t in range(n_units[i]):
                    unit = first[i] + t
                    unit_free(unit)
                    for k in range(n_k):
                        cols = w[:, width * k + P * t:width * k + P * t + P]
                        nc.tensor.matmul(bank[unit % 2][:, :], cols, src[:, k, 0:SEQ], start=(k == 0),
                                         stop=(k == n_k - 1))
                        last = nc.tensor.matmul(bank[2][:, 8 * t:8 * t + 8], cols, src[:, k, SEQ:T_ALL],
                                                start=(k == 0), stop=(k == n_k - 1))
                    last.then_inc(a["proj_ready"], 1)

            pe.wait_ge(a["s_square"], 1)
            nc.tensor.matmul(bank[7][:, 0:128], m.c(C_ONES), part_s, start=True, stop=True).then_inc(a["s_sum"], 1)
            for i in range(4):
                columns(i, 8, 512, m.hT)
            for k in range(4):
                pe.wait_ge(a["scaled"], k + 1)
                for q in range(4):
                    i = 4 * k + q
                    if i >= 2:
                        pe.wait_ge(a["turn_free"], i - 1)
                    for j in range(4):
                        at = P * (4 * q + j)
                        last = nc.tensor.transpose(bank[5 + i % 2][:, P * j:P * j + P], y[:, k, at:at + P],
                                                   m.c(C_IDENT))
                    last.then_inc(a["turned"], 1)
            columns(4, 4, 1024, m.attT)
            pe.wait_ge(a["turn_free"], 16)
            pe.wait_ge(a["s_scaled"], 1)
            for i in range(5, 9):
                columns(i, 16, 256, yT)
            pe.wait_ge(a["merged"], 4)
            for i in range(9, 11):
                b = B_GATE + i
                pe.wait_ge(s[f"ring_in{b % 2}"], 16 * (b // 2 + 1))
                for t in range(5):
                    unit = first[i] + t
                    r = rows_of(t)
                    unit_free(unit)
                    for k in range(8):
                        last = nc.tensor.matmul(bank[unit % 2][0:r, :], merged[:, k, P * t:P * t + r],
                                                m.slot[b % 2][:, 512 * k:512 * k + 512], start=(k == 0), stop=(k == 7))
                    last.then_inc(a["proj_ready"], 1)


class LoopChain:

    def __init__(self, sem, turn, length, passed, start=0):
        self.sem, self.turn, self.length, self.start, self.count = sem, turn, length, start, 0
        self.passed = passed

    def __call__(self, eng, ins):
        self.count += 1
        ins.then_inc(self.sem, 1)
        eng.wait_ge(self.sem, self.turn.times(self.length, self.start + self.count))
        eng.sem_inc(self.passed, 1)

    def close(self):
        assert self.count == self.length


U_BUFS = 8
V_BUFS, V_SIDE_BUFS = 4, 2
V_SIDE = (3, 7, 11, 15)
V_MAIN = tuple(k for k in range(TOPK) if k not in V_SIDE)
N_MAIN, N_SIDE = len(V_MAIN), len(V_SIDE)
assert N_MAIN % V_BUFS == 0 and N_SIDE % V_SIDE_BUFS == 0 and V_SIDE[0] == 3


class Head:

    def __init__(self, offset, register=None, scale=1):
        self.offset, self.register, self.scale = offset, register, scale

    def times(self, each, base=0):
        base += self.offset * each
        return base if self.register is None else self.register * (self.scale * each) + base


def peer_and_ple(sh):
    nc, ins, outs, m, bank, s = sh.nc, sh.ins, sh.outs, sh.m, sh.bank, sh.s
    x = sh.x
    hx = m.at(5120, 5120).rearrange("p (n d) -> p n d", n=N_T)
    query = m.at(10240, 8320).rearrange("p (c t) -> p c t", t=T_ALL)
    scores_of = lambda n: query[:, :, P * n:P * n + rows_of(n)]
    keys = m.at(18560, 2048).rearrange("p (c k) -> p c k", c=16)
    ple_x = m.at(20608, 1024).rearrange("p (k t) -> p k t", k=8)
    diag = [m.at(21632 + P * i, P) for i in range(V_BUFS)]
    stage = m.at(22144, 512).rearrange("p (a w k) -> p a w k", a=2, w=2)
    p_cols = m.at(22656, 1040).rearrange("p (k t) -> p k t", k=2)
    w_proj = m.at(23696, 2048).rearrange("p (k n) -> p k n", k=2)
    row_tmp = m.at(25744, 1024)
    index_f = m.at(26768, 128)
    index = [m.at(26896 + 128 * i, 128).bitcast(U32) for i in range(2)]
    gate = [m.at(27152 + 128 * i, 128) for i in range(2)]
    top_at = 27408
    val = m.at(top_at, 32).rearrange("p (w k) -> p w k", w=2)
    pos = m.at(top_at + 32, 32).bitcast(U32).rearrange("p (w k) -> p w k", w=2)
    best = m.at(top_at + 64, 16)
    best_at = m.at(top_at + 80, 16).bitcast(U32)
    all_pos = m.at(top_at + 96, 256).rearrange("p (h w k) -> p h w k", h=8, w=2)
    all_best = m.at(top_at + 352, 128).rearrange("p (h k) -> p h k", h=8)
    all_at = m.at(top_at + 480, 128).bitcast(U32)
    digit_u = m.at(top_at + 608, 128).bitcast(U32)
    digit = m.at(top_at + 736, 128)
    picked = [m.at(top_at + 864 + 128 * i, 128) for i in range(2)]
    stat = m.at(top_at + 1120, 64)
    now_u = [m.c(C_RES + 16 * i, 16).bitcast(U32) for i in range(2)]
    now_v = [m.c(C_RES + 32 + 16 * i, 16).bitcast(U32) for i in range(2)]
    dots = m.at(top_at + 1200, 16)
    acts = m.at(top_at + 1216, 16)
    coef = m.at(top_at + 1232, 16)
    index_s = m.at(top_at + 1248, 8).bitcast(U32)
    gate_s = m.at(top_at + 1256, 8)
    assert top_at + 1264 <= 28672
    cand = m.at(28672, 256).rearrange("p (a b) -> p a b", a=16)
    cand_rest = m.at(28928, 256)
    v_buf = [m.at(29184 + 1024 * i, 1024) for i in range(V_BUFS)] + [m.at(33376, 1024), m.mem[:, 8520:9544]]
    coef_s = m.at(33280, 64, P).rearrange("p (b c) -> p b c", b=8)
    dots_s = m.at(33344, 16).rearrange("p (b w) -> p b w", b=8)
    u_buf = [m.slot[i // 4][:, 1024 * (i % 4):1024 * (i % 4) + 1024] for i in range(U_BUFS)]
    w_gate_low = [m.at(18560, 2048), m.mem[:, 4360:6408]]
    w_gate_high = [scores_of(n) for n in range(2)]

    def w_gate(k, j):
        if j == 0:
            return w_gate_low[k // 4][:, 512 * (k % 4):512 * (k % 4) + 512]
        return w_gate_high[k // 4][:, 4 * (k % 4):4 * (k % 4) + 4]
    one_hot = m.mem[:, 6408:8456].rearrange("p (h k a) -> p h k a", h=8, k=16)
    norm_rows = m.mem[:, 8520:10568].rearrange("p (w d) -> p w d", w=2)
    sample_scores = m.c(C_EXPAND, 2048, N_S).rearrange("p (c k) -> p c k", c=16)
    ident = m.c(C_IDENT)
    acc = [(bank[0], bank[1]), (bank[2], bank[7])]

    with ExitStack() as c:
        names = ["small_in", "rows_in", "squares", "inverse", "roots", "scaled", "turned", "columns", "proj_ready",
                 "proj_free0", "proj_free1", "small_free", "score_ready", "score_kept", "query_read", "top_step",
                 "top_done", "gate_max", "gate_exp", "index_ready", "dot_done", "dots_ready", "acts_ready",
                 "coef_ready", "diag_ready", "v_used", "v_added", "u_staged", "v_staged", "acc_done", "acc_kept",
                 "ple_square", "ple_inverse", "ple_root", "ple_scaled", "ple_turned", "ple_columns", "ple_gate",
                 "ple_gated", "ple_proj", "ple_used", "end_square", "end_inverse", "end_root", "end_rows",
                 "stored", "w_gate_in", "s_turned", "s_kept", "s_wide", "s_read", "top_passed", "gather_passed"]
        a = stage_semaphores(nc, c, "e_", names)
        u_in = list(stage_semaphores(nc, c, "e_u_in", [str(i) for i in range(U_BUFS)]).values())
        v_in = list(stage_semaphores(nc, c, "e_v_in", [str(i) for i in range(V_BUFS + V_SIDE_BUFS)]).values())
        block = c.enter_context(nc.Block())

        @block.sync
        def _(sp):
            sp.dma_start(norm_rows.rearrange("p w d -> p (w d)"),
                         ins["norm_rows"].rearrange("w d -> (w d)").partition_broadcast(P)).then_inc(a["rows_in"], 16)
            sp.dma_start(keys.rearrange("p c k -> p (c k)"), ins["keys"]).then_inc(a["small_in"], 16)
            sp.dma_start(p_cols.rearrange("p k t -> p (k t)"), ins["p_cols"]).then_inc(a["small_in"], 16)
            sp.dma_start(w_proj.rearrange("p k n -> p (k n)"), ins["w_ple_proj"]).then_inc(a["small_in"], 16)
            for i in (2, 3):
                b = B_PQ + i
                sp.wait_ge(a["proj_ready"], 4 * (i - 1))
                sp.dma_start(m.slot[b % 2], ins["stream"][b]).then_inc(s[f"ring_in{b % 2}"], 16)
            sp.wait_ge(a["score_ready"], 4 * N_T)
            for i in range(2):
                sp.dma_start(w_gate_low[i], ins["stream"][B_PLE][:, 2048 * i:2048 * i + 2048]).then_inc(
                    a["w_gate_in"], 16)
            sp.wait_ge(a["top_done"], 2)
            for i in range(2):
                src = ins["stream"][B_PLE + 1][:, 2048 * i:2048 * i + 2048].rearrange("p (c k) -> p c k", c=16)
                sp.dma_start(w_gate_high[i], src).then_inc(a["w_gate_in"], 16)
            for n in range(N_T):
                sp.wait_ge(a["end_rows"], n + 1)
                if n == 4:
                    sp.dma_start(outs["y_sample"], x[0:N_S, 4]).then_inc(a["stored"], 16)
                else:
                    sp.dma_start(outs["y_prompt"][P * n:P * n + P], x[:, n]).then_inc(a["stored"], 16)
            sp.wait_ge(a["stored"], 16 * N_T)

        @block.gpsimd
        def _(pool):
            pool.wait_ge(a["proj_ready"], 16)

            def gather(table, idx, buf, arrived):
                nc.gpsimd.indirect_dma_start(buf, None, ins[table], bass.IndirectOffsetOnAxis(idx, 0)).then_inc(
                    arrived, 16)

            def stage_indices(u_head, v_head):
                for head, now, staged in ((u_head, now_u, "u_staged"), (v_head, now_v, "v_staged")):
                    if head is not None:
                        n, hd, odd = head
                        nc.gpsimd.tensor_copy(now[odd], index[n % 2][:, bass.ds(hd.times(16), 16)]).then_inc(
                            a[staged], 1)
                for head, staged in ((u_head, "u_staged"), (v_head, "v_staged")):
                    if head is not None:
                        pool.wait_ge(a[staged], head[1].times(1, 8 * head[0] + 1))

            def gather_u(n, hd, odd, k):
                pool.wait_ge(a["dot_done"], hd.times(16, 128 * n + k + 1))
                pool.sem_inc(a["gather_passed"], 1)
                gather("peer_u", now_u[odd][:, k:k + 1], u_buf[k % U_BUFS], u_in[k % U_BUFS])

            def gather_v(n, hd, odd, k):
                if k in V_SIDE:
                    i = V_SIDE.index(k)
                    pool.wait_ge(a["v_added"], hd.times(N_SIDE, 8 * N_SIDE * n + i + 1))
                    b = V_BUFS + i % V_SIDE_BUFS
                else:
                    i = V_MAIN.index(k)
                    pool.wait_ge(a["v_used"], hd.times(N_MAIN, 8 * N_MAIN * n + i + 1))
                    b = i % V_BUFS
                pool.sem_inc(a["gather_passed"], 1)
                gather("peer_v", now_v[odd][:, k:k + 1], v_buf[b], v_in[b])

            def step(n, hd, before, odd):
                stage_indices((n, hd, odd), (n, before, 1 - odd))
                for k in range(TOPK):
                    gather_u(n, hd, odd, k)
                    gather_v(n, before, 1 - odd, k)

            for n in range(4):
                last = Head(7)
                if n:
                    stage_indices(None, (n - 1, last, 1))
                    for k in range(8):
                        gather_v(n - 1, last, 1, k)
                pool.wait_ge(a["index_ready"], n + 1)
                stage_indices((n, Head(0), 0), None)
                for k in range(8):
                    if n:
                        gather_v(n - 1, last, 1, 8 + k)
                    gather_u(n, Head(0), 0, 2 * k)
                    gather_u(n, Head(0), 0, 2 * k + 1)
                with pool.Fori(0, 3) as two:
                    for odd in (1, 0):
                        step(n, Head(2 - odd, two, 2), Head(1 - odd, two, 2), odd)
                step(n, Head(7), Head(6), 1)
            stage_indices(None, (3, Head(7), 1))
            for k in range(TOPK):
                gather_v(3, Head(7), 1, k)
            pool.wait_ge(a["gather_passed"], 4 * 8 * 2 * TOPK)
            pool.wait_ge(a["s_kept"], 2)
            for b in range(N_S):
                pool.wait_ge(a["dot_done"], 32 * TOPK + b + 1)
                gather("peer_u", index_s[:, b:b + 1], u_buf[b], u_in[b])
            for b in range(N_S):
                pool.wait_ge(a["v_used"], 32 * N_MAIN + b + 1)
                gather("peer_v", index_s[:, b:b + 1], v_buf[b % V_BUFS], v_in[b % V_BUFS])

        @block.scalar
        def _(act):
            for n in range(N_T):
                r = rows_of(n)
                if n == 0:
                    act.wait_ge(a["squares"], 1)
                nc.scalar.activation(hx[0:r, n], x[0:r, n], ACT.Square, accum_out=stat[0:r, n:n + 1]).then_inc(
                    a["squares"], 1)
            act.wait_ge(a["inverse"], 1)
            nc.scalar.activation(stat[:, 16:21], stat[:, 8:13], ACT.Sqrt).then_inc(a["roots"], 1)
            for n in range(N_T):
                r = rows_of(n)
                for half in range(2):
                    act.wait_ge(a["turned"], 2 * n + half + 1)
                    nc.scalar.copy(m.hT[:, 4 * half:4 * half + 4, P * n:P * n + r],
                                   bank[5 + half][:, :].rearrange("p (c t) -> p c t", c=4)[:, :, 0:r]).then_inc(
                        a["columns"], 1)
            def keep_scores(i):
                for n in range(N_T):
                    r = rows_of(n)
                    unit = N_T * i + n
                    act.wait_ge(a["score_ready"], unit + 1)
                    src = bank[3 + unit % 4][0:r, :].rearrange("p (c k) -> p c k", c=4)
                    dst = query[0:r, 4 * i:4 * i + 4, P * n:P * n + P] if n < 4 else \
                        sample_scores[:, 4 * i:4 * i + 4]
                    nc.scalar.copy(dst, src).then_inc(a["score_kept"], 1)

            for i in range(4):
                for t in range(4):
                    unit = 4 * i + t
                    act.wait_ge(a["proj_ready"], unit + 1)
                    nc.scalar.copy(query[:, unit, 0:SEQ], bank[unit % 2][:, :]).then_inc(a[f"proj_free{unit % 2}"], 1)
                nc.scalar.copy(query[:, 4 * i:4 * i + 4, SEQ:T_ALL],
                               bank[2][:, 0:32].rearrange("p (c b) -> p c b", c=4)).then_inc(a["small_free"], 1)
                if i:
                    keep_scores(i - 1)
            keep_scores(3)

            def gate_exp(n):
                r = rows_of(n)
                act.wait_ge(a["gate_max"], n + 1)
                nc.scalar.activation(gate[n % 2][0:r], gate[n % 2][0:r], ACT.Exp).then_inc(a["gate_exp"], 1)

            def ple_start(n):
                r = rows_of(n)
                act.wait_ge(a["acc_kept"], n + 1)
                nc.scalar.activation(row_tmp[0:r], x[0:r, n], ACT.Square, accum_out=stat[0:r, 24:25]).then_inc(
                    a["ple_square"], 1)
                act.wait_ge(a["ple_inverse"], n + 1)
                nc.scalar.activation(stat[0:r, 26:27], stat[0:r, 25:26], ACT.Sqrt).then_inc(a["ple_root"], 1)

            def ple_end(n):
                r = rows_of(n)
                for j in range(2):
                    act.wait_ge(a["ple_gate"], 2 * n + j + 1)
                    nc.scalar.activation(row_tmp[0:r, 512 * j:512 * j + 512], bank[5 + j][0:r, :], ACT.Tanh,
                                         scale=0.5).then_inc(a["ple_gated"], 1)
                act.wait_ge(a["ple_used"], 2 * n + 2)
                nc.scalar.activation(row_tmp[0:r], x[0:r, n], ACT.Square, accum_out=stat[0:r, 28:29]).then_inc(
                    a["end_square"], 1)
                act.wait_ge(a["end_inverse"], n + 1)
                nc.scalar.activation(stat[0:r, 30:31], stat[0:r, 29:30], ACT.Sqrt).then_inc(a["end_root"], 1)

            def gelu(n, hd):
                act.wait_ge(a["dots_ready"], hd.times(1, 8 * n + 1))
                nc.scalar.activation(acts, dots, ACT.Gelu_apprx_tanh).then_inc(a["acts_ready"], 1)

            def diagonals(n, hd, some):
                act.wait_ge(a["coef_ready"], hd.times(1, 8 * n + 1))
                for i in some:
                    act.wait_ge(a["v_used"], hd.times(N_MAIN, 8 * N_MAIN * n + i + 1))
                    k = V_MAIN[i]
                    nc.scalar.mul(diag[i % V_BUFS], ident, coef[:, k:k + 1]).then_inc(a["diag_ready"], 1)

            gate_exp(0)
            for n in range(4):
                if n:
                    ple_start(n - 1)
                gelu(n, Head(0))
                diagonals(n, Head(0), range(V_BUFS))
                if n:
                    ple_end(n - 1)
                diagonals(n, Head(0), range(V_BUFS, N_MAIN))
                with act.Fori(1, 8) as reg:
                    gelu(n, Head(0, reg))
                    diagonals(n, Head(0, reg), range(N_MAIN))
                gate_exp(n + 1)
            ple_start(3)
            ple_end(3)
            act.wait_ge(a["s_turned"], 1)
            nc.scalar.copy(gate_s, bank[3][:, 8:16]).then_inc(a["s_kept"], 1)
            act.wait_ge(a["dots_ready"], 33)
            nc.scalar.activation(acts[:, 0:8], dots[:, 0:8], ACT.Gelu_apprx_tanh).then_inc(a["acts_ready"], 1)
            ple_start(4)
            ple_end(4)

        @block.vector
        def _(dve):
            link = lambda i: sh.dve(dve, i)
            link(nc.vector.memset(stat, 1.0))
            dve.sem_inc(a["squares"], 1)
            dve.sem_inc(a["dot_done"], U_BUFS)
            dve.sem_inc(a["v_used"], V_BUFS)
            dve.sem_inc(a["v_added"], V_SIDE_BUFS)
            dve.sem_inc(a["acts_ready"], 1)
            dve.sem_inc(a["diag_ready"], 1)
            nc.vector.memset(coef_s, 0.0)
            dve.wait_ge(a["squares"], 1 + N_T)
            link(nc.vector.tensor_scalar(stat[:, 0:5], stat[:, 0:5], 1.0 / D_MODEL, EPS, ALU.mult, ALU.add))
            nc.vector.reciprocal(stat[:, 8:13], stat[:, 0:5]).then_inc(a["inverse"], 1)
            dve.wait_ge(a["roots"], 1)
            dve.wait_ge(a["rows_in"], 16)
            for n in range(N_T):
                r = rows_of(n)
                nc.vector.scalar_tensor_tensor(hx[0:r, n], x[0:r, n], stat[0:r, 16 + n:17 + n], norm_rows[0:r, 0],
                                               ALU.mult, ALU.mult).then_inc(a["scaled"], 1)

            def top(n, hd, chain):
                r = rows_of(n)
                link = lambda i: chain(dve, i)
                src = sample_scores if n == 4 else query[:, :, P * n:P * n + P]
                link(nc.vector.tensor_copy(stage[0:r, 0], src[0:r, bass.ds(hd.times(2), 2)]))
                for lo in (0, 8):
                    src = stage[0:r, 0 if lo == 0 else 1]
                    for w in range(2):
                        last = nc.vector.max(val[0:r, w, lo:lo + 8], src[:, w])
                    link(last)
                    for w in range(2):
                        last = nc.vector.max_index(pos[0:r, w, lo:lo + 8], val[0:r, w, lo:lo + 8], src[:, w])
                    if lo == 0:
                        for w in range(2):
                            last = nc.vector.match_replace(stage[0:r, 1, w], val[0:r, w, 0:8], src[:, w], NEG)
                    link(last)
                link(nc.vector.tensor_tensor(cand[0:r], val[0:r, 0].unsqueeze(2).to_broadcast([r, 16, 16]),
                                             val[0:r, 1].unsqueeze(1).to_broadcast([r, 16, 16]), ALU.add))
                flat = cand[0:r].rearrange("p a b -> p (a b)")
                link(nc.vector.max(best[0:r, 0:8], flat))
                nc.vector.max_index(best_at[0:r, 0:8], best[0:r, 0:8], flat)
                link(nc.vector.match_replace(cand_rest[0:r], best[0:r, 0:8], flat, NEG))
                link(nc.vector.max(best[0:r, 8:16], cand_rest[0:r]))
                link(nc.vector.max_index(best_at[0:r, 8:16], best[0:r, 8:16], cand_rest[0:r]))
                nc.vector.tensor_copy(all_pos[0:r, bass.ds(hd.times(1), 1)].rearrange("p h w k -> p (h w k)"),
                                      pos[0:r].rearrange("p w k -> p (w k)"))
                nc.vector.tensor_copy(all_best[0:r, bass.ds(hd.times(1), 1)].rearrange("p h k -> p (h k)"), best[0:r])
                link(nc.vector.tensor_copy(all_at[0:r, bass.ds(hd.times(16), 16)], best_at[0:r]))

            N_LINKS = 11

            def decode(n):
                r = rows_of(n)
                dve.sem_inc(a["top_done"], 1)
                if n >= 2:
                    dve.wait_ge(a["coef_ready"], 8 * (n - 1))
                    dve.wait_ge(a["v_staged"], 8 * (n - 1))
                g = gate[n % 2][0:r].rearrange("p (h k) -> p h k", h=8)
                nc.vector.tensor_tensor(g, all_best[0:r], all_best[0:r, :, 0:1].to_broadcast([r, 8, 16]),
                                        ALU.subtract).then_inc(a["gate_max"], 1)
                for w in range(2):
                    if w == 0:
                        link(nc.vector.tensor_scalar(digit_u[0:r], all_at[0:r], 4, None, ALU.logical_shift_right))
                    else:
                        link(nc.vector.tensor_scalar(digit_u[0:r], all_at[0:r], 15, None, ALU.bitwise_and))
                    link(nc.vector.tensor_copy(digit[0:r], digit_u[0:r]))
                    hot = one_hot[0:r].rearrange("p h k a -> p (h k) a")
                    link(nc.vector.tensor_tensor(hot, digit[0:r].unsqueeze(2).to_broadcast([r, 128, 16]),
                                                 m.c(C_IOTA, 16, r).unsqueeze(1).to_broadcast([r, 128, 16]),
                                                 ALU.is_equal))
                    link(nc.vector.tensor_tensor(one_hot[0:r], one_hot[0:r],
                                                 all_pos[0:r, :, w].unsqueeze(2).to_broadcast([r, 8, 16, 16]), ALU.mult))
                    link(nc.vector.tensor_reduce(picked[w][0:r], hot, X_AXIS, ALU.add))
                link(nc.vector.scalar_tensor_tensor(index_f[0:r], picked[0][0:r], float(N_KEYS), picked[1][0:r],
                                                    ALU.mult, ALU.add))
                nc.vector.tensor_copy(index[n % 2][0:r], index_f[0:r]).then_inc(a["index_ready"], 1)
                dve.wait_ge(a["index_ready"], n + 1)

            def gates(n):
                r = rows_of(n)
                g = gate[n % 2][0:r].rearrange("p (h k) -> p h k", h=8)
                dve.wait_ge(a["gate_exp"], n + 1)
                link(nc.vector.tensor_reduce(stat[0:r, 32:40], g, X_AXIS, ALU.add))
                link(nc.vector.reciprocal(stat[0:r, 32:40], stat[0:r, 32:40]))
                link(nc.vector.tensor_tensor(g, g, stat[0:r, 32:40].unsqueeze(2).to_broadcast([r, 8, 16]), ALU.mult))

            def ple_start(n):
                r = rows_of(n)
                xs = x[0:r, n]
                dve.wait_ge(a["acc_done"], n + 1)
                if n < 4:
                    dve.wait_ge(a["v_added"], 8 * N_SIDE * (n + 1) + V_SIDE_BUFS)
                for j in range(2):
                    xj = xs[:, 512 * j:512 * j + 512]
                    last = nc.vector.tensor_tensor(xj, xj, acc[n % 2][j][0:r, :], ALU.add)
                last.then_inc(a["acc_kept"], 1)
                dve.wait_ge(a["ple_square"], n + 1)
                link(nc.vector.tensor_scalar(stat[0:r, 24:25], stat[0:r, 24:25], 1.0 / D_MODEL, EPS, ALU.mult, ALU.add))
                nc.vector.reciprocal(stat[0:r, 25:26], stat[0:r, 24:25]).then_inc(a["ple_inverse"], 1)
                dve.wait_ge(a["ple_root"], n + 1)
                nc.vector.tensor_scalar(row_tmp[0:r], xs, stat[0:r, 26:27], None, ALU.mult).then_inc(a["ple_scaled"], 1)
                for half in range(2):
                    dve.wait_ge(a["ple_turned"], 2 * n + half + 1)
                    nc.vector.tensor_tensor(ple_x[:, 4 * half:4 * half + 4, 0:r],
                                            bank[3 + half][:, :].rearrange("p (c t) -> p c t", c=4)[:, :, 0:r],
                                            m.norm_ple[:, 4 * half:4 * half + 4].unsqueeze(2).to_broadcast([P, 4, r]),
                                            ALU.mult).then_inc(a["ple_columns"], 1)

            def ple_end(n):
                r = rows_of(n)
                xs = x[0:r, n]
                for j in range(2):
                    dve.wait_ge(a["ple_gated"], 2 * n + j + 1)
                    dve.wait_ge(a["ple_proj"], 2 * n + j + 1)
                    t = row_tmp[0:r, 512 * j:512 * j + 512]
                    link(nc.vector.scalar_tensor_tensor(t, t, 1.0, bank[3 + j][0:r, :], ALU.add, ALU.mult))
                    xj = xs[:, 512 * j:512 * j + 512]
                    nc.vector.scalar_tensor_tensor(xj, t, 0.5, xj, ALU.mult, ALU.add).then_inc(a["ple_used"], 1)
                dve.wait_ge(a["end_square"], n + 1)
                link(nc.vector.tensor_scalar(stat[0:r, 28:29], stat[0:r, 28:29], 1.0 / D_MODEL, EPS, ALU.mult, ALU.add))
                nc.vector.reciprocal(stat[0:r, 29:30], stat[0:r, 28:29]).then_inc(a["end_inverse"], 1)
                dve.wait_ge(a["end_root"], n + 1)
                nc.vector.scalar_tensor_tensor(xs, xs, stat[0:r, 30:31], norm_rows[0:r, 1], ALU.mult,
                                               ALU.mult).then_inc(a["end_rows"], 1)

            def keep_links(n, hd):
                return LoopChain(a["top_step"], hd, N_LINKS, a["top_passed"], 8 * N_LINKS * n)

            def best_of(n, hd):
                chain = keep_links(n, hd)
                top(n, hd, chain)
                chain.close()

            def dot(n, hd, k):
                dve.wait_ge(u_in[k % U_BUFS], hd.times(32, 16 * (16 * n + k // U_BUFS + 1)))
                u = u_buf[k % U_BUFS]
                nc.vector.tensor_tensor_reduce(u, u, hx[:, n], 1.0, 0.0, ALU.mult, ALU.add,
                                               dots[:, k:k + 1]).then_inc(a["dot_done"], 1)

            def add_side(n, hd, i):
                per = N_SIDE // V_SIDE_BUFS
                b = V_BUFS + i % V_SIDE_BUFS
                dve.wait_ge(v_in[b], hd.times(16 * per, 16 * (8 * per * n + i // V_SIDE_BUFS + 1)))
                dve.wait_ge(a["v_added"], hd.times(N_SIDE, 8 * N_SIDE * n + V_SIDE_BUFS + i))
                k = V_SIDE[i]
                nc.vector.scalar_tensor_tensor(x[:, n], v_buf[b], coef[:, k:k + 1], x[:, n], ALU.mult,
                                               ALU.add).then_inc(a["v_added"], 1)

            def dots_and_sums(n, hd, before):
                dve.wait_ge(a["acts_ready"], hd.times(1, 8 * n + 1))
                for k in range(TOPK):
                    dot(n, hd, k)
                    if k in V_SIDE and before is not None:
                        add_side(*before, V_SIDE.index(k))
                dve.wait_ge(a["dot_done"], hd.times(16, 128 * n + 16 + U_BUFS))
                dve.sem_inc(a["dots_ready"], 1)

            def coefficients(n, hd):
                dve.wait_ge(a["acts_ready"], hd.times(1, 8 * n + 2))
                dve.wait_ge(a["diag_ready"], hd.times(N_MAIN, 8 * N_MAIN * n + 1))
                dve.wait_ge(a["v_added"], hd.times(N_SIDE, 8 * N_SIDE * n + V_SIDE_BUFS))
                nc.vector.tensor_tensor(coef, acts, gate[n % 2][:, bass.ds(hd.times(16), 16)], ALU.mult).then_inc(
                    a["coef_ready"], 1)
                dve.wait_ge(a["coef_ready"], hd.times(1, 8 * n + 1))

            for i in range(4):
                dve.wait_ge(a["score_kept"], N_T * i + 1)
                with dve.Fori(2 * i, 2 * i + 2) as reg:
                    best_of(0, Head(0, reg))
            dve.wait_ge(a["score_kept"], 4 * N_T)
            decode(0)
            for n in range(4):
                dots_and_sums(n, Head(0), (n - 1, Head(7)) if n else None)
                if n:
                    ple_start(n - 1)
                gates(n)
                coefficients(n, Head(0))
                best_of(n + 1, Head(0))
                if n:
                    ple_end(n - 1)
                with dve.Fori(1, 8) as reg:
                    dots_and_sums(n, Head(0, reg), (n, Head(-1, reg)))
                    coefficients(n, Head(0, reg))
                    best_of(n + 1, Head(0, reg))
                decode(n + 1)
            for i in range(N_SIDE):
                add_side(3, Head(7), i)
            ple_start(3)
            gates(4)
            ple_end(3)
            dve.wait_ge(a["top_passed"], 40 * N_LINKS)
            dve.wait_ge(a["s_turned"], 1)
            nc.vector.tensor_copy(index_s, bank[4][:, 0:8]).then_inc(a["s_kept"], 1)
            for b in range(N_S):
                dve.wait_ge(a["s_wide"], b + 1)
                dve.wait_ge(u_in[b], 16 * (64 + 1))
                for j in range(2):
                    u = u_buf[b][:, 512 * j:512 * j + 512]
                    last = nc.vector.tensor_tensor_reduce(u, u, bank[5 + j][:, :], 1.0, 0.0, ALU.mult, ALU.add,
                                                          dots_s[:, b, j:j + 1])
                last.then_inc(a["s_read"], 1)
            dve.wait_ge(a["s_read"], N_S)
            nc.vector.tensor_tensor(dots[:, 0:8], dots_s[:, :, 0], dots_s[:, :, 1], ALU.add).then_inc(
                a["dots_ready"], 1)
            dve.wait_ge(a["acts_ready"], 34)
            dve.wait_ge(a["s_kept"], 2)
            nc.vector.tensor_tensor(coef_s.rearrange("p b c -> p (b c)")[:, 0:64:9], acts[:, 0:8], gate_s,
                                    ALU.mult).then_inc(a["coef_ready"], 1)
            ple_start(4)
            ple_end(4)

        @block.tensor
        def _(pe):
            for n in range(N_T):
                r = rows_of(n)
                pe.wait_ge(a["scaled"], n + 1)
                for half in range(2):
                    if n:
                        pe.wait_ge(a["columns"], 2 * n + half - 1)
                    for j in range(4):
                        at = P * (4 * half + j)
                        last = nc.tensor.transpose(bank[5 + half][:, P * j:P * j + r], hx[0:r, n, at:at + P],
                                                   ident[0:r, 0:r])
                    last.then_inc(a["turned"], 1)
            pe.wait_ge(a["columns"], 2 * N_T)
            def score(i):
                pe.wait_ge(a["small_free"], i + 1)
                pe.wait_ge(a["proj_free0"], 2 * i + 2)
                pe.wait_ge(a["proj_free1"], 2 * i + 2)
                if i == 0:
                    pe.wait_ge(a["small_in"], 48)
                for n in range(N_T):
                    r = rows_of(n)
                    unit = N_T * i + n
                    if unit >= 4:
                        pe.wait_ge(a["score_kept"], unit - 3)
                    for j in range(4):
                        last = nc.tensor.matmul(bank[3 + unit % 4][0:r, P * j:P * j + P],
                                                query[:, 4 * i + j, P * n:P * n + r], keys[:, 4 * i + j],
                                                start=True, stop=True)
                    last.then_inc(a["score_ready"], 1)

            for i in range(4):
                b = B_PQ + i
                w = m.slot[b % 2]
                pe.wait_ge(s[f"ring_in{b % 2}"], 16 * (b // 2 + 1))
                if i:
                    pe.wait_ge(a["small_free"], i)
                for t in range(4):
                    unit = 4 * i + t
                    if unit >= 2:
                        pe.wait_ge(a[f"proj_free{unit % 2}"], unit // 2)
                    for k in range(8):
                        cols = w[:, 512 * k + P * t:512 * k + P * t + P]
                        nc.tensor.matmul(bank[unit % 2][:, :], cols, m.hT[:, k, 0:SEQ], start=(k == 0), stop=(k == 7))
                        last = nc.tensor.matmul(bank[2][:, 8 * t:8 * t + 8], cols, m.hT[:, k, SEQ:T_ALL],
                                                start=(k == 0), stop=(k == 7))
                    last.then_inc(a["proj_ready"], 1)
                if i:
                    score(i - 1)
            score(3)
            pe.wait_ge(a["score_kept"], 4 * N_T)

            def ple(n):
                r = rows_of(n)
                if n == 0:
                    pe.wait_ge(a["w_gate_in"], 64)
                pe.wait_ge(a["ple_scaled"], n + 1)
                if n == 4:
                    pe.wait_ge(a["s_kept"], 2)
                    pe.wait_ge(a["s_read"], N_S)
                for half in range(2):
                    for j in range(4):
                        at = P * (4 * half + j)
                        last = nc.tensor.transpose(bank[3 + half][:, P * j:P * j + r], row_tmp[0:r, at:at + P],
                                                   ident[0:r, 0:r])
                    last.then_inc(a["ple_turned"], 1)
                pe.wait_ge(a["ple_columns"], 2 * n + 2)
                for j in range(2):
                    for k in range(8):
                        last = nc.tensor.matmul(bank[5 + j][0:r, :], ple_x[:, k, 0:r], w_gate(k, j), start=(k == 0),
                                                stop=(k == 7))
                    last.then_inc(a["ple_gate"], 1)
                for j in range(2):
                    for k in range(2):
                        last = nc.tensor.matmul(bank[3 + j][0:r, :], p_cols[:, k, P * n:P * n + r],
                                                w_proj[:, k, 512 * j:512 * j + 512], start=(k == 0), stop=(k == 1))
                    last.then_inc(a["ple_proj"], 1)

            def sum_rows(n, hd, first):
                for i in range(N_MAIN):
                    per = N_MAIN // V_BUFS
                    b = i % V_BUFS
                    pe.wait_ge(v_in[b], hd.times(16 * per, 16 * (8 * per * n + i // V_BUFS + 1)))
                    pe.wait_ge(a["diag_ready"], hd.times(N_MAIN, 8 * N_MAIN * n + i + 2))
                    for j in range(2):
                        last = nc.tensor.matmul(acc[n % 2][j][:, :], diag[b], v_buf[b][:, 512 * j:512 * j + 512],
                                                start=first and i == 0, stop=False, skip_group_check=True)
                    last.then_inc(a["v_used"], 1)

            for n in range(4):
                if n >= 2:
                    pe.wait_ge(a["acc_kept"], n - 1)
                sum_rows(n, Head(0), True)
                with pe.Fori(1, 8) as reg:
                    sum_rows(n, Head(0, reg), False)
                pe.wait_ge(a["v_used"], 8 * N_MAIN * (n + 1) + V_BUFS)
                pe.sem_inc(a["acc_done"], 1)
                if n:
                    pe.wait_ge(a["ple_used"], 2 * n)
                ple(n)
            pe.wait_ge(a["ple_used"], 8)
            pe.wait_ge(a["index_ready"], N_T)
            nc.tensor.transpose(bank[4][:, 0:8], index_f[0:8], ident[0:8, 0:8])
            nc.tensor.transpose(bank[3][:, 8:16], gate[0][0:8], ident[0:8, 0:8]).then_inc(a["s_turned"], 1)
            pe.wait_ge(a["acc_kept"], 3)
            for b in range(N_S):
                if b:
                    pe.wait_ge(a["s_read"], b)
                for j in range(2):
                    last = nc.tensor.matmul(bank[5 + j][:, :], m.c(C_SEL + P * b, P, 8), hx[0:8, 4, 512 * j:512 * j + 512],
                                            start=True, stop=True)
                last.then_inc(a["s_wide"], 1)
            pe.wait_ge(a["coef_ready"], 33)
            for b in range(N_S):
                pe.wait_ge(v_in[b % V_BUFS], 16 * (32 * N_MAIN // V_BUFS + b // V_BUFS + 1))
                for j in range(2):
                    last = nc.tensor.matmul(acc[0][j][0:8, :], coef_s[:, b], v_buf[b % V_BUFS][:, 512 * j:512 * j + 512],
                                            start=b == 0, stop=False, skip_group_check=True)
                last.then_inc(a["v_used"], 1)
            pe.wait_ge(a["v_used"], 32 * N_MAIN + N_S + V_BUFS)
            pe.sem_inc(a["acc_done"], 1)
            ple(4)


def kernel(**inputs):
    import numpy as np
    import concourse.bacc as bacc
    from concourse import mybir as _mybir
    from concourse.bass_utils import run_bass_kernel_spmd as run

    a = {k: np.asarray(v) for k, v in inputs.items()}

    def chunks(w):
        return np.ascontiguousarray(w.reshape(w.shape[0] // P, P, w.shape[1]).transpose(1, 0, 2))

    def column(v):
        return np.ascontiguousarray(v.reshape(-1, P).T)

    w_in = chunks(a["w_in"][0])
    q0, k0, v0 = 0, Q_COLS, 2 * Q_COLS
    z0 = 3 * Q_COLS
    x0 = z0 + D_INNER
    b0 = x0 + D_INNER
    c0 = b0 + SSD_GROUPS * D_STATE
    dt0 = x0 + CONV_CH
    gate0 = dt0 + SSD_HEADS
    blocks = []
    for g in range(3):
        for base in (q0, k0, v0):
            blocks.append(w_in[:, :, base + g * ATT_W:base + (g + 1) * ATT_W])
    for g in range(SSD_GROUPS):
        blocks.append(np.concatenate([w_in[:, :, x0 + 256 * g:x0 + 256 * (g + 1)],
                                      w_in[:, :, b0 + 128 * g:b0 + 128 * (g + 1)],
                                      w_in[:, :, c0 + 128 * g:c0 + 128 * (g + 1)]], axis=2))
        if g in (2, 4, 6, 7):
            j = (g - 1) // 2
            blocks.append(w_in[:, :, z0 + 512 * j:z0 + 512 * (j + 1)])
    for j in range(4):
        blocks.append(w_in[:, :, gate0 + 512 * j:gate0 + 512 * (j + 1)])
    blocks.append(chunks(a["w_att_out"][0]))
    w_ssd = chunks(a["w_ssd_out"][0])
    for j in range(4):
        blocks.append(w_ssd[:, :, 256 * j:256 * (j + 1)])
    w_out = chunks(a["w_out"][0])
    blocks += [w_out[:, :, 512 * j:512 * (j + 1)] for j in range(2)]
    w_pq = chunks(a["w_peer_q"][0])
    blocks += [w_pq[:, :, 512 * j:512 * (j + 1)] for j in range(4)]
    w_pg = chunks(a["w_ple_gate"][0])
    blocks += [w_pg[:, :, 512 * j:512 * (j + 1)] for j in range(2)]
    stream = np.stack([b.reshape(P, 4096) for b in blocks])
    assert stream.shape[0] == N_BLOCKS

    tile_order = [t for g in range(SSD_GROUPS) for t in (2 * g, 2 * g + 1, 16 + g, 24 + g)]
    conv_w = a["conv_w"][0].reshape(CONV_W, 32, P).transpose(2, 1, 0)[:, tile_order]
    conv_b = column(a["conv_b"][0])[:, tile_order]
    state_conv = a["state_conv"][0].reshape(N_S, 3, 32, P).transpose(3, 2, 0, 1)[:, tile_order]
    keys = np.stack([a["peer_keys1"][0], a["peer_keys2"][0]], axis=1)
    keys = keys.transpose(3, 0, 1, 2).reshape(P, 2048)
    p_all = np.concatenate([a["p_prompt"][0, 0], a["p_sample"][0, :, 0]], axis=0)
    cols = np.concatenate([column(a["norm_mix"][0]), column(a["norm_ffn"][0]), column(a["norm_ple"][0]),
                           column(a["ssd_norm"][0]), conv_w.reshape(P, 128), conv_b], axis=1)
    head_rows = np.concatenate([a["dt_bias"][0], a["a_log"][0], a["d_skip"][0]]).reshape(1, 96)
    head_cols = np.stack([a["dt_bias"][0], a["a_log"][0], a["d_skip"][0]], axis=1)
    arrays = {
        "x_prompt": a["x_prompt"][0], "x_sample": a["x_sample"][:, 0],
        "cache0": a["cache_kv_w128"][0].reshape(N_S, -1, 1024),
        "cache1": a["cache_kv_w512"][0].reshape(N_S, -1, 1024),
        "cache2": a["cache_kv_w2048"][0].reshape(N_S, -1, 1024),
        "state_conv": state_conv.reshape(P, 32 * 24),
        "state_ssm": a["state_ssm"][0].reshape(N_S, SSD_HEADS * 64, D_STATE),
        "stream": stream, "w_dt": w_in[:, :, dt0:dt0 + SSD_HEADS].reshape(P, 256),
        "w_ple_proj": chunks(a["w_ple_proj"][0]).reshape(P, 2048),
        "p_cols": chunks(p_all.T).reshape(P, 2 * T_ALL),
        "keys": keys, "cols": cols, "head_rows": head_rows, "head_cols": head_cols,
        "norm_rows": np.stack([a["norm_ffn"][0], a["norm_final"]]),
        "peer_u": a["peer_u"][0], "peer_v": a["peer_v"][0],
        "consts": shape_constants(), "rope_table": rope_table(),
    }
    outs = {
        "y_prompt": (SEQ, D_MODEL), "y_sample": (N_S, D_MODEL),
        "kv0": (128, 1024), "kv1": (SEQ, 1024), "kv2": (SEQ, 1024),
        "conv_prompt": (P, 96), "ssm_prompt": (SSD_HEADS * 64, D_STATE),
        "kvs0": (N_S, 1024), "kvs1": (N_S, 1024), "kvs2": (N_S, 1024),
        "conv_sample": (P, 32 * 24), "ssm_sample": (N_S, SSD_HEADS * 64, D_STATE),
    }
    nc = bacc.Bacc("TRN2", target_bir_lowering=False, num_devices=1)
    arrays = {"in_" + k: np.ascontiguousarray(v) for k, v in arrays.items()}
    ins = {k[3:]: nc.dram_tensor(k, v.shape, _mybir.dt.from_np(v.dtype), kind="ExternalInput").ap()
           for k, v in arrays.items()}
    out_aps = {k: nc.dram_tensor("out_" + k, s, F32, kind="ExternalOutput").ap() for k, s in outs.items()}
    hybrid_decoder_step(nc, ins, out_aps)
    r = run(nc, [arrays], core_ids=[0]).results[0]
    o = {k: r["out_" + k] for k in outs}

    inverse = np.argsort(tile_order)

    def conv_rows(x, n):
        x = x.reshape(P, 32, n, 3)[:, inverse]
        return np.ascontiguousarray(x.transpose(2, 3, 1, 0)).reshape(1, n, 3, CONV_CH)

    kv_shape = (2, 8, 64)
    return (o["y_prompt"].reshape(1, SEQ, D_MODEL), o["y_sample"].reshape(N_S, 1, D_MODEL),
            o["kv0"].reshape(1, 1, 128, *kv_shape), o["kv1"].reshape(1, 1, SEQ, *kv_shape),
            o["kv2"].reshape(1, 1, SEQ, *kv_shape),
            conv_rows(o["conv_prompt"], 1), o["ssm_prompt"].reshape(1, 1, SSD_HEADS, 64, D_STATE),
            o["kvs0"].reshape(1, N_S, 1, *kv_shape), o["kvs1"].reshape(1, N_S, 1, *kv_shape),
            o["kvs2"].reshape(1, N_S, 1, *kv_shape),
            conv_rows(o["conv_sample"], N_S), o["ssm_sample"].reshape(1, N_S, SSD_HEADS, 64, D_STATE))
```

```python
import math
from contextlib import ExitStack

import numpy as np
import concourse.bass as bass
from concourse import mybir

P = 128
D_MODEL, SEQ, N_S, PAST_LEN = 1024, 512, 8, 1024
T_ALL = SEQ + N_S
N_T = 5
ATT_W, Q_COLS = 512, 1536
D_INNER, SSD_HEADS, SSD_GROUPS, D_STATE, CONV_W = 2048, 32, 8, 128, 4
CONV_CH = D_INNER + 2 * SSD_GROUPS * D_STATE
N_KEYS, TOPK = 128, 16
EPS = 1e-6
SCALE = 0.125
NEG = -1.0e30
F32 = mybir.dt.float32
U32 = mybir.dt.uint32
ALU = mybir.AluOpType
ACT = mybir.ActivationFunctionType
X_AXIS = mybir.AxisListType.X
XY_AXIS = mybir.AxisListType.XY

B_QKV = 0
B_SSD = 9
B_GATE = 21
B_ATT = 25
B_YOUT = 26
B_OUT = 30
B_PQ = 32
B_PLE = 36
N_BLOCKS = 38

C_IDENT, C_TRI, C_ONES, C_CAUSAL, C_PREV, C_RES, C_EXPAND = 0, 128, 256, 384, 512, 640, 768
C_SEL, C_DELTA, C_IND, C_IOTA, N_CONST = 2816, 3840, 3904, 3912, 3928


def shape_constants():
    c = np.zeros((P, N_CONST), np.float32)
    row, col = np.arange(P)[:, None], np.arange(P)[None, :]
    c[:, C_IDENT:C_IDENT + P] = row == col
    c[:, C_TRI:C_TRI + P] = row <= col
    c[:, C_ONES:C_ONES + P] = 1.0
    c[:, C_CAUSAL:C_CAUSAL + P] = np.where(col <= row, 0.0, NEG)
    c[:, C_PREV:C_PREV + P] = np.where(col >= row, 0.0, NEG)
    c[:, C_RES:C_RES + P] = np.where((col <= row) & (col % 4 == row % 4), 0.0, NEG)
    for pair in range(16):
        c[:32, C_EXPAND + P * pair:C_EXPAND + P * (pair + 1)] = np.arange(32)[:, None] == 2 * pair + col // 64
    c[:8, C_SEL:C_SEL + 1024] = np.arange(8)[:, None] == np.arange(1024)[None, :] // P
    c[:8, C_DELTA:C_DELTA + 64] = np.arange(8)[:, None] == np.arange(64)[None, :] // 8
    c[:64, C_IND:C_IND + 8] = np.arange(64)[:, None] // 8 == np.arange(8)[None, :]
    c[:, C_IOTA:C_IOTA + 16] = np.arange(16)[None, :]
    return c


def tile_positions(g, s):
    i = np.arange(P)
    return P * s + i if g == 0 else 4 * i + s


def rope_table():
    half = 32
    inv = np.exp(np.arange(half, dtype=np.float32) * np.float32(-2.0 * math.log(10000.0) / 64)).astype(np.float32)
    t = np.zeros((P, 13, 128), np.float32)
    for n in range(13):
        pos = tile_positions(n // 4, n % 4) if n < 12 else np.full(P, PAST_LEN)
        ang = (pos.astype(np.float32)[:, None] * inv[None, :]).astype(np.float32)
        cos, sin = np.cos(ang), np.sin(ang)
        t[:, n] = np.concatenate([cos, cos, -sin, sin], axis=1)
    return t.reshape(P, 13 * 128)


def rows_of(n):
    return P if n < 4 else N_S


def stage_semaphores(nc, stack, prefix, names):
    sems = {n: nc.alloc_semaphore(prefix + n) for n in names}

    def release():
        nc.clear_and_free_semaphores(list(sems.values()))
        nc.all_engine_barrier()

    stack.callback(release)
    return sems


HALF = T_ALL // 2


def half_of(half):
    return slice(HALF * half, HALF * half + HALF)


def uses_of_bank(b, n):
    return (n + 2 - b) // 3


class Chain:

    def __init__(self, sem):
        self.sem, self.count = sem, 0

    def __call__(self, eng, ins):
        self.count += 1
        ins.then_inc(self.sem, 1)
        eng.wait_ge(self.sem, self.count)


def hybrid_decoder_step(nc, ins, outs):
    ctx = ExitStack()
    with ctx:
        sem = lambda name: ctx.enter_context(nc.semaphore(name))
        mem = ctx.enter_context(nc.sbuf_tensor("mem", [P, 53200], F32))
        bank = [ctx.enter_context(nc.psum_tensor(f"bank{i}", [P, 512], F32)) for i in range(8)]
        head_out = nc.dram_tensor("head_out", [3, SEQ, 528], F32, kind="Internal").ap()
        m = Memory(mem)
        s = {}
        for name in SEMS:
            s[name] = sem(name)
        shared = Shared(nc, ins, outs, m, bank, s, head_out)
        attention_prompt(shared)
        attention_sample(shared)
        ssd_branch(shared)
        merge_branches(shared)
        peer_and_ple(shared)


SEMS = ["consts_in", "x_in", "ring_in0", "ring_in1", "act_step", "dve_step",
        "proj_ready", "proj_free0", "proj_free1", "proj_free2"]


class Memory:

    def __init__(self, mem):
        self.mem = mem
        self.const = mem[:, 0:N_CONST]
        at = N_CONST
        self.cols = mem[:, at:at + 200]
        self.norm_mix, self.norm_ffn, self.norm_ple = (self.cols[:, 8 * i:8 * i + 8] for i in range(3))
        self.norm_ssd = self.cols[:, 24:40]
        self.conv_w = self.cols[:, 40:168].rearrange("p (c w) -> p c w", w=4)
        self.conv_b = self.cols[:, 168:200]
        at += 200
        self.head_rows = mem[:, at:at + 96]
        self.head_cols = mem[0:32, at + 96:at + 99]
        self.small = mem[:, at + 100:at + 228]
        at += 228
        assert at <= 4360
        self.hT = mem[:, 4360:8520].rearrange("p (c t) -> p c t", t=T_ALL)
        self.attT = mem[:, 8520:10600].rearrange("p (c t) -> p c t", t=T_ALL)
        self.slot = [mem[:, 10600 + 4096 * i:10600 + 4096 * (i + 1)] for i in range(2)]
        self.phase = 18792
        self.end = 53200
        self.q_s = mem[0:8, 48592:50128].rearrange("p (g n) -> p g n", g=3)
        self.kv_s = mem[0:8, 50128:53200].rearrange("p (g n) -> p g n", g=3)

    def at(self, offset, n, parts=P):
        assert self.phase + offset + n <= self.end
        return self.mem[0:parts, self.phase + offset:self.phase + offset + n]

    def c(self, at, n=P, parts=P):
        return self.const[0:parts, at:at + n]


class Shared:
    def __init__(self, nc, ins, outs, m, bank, s, head_out):
        self.nc, self.ins, self.outs, self.m, self.bank, self.s = nc, ins, outs, m, bank, s
        self.head_out = head_out
        self.act = Chain(s["act_step"])
        self.dve = Chain(s["dve_step"])


def attention_prompt(sh):
    nc, ins, outs, m, bank, s = sh.nc, sh.ins, sh.outs, sh.m, sh.bank, sh.s
    ident = m.c(C_IDENT)
    x = m.at(0, 5120).rearrange("p (n d) -> p n d", n=N_T)
    xn = m.at(5120, 5120).rearrange("p (n d) -> p n d", n=N_T)
    q_buf = [m.at(2048 * i, 2048).rearrange("p (s n) -> p s n", s=4) for i in range(2)]
    kv_buf = [m.at(4096 + 4096 * i, 4096).rearrange("p (s n) -> p s n", s=4) for i in range(2)]
    qT = m.at(12288, 2048).rearrange("p (c t) -> p c t", c=4)
    kT = m.at(14336, 2048).rearrange("p (c t) -> p c t", c=4)
    score = [m.at(16384 + 1024 * i, 1024).rearrange("p (h w k) -> p h w k", h=4, w=2) for i in range(2)]
    probT = [m.at(18432 + 1024 * i, 1024).rearrange("p (w h q) -> p w h q", w=2, h=4) for i in range(2)]
    head_rows = m.at(20480, 2112).rearrange("p (s h c) -> p s h c", s=4, h=8)
    rope_a, rope_b = m.at(22592, 512), m.at(23104, 512)
    merge_in = [m.at(23616 + 1584 * i, 1584).rearrange("p (g h c) -> p g h c", g=3, h=8) for i in range(2)]
    rope = m.at(26784, 1664).rearrange("p (n c) -> p n c", n=13)
    neg_max = [m.at(28448 + 4 * i, 4) for i in range(2)]
    merge_max = m.at(28456, 8)
    merge_w = m.at(28464, 24).rearrange("p (g h) -> p g h", g=3)
    merge_den = m.at(28488, 24).rearrange("p (g h) -> p g h", g=3)
    merge_sum = m.at(28512, 8)
    stat = m.small

    turns = []
    for g in range(3):
        for t in range(4):
            turns += [("q", g, t), ("k", g, t)]
        for v in range(8):
            turns += [("p", g, v, w) for w in range(2 if g == 0 and v >= 2 else 1)]
    turns += [("att", n) for n in range(4)]
    turn_at = {k: i for i, k in enumerate(turns)}

    def token_columns(k, g, t):
        if t == 4:
            return m.hT[:, k, SEQ:T_ALL]
        if g == 0:
            return m.hT[:, k, P * t:P * t + P]
        return m.hT[:, k, t:SEQ:4]

    with ExitStack() as c:
        names = ("squares", "inverse", "roots", "scaled", "turned", "columns", "qk_rows", "v_rows", "kv_stored0", "kv_stored1", "kv_stored2",
                 "turn_ready", "turn_free", "score_ready", "score_free", "max_ready", "prob_ready", "out_ready",
                 "out_kept", "group_done", "head_stored", "merge_in0", "merge_in1", "merge_exp", "merge_max",
                 "merge_rows")

        def units_at(g, v):
            return range(2 * v, min(2 * v + 2, 15)) if g < 2 else ()

        a = stage_semaphores(nc, c, "a_", names)
        block = c.enter_context(nc.Block())

        @block.sync
        def _(sp):
            sp.dma_start(x[0:N_S, 4, :], ins["x_sample"]).then_inc(s["x_in"], 16)
            sp.dma_start(x[:, 0:4, :], ins["x_prompt"].rearrange("(n p) d -> p n d", p=P)).then_inc(s["x_in"], 16)
            for b in range(9):
                if b >= 2:
                    sp.wait_ge(s["proj_ready"], 5 * (b - 1))
                sp.dma_start(m.slot[b % 2], ins["stream"][b]).then_inc(s[f"ring_in{b % 2}"], 16)
            for b in (9, 10):
                sp.wait_ge(s["proj_ready"], 5 * (b - 1))
                sp.dma_start(m.slot[b % 2], ins["stream"][b]).then_inc(s[f"ring_in{b % 2}"], 16)

        @block.gpsimd
        def _(pool):
            def store_kv(g):
                pool.wait_ge(a["qk_rows"], 10 * (g + 1))
                pool.wait_ge(a["v_rows"], 5 * (g + 1))
                for t in range(4):
                    src = kv_buf[g % 2][:, t]
                    if g == 0:
                        if t == 3:
                            pool.dma_start(outs["kv0"], src).then_inc(a[f"kv_stored{g}"], 16)
                    else:
                        dst = outs[f"kv{g}"].rearrange("(i r) c -> r i c", r=4)[t]
                        pool.dma_start(dst, src).then_inc(a[f"kv_stored{g}"], 16)
                pool.dma_start(outs[f"kvs{g}"], m.kv_s[:, g]).then_inc(a[f"kv_stored{g}"], 16)

            def store_heads(g):
                for t in range(4):
                    pool.wait_ge(a["out_kept"], 8 * g + 2 * t + 2)
                    src = head_rows[:, t].rearrange("p h c -> p (h c)")
                    if g == 0:
                        pool.dma_start(sh.head_out[0, P * t:P * t + P], src).then_inc(a["head_stored"], 16)
                    else:
                        dst = sh.head_out[g].rearrange("(i r) c -> r i c", r=4)[t]
                        pool.dma_start(dst, src).then_inc(a["head_stored"], 16)

            store_kv(0)
            store_kv(1)
            store_heads(0)
            store_kv(2)
            store_heads(1)
            store_heads(2)
            pool.wait_ge(a["head_stored"], 16 * 12)
            for n in range(4):
                if n >= 2:
                    pool.wait_ge(a["merge_rows"], n - 1)
                src = sh.head_out[:, P * n:P * n + P, :].rearrange("g p c -> p g c")
                dst = merge_in[n % 2].rearrange("p g h c -> p g (h c)")
                pool.dma_start(dst, src).then_inc(a[f"merge_in{n % 2}"], 16)
            for g in range(3):
                pool.wait_ge(a[f"kv_stored{g}"], 16 * (5 if g else 2))

        @block.scalar
        def _(act):
            act.dma_start(m.const, ins["consts"]).then_inc(s["consts_in"], 16)
            act.dma_start(rope.rearrange("p n c -> p (n c)"), ins["rope_table"]).then_inc(s["consts_in"], 16)
            act.dma_start(m.cols, ins["cols"]).then_inc(s["consts_in"], 16)
            act.dma_start(m.head_rows, ins["head_rows"][0].partition_broadcast(P)).then_inc(s["consts_in"], 16)
            act.dma_start(m.head_cols, ins["head_cols"]).then_inc(s["consts_in"], 16)
            act.wait_ge(s["x_in"], 32)
            act.wait_ge(a["squares"], 1)
            for n in range(N_T):
                r = rows_of(n)
                nc.scalar.activation(xn[0:r, n], x[0:r, n], ACT.Square,
                                     accum_out=stat[0:r, n:n + 1]).then_inc(a["squares"], 1)
            act.wait_ge(a["inverse"], 1)
            nc.scalar.activation(stat[:, 16:21], stat[:, 8:13], ACT.Sqrt).then_inc(a["roots"], 1)

            def keep_v(g, units=range(10, 15)):
                for u in units:
                    if u < 10:
                        continue
                    t, unit = u - 10, 15 * g + u
                    act.wait_ge(s["proj_ready"], unit + 1)
                    if g == 2 and t == 0:
                        act.wait_ge(a["group_done"], 1)
                        act.wait_ge(a["kv_stored0"], 32)
                    dst = m.kv_s[:, g, 512:1024] if t == 4 else kv_buf[g % 2][:, t, 512:1024]
                    r = rows_of(t)
                    nc.scalar.copy(dst, bank[unit % 3][0:r, :]).then_inc(s[f"proj_free{unit % 3}"], 1)
                    act.wait_ge(s[f"proj_free{unit % 3}"], unit // 3 + 1)
                    act.sem_inc(a["v_rows"], 1)

            def turned(key, dst):
                i = turn_at[key]
                act.wait_ge(a["turn_ready"], i + 1)
                src = bank[5 + i % 2][:, :].rearrange("p (c t) -> p c t", c=4)
                nc.scalar.copy(dst, src).then_inc(a["turn_free"], 1)

            def exps(g, v):
                w = 2 if g == 0 and v >= 2 else 1
                act.wait_ge(a["max_ready"], 8 * g + v + 1)
                for hh in range(4):
                    last = nc.scalar.activation(
                        score[v % 2][:, hh, 0:w], score[v % 2][:, hh, 0:w], ACT.Exp, scale=SCALE,
                        bias=neg_max[v % 2][:, hh:hh + 1],
                        accum_out=head_rows[:, v // 2, 2 * hh + v % 2, 64:65])
                last.then_inc(a["prob_ready"], 1)

            def attend(g):
                for t in range(4):
                    turned(("q", g, t), qT[:, :, P * t:P * t + P])
                    turned(("k", g, t), kT[:, :, P * t:P * t + P])
                if g:
                    act.wait_ge(a["head_stored"], 64 * g)
                exps(g, 0)
                for v in range(8):
                    keep_v(g + 1, units_at(g, v))
                    if 8 * g + v >= 2:
                        act.wait_ge(a["out_ready"], 8 * g + v - 1)
                    for w in range(2 if g == 0 and v >= 2 else 1):
                        turned(("p", g, v, w), probT[v % 2][:, w])
                    if v < 7:
                        exps(g, v + 1)
                    act.wait_ge(a["out_ready"], 8 * g + v + 1)
                    nc.scalar.copy(head_rows[:, v // 2, v % 2:8:2, 0:64],
                                   bank[7][:, 0:256].rearrange("p (h c) -> p h c", h=4)).then_inc(a["out_kept"], 1)

            keep_v(0)
            attend(0)
            attend(1)
            attend(2)
            for n in range(4):
                act.wait_ge(a["merge_max"], n + 1)
                nc.scalar.activation(merge_w, merge_w, ACT.Exp, scale=SCALE).then_inc(a["merge_exp"], 1)
                turned(("att", n), m.attT[:, :, P * n:P * n + P])
            act.wait_ge(a["turn_free"], len(turns))

        @block.vector
        def _(dve):
            link = lambda i: sh.dve(dve, i)
            link(nc.vector.memset(stat[:, :], 1.0))
            dve.sem_inc(a["squares"], 1)
            dve.wait_ge(s["x_in"], 32)
            dve.wait_ge(a["squares"], 1 + N_T)
            link(nc.vector.tensor_scalar(stat[:, 0:5], stat[:, 0:5], 1.0 / D_MODEL, EPS, ALU.mult, ALU.add))
            nc.vector.reciprocal(stat[:, 8:13], stat[:, 0:5]).then_inc(a["inverse"], 1)
            dve.wait_ge(a["roots"], 1)
            for n in range(N_T):
                r = rows_of(n)
                nc.vector.tensor_scalar(xn[0:r, n], x[0:r, n], stat[0:r, 16 + n:17 + n], None,
                                        ALU.mult).then_inc(a["scaled"], 1)
            dve.wait_ge(s["consts_in"], 80)
            for n in range(N_T):
                r = rows_of(n)
                for half in range(2):
                    dve.wait_ge(a["turned"], 2 * n + half + 1)
                    src = bank[5 + half][:, :].rearrange("p (c t) -> p c t", c=4)[:, :, 0:r]
                    g = m.norm_mix[:, 4 * half:4 * half + 4].unsqueeze(2).to_broadcast([P, 4, r])
                    nc.vector.tensor_tensor(m.hT[:, 4 * half:4 * half + 4, P * n:P * n + r], src, g,
                                            ALU.mult).then_inc(a["columns"], 1)

            def rope_rows(g, units=range(10)):
                for u in units:
                    if u < 10:
                        j, t = divmod(u, 5)
                        unit = 15 * g + u
                        r = rows_of(t)
                        dve.wait_ge(s["proj_ready"], unit + 1)
                        if g == 2 and j == 0 and t == 0:
                            dve.wait_ge(a["group_done"], 1)
                            dve.wait_ge(a["kv_stored0"], 32)
                        tab = rope[0:r, 12 if t == 4 else 4 * g + t]
                        src = bank[unit % 3][0:r, :].rearrange("p (h c) -> p h c", h=8)
                        ra = rope_a[0:r].rearrange("p (h c) -> p h c", h=8)
                        rb = rope_b[0:r].rearrange("p (h c) -> p h c", h=8)
                        cos = tab[:, 0:64].unsqueeze(1).to_broadcast([r, 8, 64])
                        neg_sin = tab[:, 64:96].unsqueeze(1).to_broadcast([r, 8, 32])
                        sin = tab[:, 96:128].unsqueeze(1).to_broadcast([r, 8, 32])
                        nc.vector.tensor_tensor(ra, src, cos, ALU.mult)
                        nc.vector.tensor_tensor(rb[:, :, 0:32], src[:, :, 32:64], neg_sin, ALU.mult)
                        nc.vector.tensor_tensor(rb[:, :, 32:64], src[:, :, 0:32], sin,
                                                ALU.mult).then_inc(s[f"proj_free{unit % 3}"], 1)
                        dve.wait_ge(s[f"proj_free{unit % 3}"], unit // 3 + 1)
                        if t == 4:
                            dst = m.q_s[:, g] if j == 0 else m.kv_s[:, g, 0:512]
                        else:
                            dst = q_buf[g % 2][:, t] if j == 0 else kv_buf[g % 2][:, t, 0:512]
                        nc.vector.tensor_tensor(dst, rope_a[0:r], rope_b[0:r], ALU.add).then_inc(a["qk_rows"], 1)
                        dve.wait_ge(a["qk_rows"], 10 * g + 5 * j + t + 1)

            def maxima(g):
                for v in range(8):
                    if v >= 2:
                        rope_rows(g + 1, units_at(g, v - 2))
                    w = 2 if g == 0 and v >= 2 else 1
                    dve.wait_ge(a["score_ready"], 8 * g + v + 1)
                    if v >= 2:
                        dve.wait_ge(a["turn_ready"], turn_at[("p", g, v - 2, 1 if g == 0 and v >= 4 else 0)] + 1)
                    elif g:
                        dve.wait_ge(a["turn_ready"], turn_at[("p", g - 1, v + 6, 1 if g == 1 else 0)] + 1)
                    buf = score[v % 2]
                    mask = m.c(C_CAUSAL if g < 2 else C_RES)
                    srcs = [(3, mask), (4, m.c(C_PREV))][:w]
                    for i, (b, mk) in enumerate(srcs):
                        last = nc.vector.tensor_tensor(buf[:, :, i, :], bank[b][:, :].rearrange("p (h k) -> p h k", h=4),
                                                       mk.unsqueeze(1).to_broadcast([P, 4, P]), ALU.add)
                    last.then_inc(a["score_free"], 1)
                    dve.wait_ge(a["score_free"], 8 * g + v + 1)
                    top = head_rows[:, v // 2, v % 2:8:2, 65]
                    if g and v == 0:
                        dve.wait_ge(a["head_stored"], 64 * g)
                    link(nc.vector.tensor_reduce(top, buf[:, :, 0:w, :], XY_AXIS, ALU.max))
                    nc.vector.tensor_scalar(neg_max[v % 2], top, -SCALE, None, ALU.mult).then_inc(a["max_ready"], 1)
                for v in (6, 7):
                    rope_rows(g + 1, units_at(g, v))

            def merge(n):
                dve.wait_ge(a[f"merge_in{n % 2}"], 16 * (n // 2 + 1))
                rows = merge_in[n % 2]
                link(nc.vector.tensor_tensor(merge_max, rows[:, 0, :, 65], rows[:, 1, :, 65], ALU.max))
                link(nc.vector.tensor_tensor(merge_max, merge_max, rows[:, 2, :, 65], ALU.max))
                nc.vector.tensor_tensor(merge_w, rows[:, :, :, 65], merge_max.unsqueeze(1).to_broadcast([P, 3, 8]),
                                        ALU.subtract).then_inc(a["merge_max"], 1)
                dve.wait_ge(a["merge_exp"], n + 1)
                link(nc.vector.tensor_tensor(merge_den, merge_w, rows[:, :, :, 64], ALU.mult))
                link(nc.vector.tensor_reduce(merge_sum, merge_den.rearrange("p g h -> p h g"), X_AXIS, ALU.add))
                link(nc.vector.reciprocal(merge_sum, merge_sum))
                link(nc.vector.tensor_tensor(merge_w, merge_w, merge_sum.unsqueeze(1).to_broadcast([P, 3, 8]), ALU.mult))
                if n:
                    dve.wait_ge(a["turn_ready"], turn_at[("att", n - 1)] + 1)
                for g in range(3):
                    out = (rope_a, rope_b, rope_b)[g].rearrange("p (h c) -> p h c", h=8)
                    link(nc.vector.tensor_tensor(out, rows[:, g, :, 0:64],
                                                 merge_w[:, g].unsqueeze(2).to_broadcast([P, 8, 64]), ALU.mult))
                    if g == 1:
                        link(nc.vector.tensor_tensor(rope_a, rope_a, rope_b, ALU.add))
                nc.vector.tensor_tensor(rope_a, rope_a, rope_b, ALU.add).then_inc(a["merge_rows"], 1)

            rope_rows(0)
            maxima(0)
            maxima(1)
            maxima(2)
            for n in range(4):
                merge(n)

        @block.tensor
        def _(pe):
            pe.wait_ge(s["consts_in"], 80)
            for n in range(N_T):
                r = rows_of(n)
                pe.wait_ge(a["scaled"], n + 1)
                for half in range(2):
                    if n:
                        pe.wait_ge(a["columns"], 2 * n + half - 1)
                    for cc in range(4):
                        k = 4 * half + cc
                        last = nc.tensor.transpose(bank[5 + half][:, P * cc:P * cc + r], xn[0:r, n, P * k:P * k + P],
                                                   ident[0:r, 0:r])
                    last.then_inc(a["turned"], 1)
            pe.wait_ge(a["columns"], 2 * N_T)

            def project(g, units=range(15)):
                for u in units:
                    j, t = divmod(u, 5)
                    b = 3 * g + j
                    unit = 5 * b + t
                    if t == 0:
                        pe.wait_ge(s[f"ring_in{b % 2}"], 16 * (b // 2 + 1))
                    if unit >= 3:
                        pe.wait_ge(s[f"proj_free{unit % 3}"], unit // 3)
                    for k in range(8):
                        last = nc.tensor.matmul(bank[unit % 3][0:rows_of(t), :], token_columns(k, g, t),
                                                m.slot[b % 2][:, 512 * k:512 * k + 512],
                                                start=(k == 0), stop=(k == 7))
                    last.then_inc(s["proj_ready"], 1)

            def turn(key, srcs):
                i = turn_at[key]
                if i >= 2:
                    pe.wait_ge(a["turn_free"], i - 1)
                for cc in range(4):
                    last = nc.tensor.transpose(bank[5 + i % 2][:, P * cc:P * cc + P], srcs(cc), ident)
                last.then_inc(a["turn_ready"], 1)

            def scores(g, v):
                t, u = v // 2, v % 2
                if 8 * g + v:
                    pe.wait_ge(a["score_free"], 8 * g + v)
                for w in range(2 if g == 0 and t else 1):
                    for hh in range(4):
                        h = 2 * hh + u
                        lo = 64 * u
                        last = nc.tensor.matmul(bank[3 + w][:, P * hh:P * hh + P],
                                                qT[lo:lo + 64, h // 2, P * t:P * t + P],
                                                kT[lo:lo + 64, h // 2, P * (t - w):P * (t - w) + P],
                                                start=True, stop=True)
                last.then_inc(a["score_ready"], 1)

            def attend(g):
                pe.wait_ge(a["qk_rows"], 10 * g + 10)
                for t in range(4):
                    turn(("q", g, t), lambda cc: q_buf[g % 2][:, t, P * cc:P * cc + P])
                    turn(("k", g, t), lambda cc: kv_buf[g % 2][:, t, P * cc:P * cc + P])
                pe.wait_ge(a["turn_free"], turn_at[("k", g, 3)] + 1)
                pe.wait_ge(a["v_rows"], 5 * g + 5)
                scores(g, 0)
                for v in range(8):
                    t, u = v // 2, v % 2
                    wide = range(2 if g == 0 and t else 1)
                    if v < 7:
                        scores(g, v + 1)
                    project(g + 1, units_at(g, v))
                    pe.wait_ge(a["prob_ready"], 8 * g + v + 1)
                    for w in wide:
                        turn(("p", g, v, w), lambda cc: score[v % 2][:, cc, w, :])
                    pe.wait_ge(a["turn_free"], turn_at[("p", g, v, wide[-1])] + 1)
                    if 8 * g + v:
                        pe.wait_ge(a["out_kept"], 8 * g + v)
                    for hh in range(4):
                        h = 2 * hh + u
                        for w in wide:
                            last = nc.tensor.matmul(bank[7][:, 64 * hh:64 * hh + 64], probT[v % 2][:, w, hh],
                                                    kv_buf[g % 2][:, t - w, 512 + 64 * h:576 + 64 * h],
                                                    start=(w == 0), stop=(w == wide[-1]))
                    last.then_inc(a["out_ready"], 1)
                pe.wait_ge(a["out_ready"], 8 * g + 8)
                pe.sem_inc(a["group_done"], 1)

            project(0)
            attend(0)
            attend(1)
            attend(2)
            for n in range(4):
                pe.wait_ge(a["merge_rows"], n + 1)
                turn(("att", n), lambda cc: rope_a[:, P * cc:P * cc + P])


def attention_sample(sh):
    nc, ins, m, bank, s = sh.nc, sh.ins, sh.m, sh.bank, sh.s
    keys = (128, 128, 64)
    cache = m.at(0, 24576).rearrange("p (g b n) -> p g b n", g=3, b=N_S)
    product = [m.at(24576 + 512 * i, 512) for i in range(2)]
    by_key = m.at(25600, 192).rearrange("p (g r) -> p g r", g=3)
    score_rows = m.at(25792, 323, 64)
    prob_cols = m.at(26120, 192).rearrange("p (g r) -> p g r", g=3)
    new_diag = m.at(26312, 192, 64).rearrange("p (g r) -> p g r", g=3)
    new_cols = m.at(26504, 192, 8).rearrange("p (g r) -> p g r", g=3)
    new_score = m.at(26696, 24, 8).rearrange("p (g h) -> p g h", g=3)
    new_spread = m.at(26720, 192, 8).rearrange("p (g r) -> p g r", g=3)
    row_max, neg_max, row_sum, row_inv = (m.at(26912 + i, 1, 64) for i in range(4))
    new_prod = m.at(26920, 1536, 8).rearrange("p (g n) -> p g n", g=3)
    ident = m.c(C_IDENT)

    with ExitStack() as c:
        names = ("query_ready", "query_free", "key_cols", "new_ready", "rows_ready", "max_ready", "exps", "probs",
                 "cols_ready", "cols_kept", "diag_ready", "new_turned", "out_ready")
        a = stage_semaphores(nc, c, "b_", names)
        cache_in = list(stage_semaphores(nc, c, "b_cache_in", [str(i) for i in range(24)]).values())
        block = c.enter_context(nc.Block())

        def load(eng, b):
            for g in range(3):
                stride = (1, 4, 16)[g]
                eng.dma_start(cache[0:keys[g], g, b], ins[f"cache{g}"][b, 0::stride]).then_inc(
                    cache_in[8 * g + b], 16)

        @block.sync
        def _(sp):
            for b in range(N_S):
                load(sp, b)

        @block.scalar
        def _(act):
            act.wait_ge(a["max_ready"], 1)
            nc.scalar.activation(score_rows, score_rows, ACT.Exp, scale=SCALE, bias=neg_max,
                                 accum_out=row_sum).then_inc(a["exps"], 1)
            act.wait_ge(a["cols_ready"], 1)
            nc.scalar.copy(prob_cols[:, 0:2], bank[3][:, 0:128].rearrange("p (g r) -> p g r", g=2))
            nc.scalar.copy(prob_cols[0:64, 2], bank[3][0:64, 128:192]).then_inc(a["cols_kept"], 1)
            act.wait_ge(a["new_turned"], 1)
            nc.scalar.copy(new_cols, bank[4][0:8, 0:192].rearrange("p (g r) -> p g r", g=3)).then_inc(a["cols_kept"], 1)

        @block.vector
        def _(dve):
            link = lambda i: sh.dve(dve, i)
            link(nc.vector.tensor_tensor(new_prod, m.q_s, m.kv_s[:, :, 0:512], ALU.mult))
            link(nc.vector.tensor_reduce(new_score, new_prod.rearrange("p g (h c) -> p g h c", h=8), X_AXIS, ALU.add))
            for g in range(3):
                last = nc.vector.tensor_tensor(
                    new_spread[:, g].rearrange("p (b h) -> p b h", b=8),
                    m.c(C_DELTA, 64, 8).rearrange("p (b h) -> p b h", b=8),
                    new_score[:, g].unsqueeze(1).to_broadcast([8, 8, 8]), ALU.mult)
            last.then_inc(a["new_ready"], 1)
            i = 0
            for b in range(N_S):
                for g in range(3):
                    dve.wait_ge(cache_in[8 * g + b], 16)
                    dve.wait_ge(a["query_ready"], i + 1)
                    k = keys[g]
                    nc.vector.tensor_tensor(product[i % 2][0:k], cache[0:k, g, b, 0:512], bank[i % 2][0:k, :],
                                            ALU.mult).then_inc(a["query_free"], 1)
                    dve.wait_ge(a["query_free"], i + 1)
                    nc.vector.tensor_reduce(by_key[0:k, g, 8 * b:8 * b + 8],
                                            product[i % 2][0:k].rearrange("p (h c) -> p h c", h=8), X_AXIS,
                                            ALU.add).then_inc(a["key_cols"], 1)
                    i += 1
            dve.wait_ge(a["rows_ready"], 1)
            nc.vector.tensor_copy(score_rows[:, 0:320], bank[2][0:64, 0:320])
            link(nc.vector.tensor_copy(score_rows[:, 320:323], bank[2][0:64, 320:323]))
            link(nc.vector.tensor_reduce(row_max, score_rows, X_AXIS, ALU.max))
            nc.vector.tensor_scalar(neg_max, row_max, -SCALE, None, ALU.mult).then_inc(a["max_ready"], 1)
            dve.wait_ge(a["exps"], 1)
            link(nc.vector.reciprocal(row_inv, row_sum))
            nc.vector.tensor_scalar(score_rows, score_rows, row_inv, None, ALU.mult).then_inc(a["probs"], 1)
            dve.wait_ge(a["probs"], 1)
            for g in range(3):
                last = nc.vector.tensor_scalar(new_diag[:, g], m.c(C_IDENT, 64, 64), score_rows[:, 320 + g:321 + g],
                                               None, ALU.mult)
            last.then_inc(a["diag_ready"], 1)
            dve.wait_ge(a["out_ready"], 1)
            out = bank[5][:, 0:64].rearrange("p (b c w) -> p w c b", b=8, w=2)
            nc.vector.tensor_copy(m.attT[0:64, :, SEQ:T_ALL], out[0:64, 0])
            link(nc.vector.tensor_copy(m.attT[64:128, :, SEQ:T_ALL], out[64:128, 1]))

        @block.tensor
        def _(pe):
            i = 0
            for b in range(N_S):
                for g in range(3):
                    if i >= 2:
                        pe.wait_ge(a["query_free"], i - 1)
                    nc.tensor.matmul(bank[i % 2][:, :], m.c(C_SEL + P * b, P, 8), m.q_s[:, g],
                                     start=True, stop=True).then_inc(a["query_ready"], 1)
                    i += 1
            pe.wait_ge(a["key_cols"], 24)
            pe.wait_ge(a["new_ready"], 1)
            for g in range(3):
                k = keys[g]
                nc.tensor.transpose(bank[2][0:64, P * g:P * g + k], by_key[0:k, g], ident[0:k, 0:k])
            for g in range(3):
                last = nc.tensor.matmul(bank[2][0:64, 320 + g:321 + g], new_spread[:, g], m.c(C_ONES, 1, 8),
                                        start=True, stop=True)
            last.then_inc(a["rows_ready"], 1)
            pe.wait_ge(a["probs"], 1)
            for g in range(3):
                k = keys[g]
                last = nc.tensor.transpose(bank[3][0:k, 64 * g:64 * g + 64], score_rows[:, P * g:P * g + k],
                                           ident[0:64, 0:64])
            last.then_inc(a["cols_ready"], 1)
            pe.wait_ge(a["diag_ready"], 1)
            nc.tensor.matmul(bank[4][0:8, 0:192], m.c(C_IND, 8, 64), new_diag, start=True,
                             stop=True).then_inc(a["new_turned"], 1)
            pe.wait_ge(a["cols_kept"], 2)
            by_pair = lambda t, pair: t.rearrange("p (b h) -> p b h", b=8)[:, :, 2 * pair:2 * pair + 2]
            for pair in range(4):
                for g in range(3):
                    nc.tensor.matmul(by_pair(bank[5][:, 0:64], pair), m.kv_s[:, g, 512 + P * pair:640 + P * pair],
                                     by_pair(new_cols[:, g], pair), start=(g == 0), stop=False, skip_group_check=True)
            for b in range(N_S):
                for pair in range(4):
                    at = 8 * b + 2 * pair
                    for g in range(3):
                        k = keys[g]
                        last = nc.tensor.matmul(bank[5][:, at:at + 2], cache[0:k, g, b, 512 + P * pair:640 + P * pair],
                                                prob_cols[0:k, g, at:at + 2], start=False, stop=(g == 2),
                                                skip_group_check=True)
            last.then_inc(a["out_ready"], 1)


def ssd_branch(sh):
    nc, ins, outs, m, bank, s = sh.nc, sh.ins, sh.outs, sh.m, sh.bank, sh.s
    NCK, G = 4, SSD_GROUPS
    xpad = [m.at(2060 * i, 2060).rearrange("p (c t) -> p c t", c=4) for i in range(2)]
    xc = [m.at(4120 + 2080 * i, 2080).rearrange("p (c t) -> p c t", c=4) for i in range(2)]
    tanh = m.at(8280, 2080).rearrange("p (c t) -> p c t", c=4)
    update = m.at(8280, 2048).rearrange("p (c b n) -> p c b n", c=2, b=8)
    z_tanh = m.at(10360, 512)
    rows = [m.at(10872 + 1536 * i, 1536).rearrange("p (k c) -> p k c", k=4) for i in range(2)]
    xdt = m.at(13944, 1024).rearrange("p (k e c) -> p k e c", k=4, e=4)
    xdt_end = m.at(14968, 1024).rearrange("p (k e c) -> p k e c", k=4, e=4)
    y = sh.y = m.at(26216, 8192).rearrange("p (k c) -> p k c", k=4)
    z = m.at(15992, 2048).rearrange("p (k c) -> p k c", k=4)
    decay = [m.at(18040 + 512 * i, 512).rearrange("p (e t) -> p e t", e=4) for i in range(2)]
    cb = [m.at(19064 + 128 * i, 128) for i in range(2)]
    hT = [m.at(19320 + 256 * i, 256) for i in range(2)]
    off = m.at(19832, 256)
    at = 20088
    per_head = [m.at(at + 128 * i, 128) for i in range(6)]
    dt, dta, acs, to_end, from_start, chunk_decay = per_head
    by_head = lambda t: t.rearrange("p (k h) -> p k h", k=4)
    at += 768
    state = m.at(at, 2048).rearrange("p (c b n) -> p c b n", c=2, b=8)
    at += 2048
    conv_state = m.at(at, 768).rearrange("p (c b w) -> p c b w", c=32, b=8)
    at += 768
    conv_tail = m.at(at, 96).rearrange("p (c w) -> p c w", c=32)
    at += 96
    s_cols = m.at(at, 17, 32)
    at += 20
    s_head = m.at(at, 272).rearrange("p (c j) -> p c j", c=16)
    at += 272
    ys = sh.ys = m.small[:, 0:128].rearrange("p (c b) -> p c b", c=16)
    zs = m.at(at, 128).rearrange("p (c b) -> p c b", c=16)
    at += 128
    zs_tanh = m.at(at, 32).rearrange("p (c b) -> p c b", c=4)
    at += 32
    h_out = m.at(at, 256).rearrange("p (c n) -> p c n", c=2)
    at += 256
    window = m.at(at, 128).rearrange("p (c b w) -> p c b w", c=4, b=8)
    at += 128
    window_w = m.at(at, 128).rearrange("p (c b w) -> p c b w", c=4, b=8)
    at += 128
    half_w = m.at(at, 128).rearrange("p (c w) -> p c w", c=32)
    at += 128
    half_b = m.at(at, 32)
    at += 32
    w_dt = m.at(at, 256)
    at += 256
    soft_a, soft_b, soft_c = (m.at(at + 136 * i, 136) for i in range(3))
    at += 408
    exp_a = m.at(at, 33)
    at += 36
    xdt_s = m.at(at, 16).rearrange("p (c b) -> p c b", c=2)
    at += 16
    skip_s = m.at(at, 16).rearrange("p (c b) -> p c b", c=2)
    at += 16
    x_new = [m.at(at + 32 * i, 32).rearrange("p (c b) -> p c b", c=4) for i in range(2)]
    at += 64
    assert at <= 26216

    def parts_of(g):
        z = [(("z", g // 2), t) for t in ((2, 3) if g % 2 else (0, 1))]
        x = [(("x", g + 2), t) for t in range(4)] if g + 2 < G else []
        return z + x if g % 2 else x + z

    step_parts = [parts_of(g) for g in range(G)]
    seq = [("x", 0), ("x", 1)] + [key for parts in step_parts for key, t in parts if t == 3]
    place = {k: i for i, k in enumerate(seq)}

    n_units = [8 if kind == "x" else 5 for kind, _ in seq]
    units_upto = [sum(n_units[:i + 1]) for i in range(len(seq))]
    first = {key: units_upto[i] - n_units[i] for i, key in enumerate(seq)}

    points = {6: ("chunk0", "chunk1", "chunk2", "chunk3", "end0", "end1"), 2: ("chunk0", "chunk2")}

    def unit_at(g, point):
        at = points[len(step_parts[g])]
        return step_parts[g][at.index(point)] if point in at else None

    turns = [(w, g, k) for g in range(G) for w, n in (("rows", 4), ("state", 4), ("last", 1)) for k in range(n)]
    turn_at = {k: i for i, k in enumerate(turns)}

    with ExitStack() as c:
        names = ("proj_ready", "proj_free0", "proj_free1", "proj_free2", "small_in", "dt_ready",
                 "dt_a", "dt_b", "dt_c", "dt_done", "sums_ready", "sums_kept", "expand_ready", "expand_kept",
                 "pad_ready", "conv_ready", "tanh_ready", "xc_ready", "z_tanh", "z_ready", "turn_ready",
                 "turn_free", "xdt_ready", "acs_ready", "cb_ready", "cb_free", "diff_ready",
                 "exp_ready", "mix_ready", "y_ready", "y_free", "skip_ready", "h_ready", "bc_ready", "bc_free",
                 "state_in", "state_decayed", "state_new", "state_out", "h_stored", "conv_in", "conv_rows",
                 "window_ready", "pads", "conv_stored")
        a = stage_semaphores(nc, c, "c_", names)
        block = c.enter_context(nc.Block())

        @block.sync
        def _(sp):
            sp.dma_start(w_dt, ins["w_dt"]).then_inc(a["small_in"], 16)
            sp.dma_start(conv_state.rearrange("p c b w -> p (c b w)"), ins["state_conv"]).then_inc(a["conv_in"], 16)
            loaded = 2
            for g in range(G):
                upto = 4 + sum(t == 3 for parts in step_parts[:g + 1] for _, t in parts)
                if g:
                    sp.wait_ge(a["state_out"], 32 * g)
                    sp.wait_ge(a["bc_free"], 4 * g)
                for half in range(2):
                    r = 256 * g + P * half
                    sp.dma_start(state[:, half], ins["state_ssm"][:, r:r + P].rearrange("b p n -> p b n")).then_inc(
                        a["state_in"], 16)
                while loaded < upto:
                    sp.wait_ge(a["proj_ready"], units_upto[loaded - 2])
                    b = B_SSD + loaded
                    sp.dma_start(m.slot[b % 2], ins["stream"][b]).then_inc(s[f"ring_in{b % 2}"], 16)
                    loaded += 1
                sp.wait_ge(a["turn_free"], turn_at[("last", g, 0)] + 1)
                sp.dma_start(outs["ssm_prompt"][256 * g:256 * g + 256].rearrange("(c p) n -> p c n", p=P),
                             h_out).then_inc(a["h_stored"], 16)
                sp.wait_ge(a["state_new"], g + 1)
                for half in range(2):
                    r = 256 * g + P * half
                    sp.dma_start(outs["ssm_sample"][:, r:r + P].rearrange("b p n -> p b n"),
                                 state[:, half]).then_inc(a["state_out"], 16)
            sp.wait_ge(a["conv_rows"], 2 * G)
            sp.dma_start(outs["conv_prompt"], conv_tail.rearrange("p c w -> p (c w)")).then_inc(a["conv_stored"], 16)
            sp.dma_start(outs["conv_sample"], conv_state.rearrange("p c b w -> p (c b w)")).then_inc(
                a["conv_stored"], 16)
            sp.wait_ge(a["conv_stored"], 32)
            sp.wait_ge(a["state_out"], 32 * G)
            sp.wait_ge(a["h_stored"], 16 * G)

        @block.gpsimd
        def _(pool):
            for i in range(2):
                nc.gpsimd.memset(xpad[i][:, :, 0:3], 0.0).then_inc(a["pads"], 1)

            def tails(g):
                pool.wait_ge(a["pad_ready"], 4 * g + 4)
                nc.gpsimd.tensor_copy(conv_tail[:, 4 * g:4 * g + 4], xpad[g % 2][:, :, 512:515]).then_inc(
                    a["conv_rows"], 1)
                pool.wait_ge(a["window_ready"], g + 1)
                nc.gpsimd.tensor_copy(conv_state[:, 4 * g:4 * g + 4], window[:, :, :, 1:4]).then_inc(a["conv_rows"], 1)

            def mix(g, k):
                i = NCK * g + k
                pool.wait_ge(a["exp_ready"], i + 1)
                pool.wait_ge(a["cb_free"], i + 1)
                nc.gpsimd.tensor_tensor(decay[i % 2], decay[i % 2], cb[i % 2].unsqueeze(1).to_broadcast([P, 4, P]),
                                        ALU.mult).then_inc(a["mix_ready"], 1)

            tails(0)
            tails(1)
            for g in range(G):
                mix(g, 0)
                pool.wait_ge(a["turn_free"], turn_at[("rows", g, 3)] + 1)
                x_rows = rows[g % 2][:, :, 0:256].rearrange("p k (e c) -> p k e c", e=4)
                for k in range(NCK):
                    last = nc.gpsimd.tensor_tensor(
                        y[:, k, 256 * g:256 * g + 256].rearrange("p (e c) -> p e c", e=4), x_rows[:, k],
                        m.head_rows[:, 64 + 4 * g:68 + 4 * g].unsqueeze(2).to_broadcast([P, 4, 64]), ALU.mult)
                last.then_inc(a["skip_ready"], 1)
                mix(g, 1)
                pool.wait_ge(a["state_in"], 32 * (g + 1))
                if g == 0:
                    pool.wait_ge(a["expand_kept"], 1)
                for half in range(2):
                    last = nc.gpsimd.tensor_tensor(
                        state[:, half], state[:, half],
                        s_head[:, 2 * g + half, 8:16].unsqueeze(2).to_broadcast([P, 8, P]), ALU.mult)
                last.then_inc(a["state_decayed"], 1)
                mix(g, 2)
                mix(g, 3)
                if g + 2 < G:
                    tails(g + 2)

        @block.scalar
        def _(act):
            act.wait_ge(a["dt_a"], 1)
            nc.scalar.activation(soft_b, soft_b, ACT.Exp, scale=-1.0).then_inc(a["dt_b"], 1)
            nc.scalar.activation(exp_a[:, 0:32], m.head_rows[:, 32:64], ACT.Exp)
            nc.scalar.activation(exp_a[0:32, 32:33], m.head_cols[:, 1:2], ACT.Exp).then_inc(a["dt_b"], 1)
            act.wait_ge(a["dt_c"], 1)
            nc.scalar.activation(soft_b, soft_b, ACT.Ln).then_inc(a["dt_b"], 1)
            act.wait_ge(a["dt_done"], 1)
            nc.scalar.activation(s_cols[:, 8:16], s_cols[:, 8:16], ACT.Exp).then_inc(a["dt_b"], 1)
            act.wait_ge(a["pads"], 2)

            def pad(g, t):
                if g >= 2 and t == 0:
                    act.wait_ge(a["conv_ready"], g - 1)
                    act.wait_ge(a["conv_rows"], 2 * (g - 1))
                for half in range(2):
                    unit = first[("x", g)] + 2 * t + half
                    b = unit % 3
                    act.wait_ge(a["proj_ready"], unit + 1)
                    lo, hi = HALF * half, min(HALF * half + HALF, SEQ)
                    last = nc.scalar.copy(xpad[g % 2][:, t, 3 + lo:3 + hi], bank[b][:, 0:hi - lo])
                    if half:
                        last = nc.scalar.copy(x_new[g % 2][:, t], bank[b][:, hi - lo:HALF])
                    last.then_inc(a[f"proj_free{b}"], 1)
                    act.wait_ge(a[f"proj_free{b}"], unit // 3 + 1)
                act.sem_inc(a["pad_ready"], 1)

            def gate(j, t):
                unit = first[("z", j)] + t
                act.wait_ge(a["proj_ready"], unit + 1)
                if 4 * j + t:
                    act.wait_ge(a["z_ready"], 5 * j + t)
                nc.scalar.activation(z_tanh, bank[unit % 3][:, :], ACT.Tanh, scale=0.5).then_inc(a["z_tanh"], 1)
                if t == 3:
                    act.wait_ge(a["proj_ready"], unit + 2)
                    nc.scalar.activation(zs_tanh, bank[(unit + 1) % 3][:, 0:32].rearrange("p (c b) -> p c b", c=4),
                                         ACT.Tanh, scale=0.5).then_inc(a["z_tanh"], 1)

            def unit_of(g, point):
                found = unit_at(g, point)
                if found:
                    (kind, number), t = found
                    (pad if kind == "x" else gate)(number, t)

            def silu(g):
                act.wait_ge(a["conv_ready"], g + 1)
                nc.scalar.activation(tanh, xc[g % 2], ACT.Tanh).then_inc(a["tanh_ready"], 1)

            for t in range(4):
                pad(0, t)
            act.wait_ge(a["sums_kept"], 1)
            nc.scalar.activation(from_start, acs, ACT.Exp)
            nc.scalar.activation(to_end, to_end, ACT.Exp)
            nc.scalar.activation(chunk_decay, chunk_decay, ACT.Exp).then_inc(a["dt_b"], 1)
            silu(0)
            for t in range(4):
                pad(1, t)

            def keep_rows(g, k):
                act.wait_ge(a["turn_ready"], turn_at[("rows", g, k)] + 1)
                if g >= 2 and k == 0:
                    act.wait_ge(a["y_free"], NCK * (g - 1))
                    act.wait_ge(a["skip_ready"], g - 1)
                nc.scalar.copy(rows[g % 2][:, k], bank[3][:, 0:384]).then_inc(a["turn_free"], 1)

            for g in range(G):
                keep_rows(g, 0)
                keep_rows(g, 1)
                keep_rows(g, 2)
                keep_rows(g, 3)
                for k in range(NCK):
                    i = NCK * g + k
                    act.wait_ge(a["diff_ready"], i + 1)
                    nc.scalar.activation(decay[i % 2], decay[i % 2], ACT.Exp).then_inc(a["exp_ready"], 1)
                    unit_of(g, f"chunk{k}")
                    if k == 0 and g + 1 < G:
                        silu(g + 1)
                unit_of(g, "end0")
                act.wait_ge(a["turn_ready"], turn_at[("last", g, 0)] + 1)
                if g:
                    act.wait_ge(a["h_stored"], 16 * g)
                nc.scalar.copy(h_out, bank[3][:, 0:256].rearrange("p (c n) -> p c n", c=2)).then_inc(a["turn_free"], 1)
                unit_of(g, "end1")

        @block.vector
        def _(dve):
            link = lambda i: sh.dve(dve, i)
            nc.vector.tensor_scalar(half_w, m.conv_w, 0.5, None, ALU.mult)
            link(nc.vector.tensor_scalar(half_b, m.conv_b, 0.5, None, ALU.mult))
            link(nc.vector.memset(soft_a, 0.0))
            dve.wait_ge(a["conv_in"], 16)
            dve.wait_ge(a["dt_ready"], 1)
            nc.vector.tensor_tensor(by_head(soft_a[:, 0:128]), by_head(bank[5][:, 0:128]),
                                    m.head_rows[:, 0:32].unsqueeze(1).to_broadcast([P, 4, 32]), ALU.add)
            link(nc.vector.tensor_scalar(soft_a[0:32, 128:136], bank[6][0:32, 0:8], m.head_cols[:, 0:1], None, ALU.add))
            link(nc.vector.tensor_scalar(soft_b, soft_a, -1.0, None, ALU.mult))
            nc.vector.tensor_tensor(soft_b, soft_b, soft_a, ALU.max).then_inc(a["dt_a"], 1)
            dve.wait_ge(a["dt_b"], 2)
            nc.vector.tensor_scalar(soft_b, soft_b, 1.0, None, ALU.add).then_inc(a["dt_c"], 1)
            dve.wait_ge(a["dt_b"], 3)
            link(nc.vector.scalar_tensor_tensor(soft_c, soft_a, 0.0, soft_b, ALU.max, ALU.add))
            nc.vector.tensor_copy(dt, soft_c[:, 0:128])
            nc.vector.tensor_copy(s_cols[:, 0:8], soft_c[0:32, 128:136])
            nc.vector.tensor_copy(s_cols[:, 16:17], m.head_cols[:, 2:3])
            nc.vector.tensor_scalar(s_cols[:, 8:16], soft_c[0:32, 128:136], exp_a[0:32, 32:33], -1.0, ALU.mult, ALU.mult)
            nc.vector.scalar_tensor_tensor(by_head(dta), by_head(soft_c[:, 0:128]), -1.0,
                                           exp_a[:, 0:32].unsqueeze(1).to_broadcast([P, 4, 32]), ALU.mult,
                                           ALU.mult).then_inc(a["dt_done"], 1)
            def windows(g):
                dve.wait_ge(a["pad_ready"], 4 * g + 4)
                if g:
                    dve.wait_ge(a["conv_rows"], 2 * g)
                nc.vector.tensor_copy(window[:, :, :, 0:3], conv_state[:, 4 * g:4 * g + 4])
                nc.vector.tensor_copy(window[:, :, :, 3], x_new[g % 2]).then_inc(a["window_ready"], 1)
                dve.wait_ge(a["window_ready"], g + 1)

            def conv(g):
                out = xc[g % 2]
                link(nc.vector.tensor_tensor(window_w, window,
                                             half_w[:, 4 * g:4 * g + 4].unsqueeze(2).to_broadcast([P, 4, 8, 4]),
                                             ALU.mult))
                if g >= 2:
                    dve.wait_ge(a["y_ready"], NCK * (g - 1))
                    dve.wait_ge(a["bc_ready"], 4 * (g - 1))
                link(nc.vector.tensor_reduce(out[:, :, 512:520], window_w, X_AXIS, ALU.add))
                nc.vector.tensor_tensor(out[:, :, 512:520], out[:, :, 512:520],
                                        half_b[:, 4 * g:4 * g + 4].unsqueeze(2).to_broadcast([P, 4, 8]), ALU.add)
                dve.wait_ge(a["pad_ready"], 4 * g + 4)
                for t in range(4):
                    w = half_w[:, 4 * g + t]
                    last = nc.vector.tensor_scalar(out[:, t, 0:512], xpad[g % 2][:, t, 0:512], w[:, 0:1],
                                                   half_b[:, 4 * g + t:4 * g + t + 1], ALU.mult, ALU.add)
                link(last)
                for j in range(1, 4):
                    for t in range(4):
                        last = nc.vector.scalar_tensor_tensor(out[:, t, 0:512], xpad[g % 2][:, t, j:j + 512],
                                                              half_w[:, 4 * g + t, j:j + 1], out[:, t, 0:512],
                                                              ALU.mult, ALU.add)
                    if j < 3:
                        link(last)
                last.then_inc(a["conv_ready"], 1)

            def conv_silu(g):
                dve.wait_ge(a["tanh_ready"], g + 1)
                link(nc.vector.scalar_tensor_tensor(xc[g % 2], tanh, 1.0, xc[g % 2], ALU.add, ALU.mult))
                dve.sem_inc(a["xc_ready"], 1)

            def gate_values(j, t):
                unit = first[("z", j)] + t
                b = unit % 3
                dve.wait_ge(a["z_tanh"], 5 * j + t + 1)
                nc.vector.scalar_tensor_tensor(z[:, t], z_tanh, 1.0, bank[b][:, :], ALU.add,
                                               ALU.mult).then_inc(a[f"proj_free{b}"], 1)
                dve.wait_ge(a[f"proj_free{b}"], unit // 3 + 1)
                dve.sem_inc(a["z_ready"], 1)
                if t == 3:
                    b = (unit + 1) % 3
                    dve.wait_ge(a["z_tanh"], 5 * j + 5)
                    nc.vector.scalar_tensor_tensor(zs[:, 4 * j:4 * j + 4], zs_tanh, 1.0,
                                                   bank[b][:, 0:32].rearrange("p (c b) -> p c b", c=4), ALU.add,
                                                   ALU.mult).then_inc(a[f"proj_free{b}"], 1)
                    dve.wait_ge(a[f"proj_free{b}"], (unit + 1) // 3 + 1)
                    dve.sem_inc(a["z_ready"], 1)

            def unit_of(g, point):
                found = unit_at(g, point)
                if found:
                    (kind, number), t = found
                    if kind == "z":
                        gate_values(number, t)
                    elif t == 3:
                        windows(number)

            def decays(g, k):
                i = NCK * g + k
                dve.wait_ge(a["cb_ready"], i + 1)
                if i >= 2:
                    dve.wait_ge(a["mix_ready"], i - 1)
                    dve.wait_ge(a["y_ready"], i - 1)
                nc.vector.tensor_tensor(cb[i % 2], bank[5][:, 0:128], m.c(C_TRI), ALU.mult).then_inc(a["cb_free"], 1)
                dve.wait_ge(a["acs_ready"], i + 1)
                for e in range(4):
                    h = 32 * k + 4 * g + e
                    last = nc.vector.tensor_scalar(decay[i % 2][:, e], bank[4][:, P * e:P * e + P], acs[:, h:h + 1], 0.0,
                                                   ALU.subtract, ALU.min)
                last.then_inc(a["diff_ready"], 1)

            def start_chunks(g):
                dve.wait_ge(a["turn_free"], turn_at[("rows", g, 3)] + 1)
                if g:
                    dve.wait_ge(a["turn_ready"], turn_at[("state", g - 1, 3)] + 1)
                x_rows = rows[g % 2][:, :, 0:256].rearrange("p k (e c) -> p k e c", e=4)
                heads = slice(4 * g, 4 * g + 4)
                link(nc.vector.tensor_tensor(xdt, x_rows, by_head(dt)[:, :, heads].unsqueeze(3).to_broadcast([P, 4, 4, 64]),
                                             ALU.mult))
                nc.vector.tensor_tensor(xdt_end, xdt, by_head(to_end)[:, :, heads].unsqueeze(3).to_broadcast([P, 4, 4, 64]),
                                        ALU.mult).then_inc(a["xdt_ready"], 1)
                decays(g, 0)

            def chunk(g, k):
                heads = slice(4 * g, 4 * g + 4)
                i = NCK * g + k
                if k == 0:
                    dve.wait_ge(a["skip_ready"], g + 1)
                dve.wait_ge(a["y_ready"], i + 1)
                yk = y[:, k, 256 * g:256 * g + 256]
                if k:
                    nc.vector.tensor_tensor(off.rearrange("p (e c) -> p e c", e=4),
                                            bank[6][:, 256:512].rearrange("p (e c) -> p e c", e=4),
                                            by_head(from_start)[:, k, heads].unsqueeze(2).to_broadcast([P, 4, 64]),
                                            ALU.mult)
                nc.vector.tensor_tensor(yk, yk, bank[6][:, 0:256], ALU.add).then_inc(a["y_free"], 1)
                dve.wait_ge(a["y_free"], i + 1)
                if k:
                    nc.vector.tensor_tensor(yk, yk, off, ALU.add)
                if k:
                    link(nc.vector.tensor_tensor(
                        hT[k % 2].rearrange("p (e c) -> p e c", e=4), hT[(k - 1) % 2].rearrange("p (e c) -> p e c", e=4),
                        by_head(chunk_decay)[:, k, heads].unsqueeze(2).to_broadcast([P, 4, 64]), ALU.mult))
                t = turn_at[("state", g, k)]
                dve.wait_ge(a["turn_ready"], t + 1)
                if k:
                    last = nc.vector.tensor_tensor(hT[k % 2], hT[k % 2], bank[3][:, 0:256], ALU.add)
                else:
                    last = nc.vector.tensor_copy(hT[0], bank[3][:, 0:256])
                last.then_inc(a["turn_free"], 1)
                dve.wait_ge(a["turn_free"], t + 1)
                dve.sem_inc(a["h_ready"], 1)

            def sample(g, q):
                if q == 0:
                    xs = xc[g % 2][:, 0:2, 512:520]
                    nc.vector.tensor_tensor(skip_s, xs, s_head[:, 2 * g:2 * g + 2, 16:17].to_broadcast([P, 2, 8]),
                                            ALU.mult)
                    link(nc.vector.tensor_tensor(xdt_s, xs, s_head[:, 2 * g:2 * g + 2, 0:8], ALU.mult))
                i = 4 * g + q
                part = slice(4 * (q % 2), 4 * (q % 2) + 4)
                dve.wait_ge(a["bc_ready"], i + 1)
                wide = bank[7][:, :].rearrange("p (b n) -> p b n", b=4)
                for half in range(2):
                    other = state[:, half, part] if q >= 2 else \
                        xdt_s[:, half, part].unsqueeze(2).to_broadcast([P, 4, P])
                    last = nc.vector.tensor_tensor(update[:, half, part], wide, other, ALU.mult)
                last.then_inc(a["bc_free"], 1)
                dve.wait_ge(a["bc_free"], i + 1)
                if q == 1:
                    dve.wait_ge(a["state_decayed"], g + 1)
                    nc.vector.tensor_tensor(state, state, update, ALU.add).then_inc(a["state_new"], 1)
                    dve.wait_ge(a["state_new"], g + 1)
                if q == 3:
                    link(nc.vector.tensor_reduce(ys[:, 2 * g:2 * g + 2], update, X_AXIS, ALU.add))
                    link(nc.vector.tensor_tensor(ys[:, 2 * g:2 * g + 2], ys[:, 2 * g:2 * g + 2], skip_s, ALU.add))

            windows(0)
            dve.wait_ge(a["sums_ready"], 1)
            nc.vector.tensor_copy(acs, bank[4][:, 0:128])
            link(nc.vector.tensor_copy(chunk_decay, bank[4][:, 128:256]))
            nc.vector.tensor_tensor(to_end, chunk_decay, acs, ALU.subtract).then_inc(a["sums_kept"], 1)
            dve.wait_ge(a["expand_ready"], 1)
            nc.vector.tensor_copy(s_head, bank[6][:, 0:272].rearrange("p (c j) -> p c j", c=16)).then_inc(
                a["expand_kept"], 1)
            conv(0)
            conv_silu(0)
            windows(1)
            dve.wait_ge(a["dt_b"], 5)
            for g in range(G):
                start_chunks(g)
                if g + 1 < G:
                    conv(g + 1)
                unit_of(g, "chunk0")
                for k in range(NCK):
                    if k + 1 < NCK:
                        decays(g, k + 1)
                    chunk(g, k)
                    if k == 0:
                        if g + 1 < G:
                            conv_silu(g + 1)
                    else:
                        sample(g, k - 1)
                    if k + 1 < NCK:
                        unit_of(g, f"chunk{k + 1}")
                unit_of(g, "end0")
                sample(g, 3)
                unit_of(g, "end1")
                if g % 2:
                    j = g // 2
                    link(nc.vector.scalar_tensor_tensor(y[:, :, 512 * j:512 * j + 512], z, 0.5,
                                                        y[:, :, 512 * j:512 * j + 512], ALU.mult, ALU.mult))
            link(nc.vector.scalar_tensor_tensor(ys, zs, 0.5, ys, ALU.mult, ALU.mult))

        @block.tensor
        def _(pe):
            pe.wait_ge(a["small_in"], 16)
            for k4 in range(4):
                for k in range(8):
                    nc.tensor.matmul(bank[5][:, 32 * k4:32 * k4 + 32], m.hT[:, k, P * k4:P * k4 + P],
                                     w_dt[:, 32 * k:32 * k + 32], start=(k == 0), stop=(k == 7))
            for k in range(8):
                last = nc.tensor.matmul(bank[6][0:32, 0:8], w_dt[:, 32 * k:32 * k + 32], m.hT[:, k, SEQ:T_ALL],
                                        start=(k == 0), stop=(k == 7))
            last.then_inc(a["dt_ready"], 1)

            def project(key, t):
                i = place[key]
                b = B_SSD + i
                w = m.slot[b % 2]
                if t == 0:
                    pe.wait_ge(s[f"ring_in{b % 2}"], 16 * (b // 2 + 1))
                parts = [2 * t, 2 * t + 1] if key[0] == "x" else [t, 4][:1 + (t == 3)]
                for part in parts:
                    unit = first[key] + part
                    out = bank[unit % 3]
                    if unit >= 3:
                        pe.wait_ge(a[f"proj_free{unit % 3}"], unit // 3)
                    weights = lambda k, c: w[:, 512 * k + P * c:512 * k + P * c + P]
                    if key[0] == "x":
                        sums = [(out[:, 0:HALF], lambda k: weights(k, t), lambda k: m.hT[:, k, half_of(part % 2)])]
                    elif part < 4:
                        sums = [(out[:, :], lambda k: m.hT[:, k, P * t:P * t + P],
                                 lambda k: w[:, 512 * k:512 * k + 512])]
                    else:
                        sums = [(out[:, 8 * c:8 * c + 8], lambda k, c=c: weights(k, c),
                                 lambda k: m.hT[:, k, SEQ:T_ALL]) for c in range(4)]
                    for result, stationary, moving in sums:
                        for k in range(8):
                            last = nc.tensor.matmul(result, stationary(k), moving(k), start=(k == 0), stop=(k == 7))
                    last.then_inc(a["proj_ready"], 1)

            def unit_of(g, point):
                found = unit_at(g, point)
                if found:
                    project(*found)

            for t in range(4):
                project(("x", 0), t)
            pe.wait_ge(a["dt_done"], 1)
            nc.tensor.matmul(bank[4][:, 0:128], m.c(C_TRI), dta, start=True, stop=True)
            nc.tensor.matmul(bank[4][:, 128:256], m.c(C_ONES), dta, start=True, stop=True).then_inc(a["sums_ready"], 1)
            pe.wait_ge(a["dt_b"], 4)
            for pair in range(16):
                last = nc.tensor.matmul(bank[6][:, 17 * pair:17 * pair + 17], m.c(C_EXPAND + P * pair, P, 32), s_cols,
                                        start=True, stop=True)
            last.then_inc(a["expand_ready"], 1)
            for t in range(4):
                project(("x", 1), t)
            pe.wait_ge(a["sums_kept"], 1)
            pe.wait_ge(a["expand_kept"], 1)

            def own_turn(key):
                i = turn_at[key]
                if i:
                    pe.wait_ge(a["turn_free"], i)

            def weigh(g, k):
                i = NCK * g + k
                x = xc[g % 2]
                if i:
                    pe.wait_ge(a["cb_free"], i)
                nc.tensor.matmul(bank[5][:, 0:128], x[:, 2, P * k:P * k + P], x[:, 3, P * k:P * k + P], start=True,
                                 stop=True).then_inc(a["cb_ready"], 1)
                if i:
                    pe.wait_ge(a["diff_ready"], i)
                for e in range(4):
                    h = 32 * k + 4 * g + e
                    last = nc.tensor.matmul(bank[4][:, P * e:P * e + P], dta[:, h:h + 1].to_broadcast([P, P]),
                                            m.c(C_TRI), start=True, stop=True)
                last.then_inc(a["acs_ready"], 1)

            def spread(g, q):
                i = 4 * g + q
                if i:
                    pe.wait_ge(a["bc_free"], i)
                for b in range(4):
                    at_b = SEQ + 4 * (q % 2) + b
                    last = nc.tensor.matmul(bank[7][:, P * b:P * b + P],
                                            xc[g % 2][:, 2 + q // 2, at_b:at_b + 1].to_broadcast([P, P]),
                                            m.c(C_IDENT), start=True, stop=True)
                last.then_inc(a["bc_ready"], 1)

            def chunk_products(g, k):
                i = NCK * g + k
                x = xc[g % 2]
                if k == 0:
                    pe.wait_ge(a["xdt_ready"], g + 1)
                pe.wait_ge(a["mix_ready"], i + 1)
                if i:
                    pe.wait_ge(a["y_free"], i)
                if k:
                    pe.wait_ge(a["h_ready"], i)
                    nc.tensor.matmul(bank[6][:, 256:512], x[:, 3, P * k:P * k + P], hT[(k - 1) % 2], start=True,
                                     stop=True)
                for e in range(4):
                    last = nc.tensor.matmul(bank[6][:, 64 * e:64 * e + 64], decay[i % 2][:, e], xdt[:, k, e],
                                            start=True, stop=True)
                last.then_inc(a["y_ready"], 1)
                own_turn(("state", g, k))
                nc.tensor.matmul(bank[3][:, 0:256], rows[g % 2][:, k, 256:384], xdt_end[:, k], start=True,
                                 stop=True).then_inc(a["turn_ready"], 1)

            def turn_rows(g, k):
                own_turn(("rows", g, k))
                for j in range(3):
                    last = nc.tensor.transpose(bank[3][:, P * j:P * j + P], xc[g % 2][:, j, P * k:P * k + P],
                                               m.c(C_IDENT))
                last.then_inc(a["turn_ready"], 1)

            for g in range(G):
                pe.wait_ge(a["xc_ready"], g + 1)
                turn_rows(g, 0)
                turn_rows(g, 1)
                turn_rows(g, 2)
                turn_rows(g, 3)
                weigh(g, 0)
                for k in range(NCK):
                    unit_of(g, f"chunk{k}")
                    if k + 1 < NCK:
                        weigh(g, k + 1)
                    chunk_products(g, k)
                    if k:
                        spread(g, k - 1)
                unit_of(g, "end0")
                spread(g, 3)
                own_turn(("last", g, 0))
                for half in range(2):
                    last = nc.tensor.transpose(bank[3][:, P * half:P * half + P], hT[1][:, P * half:P * half + P],
                                               m.c(C_IDENT))
                last.then_inc(a["turn_ready"], 1)
                unit_of(g, "end1")


def merge_branches(sh):
    nc, ins, m, bank, s = sh.nc, sh.ins, sh.m, sh.bank, sh.s
    x = sh.x = m.at(0, 5120).rearrange("p (n d) -> p n d", n=N_T)
    gates = m.at(5120, 8320).rearrange("p (c t) -> p c t", t=T_ALL)
    yT = m.at(13440, 8320).rearrange("p (c t) -> p c t", t=T_ALL)
    squares = m.at(13440, 8192).rearrange("p (k c) -> p k c", k=4)
    merged = m.at(21760, 4160).rearrange("p (c t) -> p c t", t=T_ALL)
    y, ys = sh.y, sh.ys
    parts = [m.at(26216 + HALF * i, HALF) for i in range(4)]
    stat = m.at(25920, 32)
    part_s = m.at(25952, 128)
    n_units = [8] * 4 + [16] + [4] * 4 + [5] * 2
    upto = [sum(n_units[:i + 1]) for i in range(len(n_units))]
    first = [u - n for u, n in zip(upto, n_units)]

    with ExitStack() as c:
        names = ("x_in", "squares", "inverse", "roots", "scaled", "turned", "turn_free", "s_square", "s_sum",
                 "s_inverse", "s_scaled", "proj_ready", "proj_free0", "proj_free1", "proj_free2", "gates", "merged",
                 "done")
        a = stage_semaphores(nc, c, "d_", names)
        block = c.enter_context(nc.Block())

        @block.sync
        def _(sp):
            sp.dma_start(x[:, 0:4, :], ins["x_prompt"].rearrange("(n p) d -> p n d", p=P)).then_inc(a["x_in"], 16)
            sp.dma_start(x[0:N_S, 4, :], ins["x_sample"]).then_inc(a["x_in"], 16)
            for i in range(2, 13):
                b = B_GATE + i
                sp.wait_ge(a["proj_ready"], upto[i - 2])
                sp.dma_start(m.slot[b % 2], ins["stream"][b]).then_inc(s[f"ring_in{b % 2}"], 16)

        @block.scalar
        def _(act):
            for k in range(4):
                nc.scalar.activation(squares[:, k], y[:, k], ACT.Square, accum_out=stat[:, k:k + 1]).then_inc(a["squares"], 1)
            act.wait_ge(a["inverse"], 1)
            nc.scalar.activation(stat[:, 8:12], stat[:, 4:8], ACT.Sqrt).then_inc(a["roots"], 1)
            act.wait_ge(a["s_inverse"], 1)
            nc.scalar.activation(stat[:, 24:32], stat[:, 16:24], ACT.Sqrt).then_inc(a["roots"], 1)
            for i in range(4):
                for u in range(8):
                    t, half = divmod(u, 2)
                    unit = first[i] + u
                    act.wait_ge(a["proj_ready"], unit + 1)
                    nc.scalar.activation(gates[:, 4 * i + t, half_of(half)], bank[unit % 3][:, 0:HALF], ACT.Tanh,
                                         scale=0.5).then_inc(a[f"proj_free{unit % 3}"], 1)
            for b in range(3):
                act.wait_ge(a[f"proj_free{b}"], uses_of_bank(b, upto[3]))
            act.sem_inc(a["gates"], 1)

        @block.vector
        def _(dve):
            link = lambda i: sh.dve(dve, i)
            dve.wait_ge(a["squares"], 4)
            link(nc.vector.tensor_scalar(stat[:, 0:4], stat[:, 0:4], 1.0 / D_INNER, EPS, ALU.mult, ALU.add))
            nc.vector.reciprocal(stat[:, 4:8], stat[:, 0:4]).then_inc(a["inverse"], 1)
            nc.vector.tensor_tensor(part_s, ys.rearrange("p c b -> p (c b)"), ys.rearrange("p c b -> p (c b)"),
                                    ALU.mult).then_inc(a["s_square"], 1)
            dve.wait_ge(a["s_sum"], 1)
            link(nc.vector.tensor_reduce(stat[:, 16:24], bank[7][:, 0:128].rearrange("p (c b) -> p b c", c=16), X_AXIS,
                                         ALU.add))
            link(nc.vector.tensor_scalar(stat[:, 16:24], stat[:, 16:24], 1.0 / D_INNER, EPS, ALU.mult, ALU.add))
            nc.vector.reciprocal(stat[:, 16:24], stat[:, 16:24]).then_inc(a["s_inverse"], 1)
            dve.wait_ge(a["roots"], 1)
            for k in range(4):
                nc.vector.tensor_scalar(y[:, k], y[:, k], stat[:, 8 + k:9 + k], None, ALU.mult).then_inc(a["scaled"], 1)
            dve.wait_ge(a["roots"], 2)
            link(nc.vector.tensor_tensor(ys, ys, stat[:, 24:32].unsqueeze(1).to_broadcast([P, 16, 8]), ALU.mult))
            nc.vector.tensor_tensor(yT[:, :, SEQ:T_ALL], ys, m.norm_ssd.unsqueeze(2).to_broadcast([P, 16, 8]),
                                    ALU.mult).then_inc(a["s_scaled"], 1)
            for k in range(4):
                for q in range(4):
                    i = 4 * k + q
                    dve.wait_ge(a["turned"], i + 1)
                    nc.vector.tensor_tensor(yT[:, 4 * q:4 * q + 4, P * k:P * k + P],
                                            bank[5 + i % 2][:, :].rearrange("p (c t) -> p c t", c=4),
                                            m.norm_ssd[:, 4 * q:4 * q + 4].unsqueeze(2).to_broadcast([P, 4, P]),
                                            ALU.mult).then_inc(a["turn_free"], 1)
            dve.wait_ge(a["turn_free"], 16)
            dve.wait_ge(a["gates"], 1)
            for u in range(16):
                t, half = divmod(u, 2)
                unit = first[4] + u
                dve.wait_ge(a["proj_ready"], unit + 1)
                nc.vector.scalar_tensor_tensor(merged[:, t, half_of(half)], gates[:, t, half_of(half)], 1.0,
                                               bank[unit % 3][:, 0:HALF], ALU.add,
                                               ALU.mult).then_inc(a[f"proj_free{unit % 3}"], 1)
            for j in range(4):
                for u in range(4):
                    t, half = divmod(u, 2)
                    unit = first[5 + j] + u
                    row = 2 * j + t
                    part = parts[u]
                    dve.wait_ge(a["proj_ready"], unit + 1)
                    nc.vector.scalar_tensor_tensor(part, gates[:, 8 + row, half_of(half)], 1.0,
                                                   bank[unit % 3][:, 0:HALF], ALU.add,
                                                   ALU.mult).then_inc(a[f"proj_free{unit % 3}"], 1)
                    dve.wait_ge(a[f"proj_free{unit % 3}"], unit // 3 + 1)
                    last = nc.vector.tensor_tensor(merged[:, row, half_of(half)], merged[:, row, half_of(half)], part,
                                                   ALU.add)
                last.then_inc(a["merged"], 1)
                dve.wait_ge(a["merged"], j + 1)
            for j in range(2):
                for t in range(5):
                    unit = first[9 + j] + t
                    r = rows_of(t)
                    dve.wait_ge(a["proj_ready"], unit + 1)
                    xs = x[0:r, t, 512 * j:512 * j + 512]
                    if unit == first[9]:
                        dve.wait_ge(a["x_in"], 32)
                    nc.vector.scalar_tensor_tensor(xs, bank[unit % 3][0:r, :], 0.5, xs, ALU.mult,
                                                   ALU.add).then_inc(a[f"proj_free{unit % 3}"], 1)
            for b in range(3):
                dve.wait_ge(a[f"proj_free{b}"], uses_of_bank(b, upto[-1]))

        @block.tensor
        def _(pe):
            def unit_free(unit):
                if unit >= 3:
                    pe.wait_ge(a[f"proj_free{unit % 3}"], unit // 3)

            def columns(i, n_k, width, src):
                b = B_GATE + i
                w = m.slot[b % 2]
                pe.wait_ge(s[f"ring_in{b % 2}"], 16 * (b // 2 + 1))
                for u in range(n_units[i]):
                    t, half = divmod(u, 2)
                    unit = first[i] + u
                    unit_free(unit)
                    for k in range(n_k):
                        last = nc.tensor.matmul(bank[unit % 3][:, 0:HALF], w[:, width * k + P * t:width * k + P * t + P],
                                                src[:, k, half_of(half)], start=(k == 0), stop=(k == n_k - 1))
                    last.then_inc(a["proj_ready"], 1)

            pe.wait_ge(a["s_square"], 1)
            nc.tensor.matmul(bank[7][:, 0:128], m.c(C_ONES), part_s, start=True, stop=True).then_inc(a["s_sum"], 1)
            for i in range(4):
                columns(i, 8, 512, m.hT)
            for k in range(4):
                pe.wait_ge(a["scaled"], k + 1)
                for q in range(4):
                    i = 4 * k + q
                    if i >= 2:
                        pe.wait_ge(a["turn_free"], i - 1)
                    for j in range(4):
                        at = P * (4 * q + j)
                        last = nc.tensor.transpose(bank[5 + i % 2][:, P * j:P * j + P], y[:, k, at:at + P],
                                                   m.c(C_IDENT))
                    last.then_inc(a["turned"], 1)
            columns(4, 4, 1024, m.attT)
            pe.wait_ge(a["turn_free"], 16)
            pe.wait_ge(a["s_scaled"], 1)
            for i in range(5, 9):
                columns(i, 16, 256, yT)
            pe.wait_ge(a["merged"], 4)
            for i in range(9, 11):
                b = B_GATE + i
                pe.wait_ge(s[f"ring_in{b % 2}"], 16 * (b // 2 + 1))
                for t in range(5):
                    unit = first[i] + t
                    r = rows_of(t)
                    unit_free(unit)
                    for k in range(8):
                        last = nc.tensor.matmul(bank[unit % 3][0:r, :], merged[:, k, P * t:P * t + r],
                                                m.slot[b % 2][:, 512 * k:512 * k + 512], start=(k == 0), stop=(k == 7))
                    last.then_inc(a["proj_ready"], 1)


class LoopChain:

    def __init__(self, sem, turn, length, passed, start=0):
        self.sem, self.turn, self.length, self.start, self.count = sem, turn, length, start, 0
        self.passed = passed

    def __call__(self, eng, ins):
        self.count += 1
        ins.then_inc(self.sem, 1)
        eng.wait_ge(self.sem, self.turn.times(self.length, self.start + self.count))
        eng.sem_inc(self.passed, 1)

    def close(self):
        assert self.count == self.length


U_BUFS, V_BUFS = 8, 8
assert TOPK % U_BUFS == 0 and TOPK % V_BUFS == 0


class Head:

    def __init__(self, offset, register=None, scale=1):
        self.offset, self.register, self.scale = offset, register, scale

    def times(self, each, base=0):
        base += self.offset * each
        return base if self.register is None else self.register * (self.scale * each) + base


def peer_and_ple(sh):
    nc, ins, outs, m, bank, s = sh.nc, sh.ins, sh.outs, sh.m, sh.bank, sh.s
    x = sh.x
    hx = m.at(5120, 5120).rearrange("p (n d) -> p n d", n=N_T)
    query = m.at(10240, 8320).rearrange("p (c t) -> p c t", t=T_ALL)
    scores_of = lambda n: query[:, :, P * n:P * n + rows_of(n)]
    keys = m.at(18560, 2048).rearrange("p (c k) -> p c k", c=16)
    ple_x = m.at(20608, 1024).rearrange("p (k t) -> p k t", k=8)
    diag = [m.at(21632 + P * i, P) for i in range(4)] + [m.c(C_TRI + P * i) for i in range(4)]
    stage = m.at(22144, 512).rearrange("p (a w k) -> p a w k", a=2, w=2)
    p_cols = m.at(22656, 1040).rearrange("p (k t) -> p k t", k=2)
    w_proj = m.at(23696, 2048).rearrange("p (k n) -> p k n", k=2)
    row_tmp = m.at(25744, 1024)
    index_f = m.at(26768, 128)
    index = [m.at(26896 + 128 * i, 128).bitcast(U32) for i in range(2)]
    gate = [m.at(27152 + 128 * i, 128) for i in range(2)]
    top_at = 27408
    val = m.at(top_at, 32).rearrange("p (w k) -> p w k", w=2)
    pos = m.at(top_at + 32, 32).bitcast(U32).rearrange("p (w k) -> p w k", w=2)
    best = m.at(top_at + 64, 16)
    best_at = m.at(top_at + 80, 16).bitcast(U32)
    all_best = m.at(top_at + 352, 128).rearrange("p (h k) -> p h k", h=8)
    one_hot = m.at(top_at + 480, 512).rearrange("p (w k a) -> p w k a", w=2, k=16)
    digit_u = m.at(top_at + 992, 32).bitcast(U32)
    digit = m.at(top_at + 1024, 32)
    pos_f = m.at(top_at + 1056, 32)
    picked = m.at(top_at + 1088, 32)
    stat = m.at(top_at + 1120, 64)
    now_u = [m.c(C_RES + 16 * i, 16).bitcast(U32) for i in range(2)]
    now_v = [m.c(C_RES + 32 + 16 * i, 16).bitcast(U32) for i in range(2)]
    dots = m.at(top_at + 1200, 16)
    acts = m.at(top_at + 1216, 16)
    coef = m.at(top_at + 1232, 16)
    index_s = m.at(top_at + 1248, 8).bitcast(U32)
    gate_s = m.at(top_at + 1256, 8)
    assert top_at + 1264 <= 28672
    cand = m.at(28672, 256).rearrange("p (a b) -> p a b", a=16)
    cand_rest = m.at(28928, 256)
    v_buf = [m.at(29184 + 1024 * i, 1024) for i in range(4)] + [m.at(33376, 1024)] + \
        [m.mem[:, at:at + 1024] for at in (8520, 6408, 7432)]
    coef_s = m.at(33280, 64, P).rearrange("p (b c) -> p b c", b=8)
    dots_s = m.at(33344, 16).rearrange("p (b w) -> p b w", b=8)
    u_buf = [m.slot[i // 4][:, 1024 * (i % 4):1024 * (i % 4) + 1024] for i in range(U_BUFS)]
    w_gate_low = [m.at(18560, 2048), m.mem[:, 4360:6408]]
    w_gate_high = [scores_of(n) for n in range(2)]

    def w_gate(k, j):
        if j == 0:
            return w_gate_low[k // 4][:, 512 * (k % 4):512 * (k % 4) + 512]
        return w_gate_high[k // 4][:, 4 * (k % 4):4 * (k % 4) + 4]
    norm_rows = m.mem[:, 8520:10568].rearrange("p (w d) -> p w d", w=2)
    sample_scores = m.c(C_EXPAND, 2048, N_S).rearrange("p (c k) -> p c k", c=16)
    ident = m.c(C_IDENT)
    acc = [(bank[0], bank[1]), (bank[2], bank[7])]

    with ExitStack() as c:
        names = ["small_in", "rows_in", "squares", "inverse", "roots", "scaled", "turned", "columns", "proj_ready",
                 "proj_free0", "proj_free1", "proj_free2", "score_ready", "score_kept", "top_step",
                 "top_done", "gate_max", "gate_exp", "index_ready", "dot_done", "dots_ready", "acts_ready",
                 "coef_ready", "diag_ready", "v_used", "u_staged", "v_staged", "acc_done", "acc_kept",
                 "ple_square", "ple_inverse", "ple_root", "ple_scaled", "ple_turned", "ple_columns", "ple_gate",
                 "ple_gated", "ple_proj", "ple_used", "end_square", "end_inverse", "end_root", "end_rows",
                 "stored", "w_gate_in", "s_turned", "s_index", "s_kept", "s_wide", "s_read", "top_passed", "gather_passed"]
        a = stage_semaphores(nc, c, "e_", names)
        u_in = list(stage_semaphores(nc, c, "e_u_in", [str(i) for i in range(U_BUFS)]).values())
        v_in = list(stage_semaphores(nc, c, "e_v_in", [str(i) for i in range(V_BUFS)]).values())
        block = c.enter_context(nc.Block())

        @block.sync
        def _(sp):
            sp.dma_start(norm_rows.rearrange("p w d -> p (w d)"),
                         ins["norm_rows"].rearrange("w d -> (w d)").partition_broadcast(P)).then_inc(a["rows_in"], 16)
            sp.dma_start(keys.rearrange("p c k -> p (c k)"), ins["keys"]).then_inc(a["small_in"], 16)
            sp.dma_start(p_cols.rearrange("p k t -> p (k t)"), ins["p_cols"]).then_inc(a["small_in"], 16)
            sp.dma_start(w_proj.rearrange("p k n -> p (k n)"), ins["w_ple_proj"]).then_inc(a["small_in"], 16)
            for i in (2, 3):
                b = B_PQ + i
                sp.wait_ge(a["proj_ready"], 8 * (i - 1))
                sp.dma_start(m.slot[b % 2], ins["stream"][b]).then_inc(s[f"ring_in{b % 2}"], 16)
            sp.wait_ge(a["score_ready"], 4 * N_T)
            for i in range(2):
                sp.dma_start(w_gate_low[i], ins["stream"][B_PLE][:, 2048 * i:2048 * i + 2048]).then_inc(
                    a["w_gate_in"], 16)
            sp.wait_ge(a["top_done"], 2)
            for i in range(2):
                src = ins["stream"][B_PLE + 1][:, 2048 * i:2048 * i + 2048].rearrange("p (c k) -> p c k", c=16)
                sp.dma_start(w_gate_high[i], src).then_inc(a["w_gate_in"], 16)
            for n in range(N_T):
                sp.wait_ge(a["end_rows"], n + 1)
                if n == 4:
                    sp.dma_start(outs["y_sample"], x[0:N_S, 4]).then_inc(a["stored"], 16)
                else:
                    sp.dma_start(outs["y_prompt"][P * n:P * n + P], x[:, n]).then_inc(a["stored"], 16)
            sp.wait_ge(a["stored"], 16 * N_T)

        @block.gpsimd
        def _(pool):
            pool.wait_ge(a["proj_ready"], 32)

            def gather(table, idx, buf, arrived):
                nc.gpsimd.indirect_dma_start(buf, None, ins[table], bass.IndirectOffsetOnAxis(idx, 0)).then_inc(
                    arrived, 16)

            def stage_indices(u_head, v_head):
                for head, now, staged in ((u_head, now_u, "u_staged"), (v_head, now_v, "v_staged")):
                    if head is not None:
                        n, hd, odd = head
                        nc.gpsimd.tensor_copy(now[odd], index[n % 2][:, bass.ds(hd.times(16), 16)]).then_inc(
                            a[staged], 1)
                for head, staged in ((u_head, "u_staged"), (v_head, "v_staged")):
                    if head is not None:
                        pool.wait_ge(a[staged], head[1].times(1, 8 * head[0] + 1))

            def gather_u(n, hd, odd, k):
                pool.wait_ge(a["dot_done"], hd.times(16, 128 * n + k + 1))
                pool.sem_inc(a["gather_passed"], 1)
                gather("peer_u", now_u[odd][:, k:k + 1], u_buf[k % U_BUFS], u_in[k % U_BUFS])

            def gather_v(n, hd, odd, k):
                pool.wait_ge(a["v_used"], hd.times(16, 128 * n + k + 1))
                pool.sem_inc(a["gather_passed"], 1)
                gather("peer_v", now_v[odd][:, k:k + 1], v_buf[k % V_BUFS], v_in[k % V_BUFS])

            def step(n, hd, before, odd):
                stage_indices((n, hd, odd), (n, before, 1 - odd))
                for k in range(TOPK):
                    gather_u(n, hd, odd, k)
                    gather_v(n, before, 1 - odd, k)

            for n in range(4):
                last = Head(7)
                if n:
                    stage_indices(None, (n - 1, last, 1))
                    for k in range(8):
                        gather_v(n - 1, last, 1, k)
                pool.wait_ge(a["index_ready"], n + 1)
                stage_indices((n, Head(0), 0), None)
                for k in range(8):
                    if n:
                        gather_v(n - 1, last, 1, 8 + k)
                    gather_u(n, Head(0), 0, 2 * k)
                    gather_u(n, Head(0), 0, 2 * k + 1)
                with pool.Fori(0, 3) as two:
                    for odd in (1, 0):
                        step(n, Head(2 - odd, two, 2), Head(1 - odd, two, 2), odd)
                step(n, Head(7), Head(6), 1)
            stage_indices(None, (3, Head(7), 1))
            for k in range(8):
                gather_v(3, Head(7), 1, k)
            pool.wait_ge(a["s_index"], 1)
            for b in range(N_S):
                pool.wait_ge(a["dot_done"], 32 * TOPK + b + 1)
                gather("peer_u", index_s[:, b:b + 1], u_buf[b], u_in[b])
            for k in range(8, TOPK):
                gather_v(3, Head(7), 1, k)
            pool.wait_ge(a["gather_passed"], 4 * 8 * 2 * TOPK)
            for b in range(N_S):
                pool.wait_ge(a["v_used"], 32 * TOPK + b + 1)
                gather("peer_v", index_s[:, b:b + 1], v_buf[b], v_in[b])

        @block.scalar
        def _(act):
            for n in range(N_T):
                r = rows_of(n)
                if n == 0:
                    act.wait_ge(a["squares"], 1)
                nc.scalar.activation(hx[0:r, n], x[0:r, n], ACT.Square, accum_out=stat[0:r, n:n + 1]).then_inc(
                    a["squares"], 1)
            act.wait_ge(a["inverse"], 1)
            nc.scalar.activation(stat[:, 16:21], stat[:, 8:13], ACT.Sqrt).then_inc(a["roots"], 1)
            for n in range(N_T):
                r = rows_of(n)
                for half in range(2):
                    act.wait_ge(a["turned"], 2 * n + half + 1)
                    nc.scalar.copy(m.hT[:, 4 * half:4 * half + 4, P * n:P * n + r],
                                   bank[5 + half][:, :].rearrange("p (c t) -> p c t", c=4)[:, :, 0:r]).then_inc(
                        a["columns"], 1)
            def keep_scores(i):
                for n in range(N_T):
                    r = rows_of(n)
                    unit = N_T * i + n
                    act.wait_ge(a["score_ready"], unit + 1)
                    src = bank[3 + unit % 4][0:r, :].rearrange("p (c k) -> p c k", c=4)
                    dst = query[0:r, 4 * i:4 * i + 4, P * n:P * n + P] if n < 4 else \
                        sample_scores[:, 4 * i:4 * i + 4]
                    nc.scalar.copy(dst, src).then_inc(a["score_kept"], 1)

            for i in range(4):
                for u in range(8):
                    t, half = divmod(u, 2)
                    unit = 8 * i + u
                    act.wait_ge(a["proj_ready"], unit + 1)
                    nc.scalar.copy(query[:, 4 * i + t, half_of(half)], bank[unit % 3][:, 0:HALF]).then_inc(
                        a[f"proj_free{unit % 3}"], 1)
                    if i and u == 2:
                        keep_scores(i - 1)
            keep_scores(3)

            def gate_exp(n):
                r = rows_of(n)
                act.wait_ge(a["gate_max"], n + 1)
                nc.scalar.activation(gate[n % 2][0:r], gate[n % 2][0:r], ACT.Exp).then_inc(a["gate_exp"], 1)

            def ple_start(n):
                r = rows_of(n)
                act.wait_ge(a["acc_kept"], n + 1)
                nc.scalar.activation(row_tmp[0:r], x[0:r, n], ACT.Square, accum_out=stat[0:r, 24:25]).then_inc(
                    a["ple_square"], 1)
                act.wait_ge(a["ple_inverse"], n + 1)
                nc.scalar.activation(stat[0:r, 26:27], stat[0:r, 25:26], ACT.Sqrt).then_inc(a["ple_root"], 1)

            def ple_gates(n):
                r = rows_of(n)
                for j in range(2):
                    act.wait_ge(a["ple_gate"], 2 * n + j + 1)
                    nc.scalar.activation(row_tmp[0:r, 512 * j:512 * j + 512], bank[5 + j][0:r, :], ACT.Tanh,
                                         scale=0.5).then_inc(a["ple_gated"], 1)

            def ple_end(n):
                r = rows_of(n)
                act.wait_ge(a["ple_used"], 2 * n + 2)
                nc.scalar.activation(row_tmp[0:r], x[0:r, n], ACT.Square, accum_out=stat[0:r, 28:29]).then_inc(
                    a["end_square"], 1)
                act.wait_ge(a["end_inverse"], n + 1)
                nc.scalar.activation(stat[0:r, 30:31], stat[0:r, 29:30], ACT.Sqrt).then_inc(a["end_root"], 1)

            def gelu(n, hd):
                act.wait_ge(a["dots_ready"], hd.times(1, 8 * n + 1))
                nc.scalar.activation(acts, dots, ACT.Gelu_apprx_tanh).then_inc(a["acts_ready"], 1)

            def diagonals(n, hd, some):
                act.wait_ge(a["coef_ready"], hd.times(1, 8 * n + 1))
                for k in some:
                    act.wait_ge(a["v_used"], hd.times(16, 128 * n + k + 1))
                    nc.scalar.mul(diag[k % V_BUFS], ident, coef[:, k:k + 1]).then_inc(a["diag_ready"], 1)

            gate_exp(0)
            for n in range(4):
                if n:
                    ple_start(n - 1)
                gelu(n, Head(0))
                diagonals(n, Head(0), range(V_BUFS))
                if n:
                    ple_gates(n - 1)
                diagonals(n, Head(0), range(V_BUFS, TOPK))
                gelu(n, Head(1))
                if n:
                    ple_end(n - 1)
                diagonals(n, Head(1), range(TOPK))
                with act.Fori(2, 8) as reg:
                    gelu(n, Head(0, reg))
                    diagonals(n, Head(0, reg), range(TOPK))
                gate_exp(n + 1)
            act.wait_ge(a["dots_ready"], 33)
            nc.scalar.activation(acts[:, 0:8], dots[:, 0:8], ACT.Gelu_apprx_tanh).then_inc(a["acts_ready"], 1)
            ple_start(3)
            ple_gates(3)
            ple_end(3)
            act.wait_ge(a["s_turned"], 2)
            nc.scalar.copy(gate_s, bank[3][:, 8:16]).then_inc(a["s_kept"], 1)
            ple_start(4)
            ple_gates(4)
            ple_end(4)

        @block.vector
        def _(dve):
            link = lambda i: sh.dve(dve, i)
            link(nc.vector.memset(stat, 1.0))
            dve.sem_inc(a["squares"], 1)
            dve.sem_inc(a["dot_done"], U_BUFS)
            dve.sem_inc(a["v_used"], V_BUFS)
            dve.sem_inc(a["acts_ready"], 1)
            dve.sem_inc(a["diag_ready"], 1)
            nc.vector.memset(coef_s, 0.0)
            dve.wait_ge(a["squares"], 1 + N_T)
            link(nc.vector.tensor_scalar(stat[:, 0:5], stat[:, 0:5], 1.0 / D_MODEL, EPS, ALU.mult, ALU.add))
            nc.vector.reciprocal(stat[:, 8:13], stat[:, 0:5]).then_inc(a["inverse"], 1)
            dve.wait_ge(a["roots"], 1)
            dve.wait_ge(a["rows_in"], 16)
            for n in range(N_T):
                r = rows_of(n)
                nc.vector.scalar_tensor_tensor(hx[0:r, n], x[0:r, n], stat[0:r, 16 + n:17 + n], norm_rows[0:r, 0],
                                               ALU.mult, ALU.mult).then_inc(a["scaled"], 1)

            def top(n, hd, chain):
                r = rows_of(n)
                link = lambda i: chain(dve, i)
                src = sample_scores if n == 4 else query[:, :, P * n:P * n + P]
                link(nc.vector.tensor_copy(stage[0:r, 0], src[0:r, bass.ds(hd.times(2), 2)]))
                for lo in (0, 8):
                    src = stage[0:r, 0 if lo == 0 else 1]
                    for w in range(2):
                        last = nc.vector.max(val[0:r, w, lo:lo + 8], src[:, w])
                    link(last)
                    for w in range(2):
                        last = nc.vector.max_index(pos[0:r, w, lo:lo + 8], val[0:r, w, lo:lo + 8], src[:, w])
                    if lo == 0:
                        for w in range(2):
                            last = nc.vector.match_replace(stage[0:r, 1, w], val[0:r, w, 0:8], src[:, w], NEG)
                    link(last)
                link(nc.vector.tensor_tensor(cand[0:r], val[0:r, 0].unsqueeze(2).to_broadcast([r, 16, 16]),
                                             val[0:r, 1].unsqueeze(1).to_broadcast([r, 16, 16]), ALU.add))
                flat = cand[0:r].rearrange("p a b -> p (a b)")
                link(nc.vector.max(best[0:r, 0:8], flat))
                nc.vector.max_index(best_at[0:r, 0:8], best[0:r, 0:8], flat)
                link(nc.vector.match_replace(cand_rest[0:r], best[0:r, 0:8], flat, NEG))
                link(nc.vector.max(best[0:r, 8:16], cand_rest[0:r]))
                link(nc.vector.max_index(best_at[0:r, 8:16], best[0:r, 8:16], cand_rest[0:r]))
                link(nc.vector.tensor_copy(all_best[0:r, bass.ds(hd.times(1), 1)].rearrange("p h k -> p (h k)"),
                                           best[0:r]))
                nc.vector.tensor_copy(pos_f[0:r], pos[0:r].rearrange("p w k -> p (w k)"))
                nc.vector.tensor_scalar(digit_u[0:r, 0:16], best_at[0:r], 4, None, ALU.logical_shift_right)
                link(nc.vector.tensor_scalar(digit_u[0:r, 16:32], best_at[0:r], 15, None, ALU.bitwise_and))
                link(nc.vector.tensor_copy(digit[0:r], digit_u[0:r]))
                hot = one_hot[0:r].rearrange("p w k a -> p (w k) a")
                link(nc.vector.tensor_tensor(hot, digit[0:r].unsqueeze(2).to_broadcast([r, 32, 16]),
                                             m.c(C_IOTA, 16, r).unsqueeze(1).to_broadcast([r, 32, 16]), ALU.is_equal))
                link(nc.vector.tensor_tensor(
                    one_hot[0:r], one_hot[0:r],
                    pos_f[0:r].rearrange("p (w k) -> p w k", w=2).unsqueeze(2).to_broadcast([r, 2, 16, 16]), ALU.mult))
                link(nc.vector.tensor_reduce(picked[0:r], hot, X_AXIS, ALU.add))
                link(nc.vector.scalar_tensor_tensor(index_f[0:r, bass.ds(hd.times(16), 16)], picked[0:r, 0:16],
                                                    float(N_KEYS), picked[0:r, 16:32], ALU.mult, ALU.add))

            N_LINKS = 17

            def finish_top(n):
                r = rows_of(n)
                dve.sem_inc(a["top_done"], 1)
                if n >= 2:
                    dve.wait_ge(a["coef_ready"], 8 * (n - 1))
                    dve.wait_ge(a["v_staged"], 8 * (n - 1))
                g = gate[n % 2][0:r].rearrange("p (h k) -> p h k", h=8)
                nc.vector.tensor_tensor(g, all_best[0:r], all_best[0:r, :, 0:1].to_broadcast([r, 8, 16]),
                                        ALU.subtract).then_inc(a["gate_max"], 1)
                nc.vector.tensor_copy(index[n % 2][0:r], index_f[0:r]).then_inc(a["index_ready"], 1)
                dve.wait_ge(a["index_ready"], n + 1)

            def gates(n):
                r = rows_of(n)
                g = gate[n % 2][0:r].rearrange("p (h k) -> p h k", h=8)
                dve.wait_ge(a["gate_exp"], n + 1)
                link(nc.vector.tensor_reduce(stat[0:r, 32:40], g, X_AXIS, ALU.add))
                link(nc.vector.reciprocal(stat[0:r, 32:40], stat[0:r, 32:40]))
                link(nc.vector.tensor_tensor(g, g, stat[0:r, 32:40].unsqueeze(2).to_broadcast([r, 8, 16]), ALU.mult))

            def ple_start(n):
                r = rows_of(n)
                xs = x[0:r, n]
                dve.wait_ge(a["acc_done"], n + 1)
                for j in range(2):
                    xj = xs[:, 512 * j:512 * j + 512]
                    last = nc.vector.tensor_tensor(xj, xj, acc[n % 2][j][0:r, :], ALU.add)
                last.then_inc(a["acc_kept"], 1)
                dve.wait_ge(a["ple_square"], n + 1)
                link(nc.vector.tensor_scalar(stat[0:r, 24:25], stat[0:r, 24:25], 1.0 / D_MODEL, EPS, ALU.mult, ALU.add))
                nc.vector.reciprocal(stat[0:r, 25:26], stat[0:r, 24:25]).then_inc(a["ple_inverse"], 1)
                dve.wait_ge(a["ple_root"], n + 1)
                nc.vector.tensor_scalar(row_tmp[0:r], xs, stat[0:r, 26:27], None, ALU.mult).then_inc(a["ple_scaled"], 1)
                for half in range(2):
                    dve.wait_ge(a["ple_turned"], 2 * n + half + 1)
                    nc.vector.tensor_tensor(ple_x[:, 4 * half:4 * half + 4, 0:r],
                                            bank[3 + half][:, :].rearrange("p (c t) -> p c t", c=4)[:, :, 0:r],
                                            m.norm_ple[:, 4 * half:4 * half + 4].unsqueeze(2).to_broadcast([P, 4, r]),
                                            ALU.mult).then_inc(a["ple_columns"], 1)

            def ple_end(n):
                r = rows_of(n)
                xs = x[0:r, n]
                for j in range(2):
                    dve.wait_ge(a["ple_gated"], 2 * n + j + 1)
                    dve.wait_ge(a["ple_proj"], 2 * n + j + 1)
                    t = row_tmp[0:r, 512 * j:512 * j + 512]
                    link(nc.vector.scalar_tensor_tensor(t, t, 1.0, bank[3 + j][0:r, :], ALU.add, ALU.mult))
                    xj = xs[:, 512 * j:512 * j + 512]
                    nc.vector.scalar_tensor_tensor(xj, t, 0.5, xj, ALU.mult, ALU.add).then_inc(a["ple_used"], 1)
                dve.wait_ge(a["end_square"], n + 1)
                link(nc.vector.tensor_scalar(stat[0:r, 28:29], stat[0:r, 28:29], 1.0 / D_MODEL, EPS, ALU.mult, ALU.add))
                nc.vector.reciprocal(stat[0:r, 29:30], stat[0:r, 28:29]).then_inc(a["end_inverse"], 1)
                dve.wait_ge(a["end_root"], n + 1)
                nc.vector.scalar_tensor_tensor(xs, xs, stat[0:r, 30:31], norm_rows[0:r, 1], ALU.mult,
                                               ALU.mult).then_inc(a["end_rows"], 1)

            def best_of(n, hd):
                chain = LoopChain(a["top_step"], hd, N_LINKS, a["top_passed"], 8 * N_LINKS * n)
                top(n, hd, chain)
                chain.close()

            def dot(n, hd, k):
                dve.wait_ge(u_in[k % U_BUFS], hd.times(32, 16 * (16 * n + k // U_BUFS + 1)))
                u = u_buf[k % U_BUFS]
                nc.vector.tensor_tensor_reduce(u, u, hx[:, n], 1.0, 0.0, ALU.mult, ALU.add,
                                               dots[:, k:k + 1]).then_inc(a["dot_done"], 1)

            def dots_of(n, hd):
                dve.wait_ge(a["acts_ready"], hd.times(1, 8 * n + 1))
                for k in range(TOPK):
                    dot(n, hd, k)
                dve.wait_ge(a["dot_done"], hd.times(16, 128 * n + 16 + U_BUFS))
                dve.sem_inc(a["dots_ready"], 1)

            def coefficients(n, hd):
                dve.wait_ge(a["acts_ready"], hd.times(1, 8 * n + 2))
                dve.wait_ge(a["diag_ready"], hd.times(16, 128 * n + 1))
                nc.vector.tensor_tensor(coef, acts, gate[n % 2][:, bass.ds(hd.times(16), 16)], ALU.mult).then_inc(
                    a["coef_ready"], 1)
                dve.wait_ge(a["coef_ready"], hd.times(1, 8 * n + 1))

            for i in range(4):
                dve.wait_ge(a["score_kept"], N_T * i + 1)
                with dve.Fori(2 * i, 2 * i + 2) as reg:
                    best_of(0, Head(0, reg))
            dve.wait_ge(a["score_kept"], 4 * N_T)
            finish_top(0)
            for n in range(4):
                dots_of(n, Head(0))
                if n:
                    ple_start(n - 1)
                gates(n)
                coefficients(n, Head(0))
                best_of(n + 1, Head(0))
                dots_of(n, Head(1))
                if n:
                    ple_end(n - 1)
                coefficients(n, Head(1))
                best_of(n + 1, Head(1))
                with dve.Fori(2, 8) as reg:
                    dots_of(n, Head(0, reg))
                    coefficients(n, Head(0, reg))
                    best_of(n + 1, Head(0, reg))
                finish_top(n + 1)
            dve.wait_ge(a["s_turned"], 1)
            nc.vector.tensor_copy(index_s, bank[4][:, 0:8]).then_inc(a["s_index"], 1)
            dve.wait_ge(a["top_passed"], 40 * N_LINKS)
            for b in range(N_S):
                dve.wait_ge(a["s_wide"], b + 1)
                dve.wait_ge(u_in[b], 16 * (64 + 1))
                for j in range(2):
                    u = u_buf[b][:, 512 * j:512 * j + 512]
                    last = nc.vector.tensor_tensor_reduce(u, u, bank[5 + j][:, :], 1.0, 0.0, ALU.mult, ALU.add,
                                                          dots_s[:, b, j:j + 1])
                last.then_inc(a["s_read"], 1)
            dve.wait_ge(a["s_read"], N_S)
            nc.vector.tensor_tensor(dots[:, 0:8], dots_s[:, :, 0], dots_s[:, :, 1], ALU.add).then_inc(
                a["dots_ready"], 1)
            ple_start(3)
            gates(4)
            ple_end(3)
            dve.wait_ge(a["acts_ready"], 34)
            dve.wait_ge(a["s_kept"], 1)
            nc.vector.tensor_tensor(coef_s.rearrange("p b c -> p (b c)")[:, 0:64:9], acts[:, 0:8], gate_s,
                                    ALU.mult).then_inc(a["coef_ready"], 1)
            ple_start(4)
            ple_end(4)

        @block.tensor
        def _(pe):
            for n in range(N_T):
                r = rows_of(n)
                pe.wait_ge(a["scaled"], n + 1)
                for half in range(2):
                    if n:
                        pe.wait_ge(a["columns"], 2 * n + half - 1)
                    for j in range(4):
                        at = P * (4 * half + j)
                        last = nc.tensor.transpose(bank[5 + half][:, P * j:P * j + r], hx[0:r, n, at:at + P],
                                                   ident[0:r, 0:r])
                    last.then_inc(a["turned"], 1)
            pe.wait_ge(a["columns"], 2 * N_T)
            def score(i):
                for b in range(3):
                    pe.wait_ge(a[f"proj_free{b}"], uses_of_bank(b, 8 * i + 8))
                if i == 0:
                    pe.wait_ge(a["small_in"], 48)
                for n in range(N_T):
                    r = rows_of(n)
                    unit = N_T * i + n
                    if unit >= 4:
                        pe.wait_ge(a["score_kept"], unit - 3)
                    for j in range(4):
                        last = nc.tensor.matmul(bank[3 + unit % 4][0:r, P * j:P * j + P],
                                                query[:, 4 * i + j, P * n:P * n + r], keys[:, 4 * i + j],
                                                start=True, stop=True)
                    last.then_inc(a["score_ready"], 1)

            for i in range(4):
                b = B_PQ + i
                w = m.slot[b % 2]
                pe.wait_ge(s[f"ring_in{b % 2}"], 16 * (b // 2 + 1))
                for u in range(8):
                    t, half = divmod(u, 2)
                    unit = 8 * i + u
                    if unit >= 3:
                        pe.wait_ge(a[f"proj_free{unit % 3}"], unit // 3)
                    for k in range(8):
                        last = nc.tensor.matmul(bank[unit % 3][:, 0:HALF], w[:, 512 * k + P * t:512 * k + P * t + P],
                                                m.hT[:, k, half_of(half)], start=(k == 0), stop=(k == 7))
                    last.then_inc(a["proj_ready"], 1)
                    if i and u == 2:
                        score(i - 1)
            score(3)
            pe.wait_ge(a["score_kept"], 4 * N_T)

            def ple(n):
                r = rows_of(n)
                if n == 0:
                    pe.wait_ge(a["w_gate_in"], 64)
                pe.wait_ge(a["ple_scaled"], n + 1)
                if n == 3:
                    pe.wait_ge(a["s_index"], 1)
                    pe.wait_ge(a["s_read"], N_S)
                if n == 4:
                    pe.wait_ge(a["s_kept"], 1)
                for half in range(2):
                    for j in range(4):
                        at = P * (4 * half + j)
                        last = nc.tensor.transpose(bank[3 + half][:, P * j:P * j + r], row_tmp[0:r, at:at + P],
                                                   ident[0:r, 0:r])
                    last.then_inc(a["ple_turned"], 1)
                pe.wait_ge(a["ple_columns"], 2 * n + 2)
                for j in range(2):
                    for k in range(8):
                        last = nc.tensor.matmul(bank[5 + j][0:r, :], ple_x[:, k, 0:r], w_gate(k, j), start=(k == 0),
                                                stop=(k == 7))
                    last.then_inc(a["ple_gate"], 1)
                for j in range(2):
                    for k in range(2):
                        last = nc.tensor.matmul(bank[3 + j][0:r, :], p_cols[:, k, P * n:P * n + r],
                                                w_proj[:, k, 512 * j:512 * j + 512], start=(k == 0), stop=(k == 1))
                    last.then_inc(a["ple_proj"], 1)

            def sum_rows(n, hd, first, some=range(TOPK)):
                for k in some:
                    b = k % V_BUFS
                    pe.wait_ge(v_in[b], hd.times(32, 16 * (16 * n + k // V_BUFS + 1)))
                    pe.wait_ge(a["diag_ready"], hd.times(16, 128 * n + k + 2))
                    for j in range(2):
                        last = nc.tensor.matmul(acc[n % 2][j][:, :], diag[b], v_buf[b][:, 512 * j:512 * j + 512],
                                                start=first and k == 0, stop=False, skip_group_check=True)
                    last.then_inc(a["v_used"], 1)

            def spread_features(b):
                if b:
                    pe.wait_ge(a["s_read"], b)
                for j in range(2):
                    last = nc.tensor.matmul(bank[5 + j][:, :], m.c(C_SEL + P * b, P, 8), hx[0:8, 4, 512 * j:512 * j + 512],
                                            start=True, stop=True)
                last.then_inc(a["s_wide"], 1)

            for n in range(4):
                if n >= 2:
                    pe.wait_ge(a["acc_kept"], n - 1)
                sum_rows(n, Head(0), True)
                with pe.Fori(1, 7) as reg:
                    sum_rows(n, Head(0, reg), False)
                sum_rows(n, Head(7), False, range(8))
                if n == 3:
                    pe.wait_ge(a["ple_used"], 6)
                    pe.wait_ge(a["index_ready"], N_T)
                    nc.tensor.transpose(bank[4][:, 0:8], index_f[0:8], ident[0:8, 0:8]).then_inc(a["s_turned"], 1)
                    pe.wait_ge(a["ple_gated"], 6)
                for k in range(8, TOPK):
                    if n == 3:
                        spread_features(k - 8)
                    sum_rows(n, Head(7), False, [k])
                pe.wait_ge(a["v_used"], 128 * (n + 1) + V_BUFS)
                pe.sem_inc(a["acc_done"], 1)
                if n:
                    pe.wait_ge(a["ple_used"], 2 * n)
                ple(n)
            pe.wait_ge(a["ple_used"], 8)
            nc.tensor.transpose(bank[3][:, 8:16], gate[0][0:8], ident[0:8, 0:8]).then_inc(a["s_turned"], 1)
            pe.wait_ge(a["acc_kept"], 3)
            pe.wait_ge(a["coef_ready"], 33)
            for b in range(N_S):
                pe.wait_ge(v_in[b], 16 * (64 + 1))
                for j in range(2):
                    last = nc.tensor.matmul(acc[0][j][0:8, :], coef_s[:, b], v_buf[b][:, 512 * j:512 * j + 512],
                                            start=b == 0, stop=False, skip_group_check=True)
                last.then_inc(a["v_used"], 1)
            pe.wait_ge(a["v_used"], 32 * TOPK + N_S + V_BUFS)
            pe.sem_inc(a["acc_done"], 1)
            ple(4)


def kernel(**inputs):
    import numpy as np
    import concourse.bacc as bacc
    from concourse import mybir as _mybir
    from concourse.bass_utils import run_bass_kernel_spmd as run

    a = {k: np.asarray(v) for k, v in inputs.items()}

    def chunks(w):
        return np.ascontiguousarray(w.reshape(w.shape[0] // P, P, w.shape[1]).transpose(1, 0, 2))

    def column(v):
        return np.ascontiguousarray(v.reshape(-1, P).T)

    w_in = chunks(a["w_in"][0])
    q0, k0, v0 = 0, Q_COLS, 2 * Q_COLS
    z0 = 3 * Q_COLS
    x0 = z0 + D_INNER
    b0 = x0 + D_INNER
    c0 = b0 + SSD_GROUPS * D_STATE
    dt0 = x0 + CONV_CH
    gate0 = dt0 + SSD_HEADS
    blocks = []
    for g in range(3):
        for base in (q0, k0, v0):
            blocks.append(w_in[:, :, base + g * ATT_W:base + (g + 1) * ATT_W])
    for g in range(SSD_GROUPS):
        blocks.append(np.concatenate([w_in[:, :, x0 + 256 * g:x0 + 256 * (g + 1)],
                                      w_in[:, :, b0 + 128 * g:b0 + 128 * (g + 1)],
                                      w_in[:, :, c0 + 128 * g:c0 + 128 * (g + 1)]], axis=2))
        if g in (2, 4, 6, 7):
            j = (g - 1) // 2
            blocks.append(w_in[:, :, z0 + 512 * j:z0 + 512 * (j + 1)])
    for j in range(4):
        blocks.append(w_in[:, :, gate0 + 512 * j:gate0 + 512 * (j + 1)])
    blocks.append(chunks(a["w_att_out"][0]))
    w_ssd = chunks(a["w_ssd_out"][0])
    for j in range(4):
        blocks.append(w_ssd[:, :, 256 * j:256 * (j + 1)])
    w_out = chunks(a["w_out"][0])
    blocks += [w_out[:, :, 512 * j:512 * (j + 1)] for j in range(2)]
    w_pq = chunks(a["w_peer_q"][0])
    blocks += [w_pq[:, :, 512 * j:512 * (j + 1)] for j in range(4)]
    w_pg = chunks(a["w_ple_gate"][0])
    blocks += [w_pg[:, :, 512 * j:512 * (j + 1)] for j in range(2)]
    stream = np.stack([b.reshape(P, 4096) for b in blocks])
    assert stream.shape[0] == N_BLOCKS

    tile_order = [t for g in range(SSD_GROUPS) for t in (2 * g, 2 * g + 1, 16 + g, 24 + g)]
    conv_w = a["conv_w"][0].reshape(CONV_W, 32, P).transpose(2, 1, 0)[:, tile_order]
    conv_b = column(a["conv_b"][0])[:, tile_order]
    state_conv = a["state_conv"][0].reshape(N_S, 3, 32, P).transpose(3, 2, 0, 1)[:, tile_order]
    keys = np.stack([a["peer_keys1"][0], a["peer_keys2"][0]], axis=1)
    keys = keys.transpose(3, 0, 1, 2).reshape(P, 2048)
    p_all = np.concatenate([a["p_prompt"][0, 0], a["p_sample"][0, :, 0]], axis=0)
    cols = np.concatenate([column(a["norm_mix"][0]), column(a["norm_ffn"][0]), column(a["norm_ple"][0]),
                           column(a["ssd_norm"][0]), conv_w.reshape(P, 128), conv_b], axis=1)
    head_rows = np.concatenate([a["dt_bias"][0], a["a_log"][0], a["d_skip"][0]]).reshape(1, 96)
    head_cols = np.stack([a["dt_bias"][0], a["a_log"][0], a["d_skip"][0]], axis=1)
    arrays = {
        "x_prompt": a["x_prompt"][0], "x_sample": a["x_sample"][:, 0],
        "cache0": a["cache_kv_w128"][0].reshape(N_S, -1, 1024),
        "cache1": a["cache_kv_w512"][0].reshape(N_S, -1, 1024),
        "cache2": a["cache_kv_w2048"][0].reshape(N_S, -1, 1024),
        "state_conv": state_conv.reshape(P, 32 * 24),
        "state_ssm": a["state_ssm"][0].reshape(N_S, SSD_HEADS * 64, D_STATE),
        "stream": stream, "w_dt": w_in[:, :, dt0:dt0 + SSD_HEADS].reshape(P, 256),
        "w_ple_proj": chunks(a["w_ple_proj"][0]).reshape(P, 2048),
        "p_cols": chunks(p_all.T).reshape(P, 2 * T_ALL),
        "keys": keys, "cols": cols, "head_rows": head_rows, "head_cols": head_cols,
        "norm_rows": np.stack([a["norm_ffn"][0], a["norm_final"]]),
        "peer_u": a["peer_u"][0], "peer_v": a["peer_v"][0],
        "consts": shape_constants(), "rope_table": rope_table(),
    }
    outs = {
        "y_prompt": (SEQ, D_MODEL), "y_sample": (N_S, D_MODEL),
        "kv0": (128, 1024), "kv1": (SEQ, 1024), "kv2": (SEQ, 1024),
        "conv_prompt": (P, 96), "ssm_prompt": (SSD_HEADS * 64, D_STATE),
        "kvs0": (N_S, 1024), "kvs1": (N_S, 1024), "kvs2": (N_S, 1024),
        "conv_sample": (P, 32 * 24), "ssm_sample": (N_S, SSD_HEADS * 64, D_STATE),
    }
    nc = bacc.Bacc("TRN2", target_bir_lowering=False, num_devices=1)
    arrays = {"in_" + k: np.ascontiguousarray(v) for k, v in arrays.items()}
    ins = {k[3:]: nc.dram_tensor(k, v.shape, _mybir.dt.from_np(v.dtype), kind="ExternalInput").ap()
           for k, v in arrays.items()}
    out_aps = {k: nc.dram_tensor("out_" + k, s, F32, kind="ExternalOutput").ap() for k, s in outs.items()}
    hybrid_decoder_step(nc, ins, out_aps)
    r = run(nc, [arrays], core_ids=[0]).results[0]
    o = {k: r["out_" + k] for k in outs}

    inverse = np.argsort(tile_order)

    def conv_rows(x, n):
        x = x.reshape(P, 32, n, 3)[:, inverse]
        return np.ascontiguousarray(x.transpose(2, 3, 1, 0)).reshape(1, n, 3, CONV_CH)

    kv_shape = (2, 8, 64)
    return (o["y_prompt"].reshape(1, SEQ, D_MODEL), o["y_sample"].reshape(N_S, 1, D_MODEL),
            o["kv0"].reshape(1, 1, 128, *kv_shape), o["kv1"].reshape(1, 1, SEQ, *kv_shape),
            o["kv2"].reshape(1, 1, SEQ, *kv_shape),
            conv_rows(o["conv_prompt"], 1), o["ssm_prompt"].reshape(1, 1, SSD_HEADS, 64, D_STATE),
            o["kvs0"].reshape(1, N_S, 1, *kv_shape), o["kvs1"].reshape(1, N_S, 1, *kv_shape),
            o["kvs2"].reshape(1, N_S, 1, *kv_shape),
            conv_rows(o["conv_sample"], N_S), o["ssm_sample"].reshape(1, N_S, SSD_HEADS, 64, D_STATE))
```
